# Optimizing a Trainium2 kernel written in Bass

```python
import math
import jax, jax.numpy as jnp
from jax import lax
import numpy as np

D_MODEL = 1024
BATCH = 1
SEQ = 1024
DEPTH = 1

ATT_HEAD_DIM = 64
ATT_HEADS_PER_GROUP = 8
ATT_GROUPS = ((128, 1), (512, 4), (2048, 16))
ATT_N_HEADS = ATT_HEADS_PER_GROUP * len(ATT_GROUPS)
ATT_WIDTH = ATT_N_HEADS * ATT_HEAD_DIM
ATT_OUT_WIDTH = ATT_HEADS_PER_GROUP * ATT_HEAD_DIM
ATT_BLOCK = 128
ROPE_THETA = 500000.0
ROPE_DIM = ATT_HEAD_DIM // 4
HGRN_EXPAND = 128
HGRN_HEADS = D_MODEL // HGRN_EXPAND
HGRN_KEY_DIM = HGRN_EXPAND
HGRN_VAL_DIM = D_MODEL // HGRN_HEADS
HGRN_WIDTH = HGRN_HEADS * HGRN_KEY_DIM
HGRN_V_WIDTH = HGRN_HEADS * HGRN_VAL_DIM
HGRN_CHUNK = 64
N_BRANCH = 2
MIX_IN_WIDTH = 3 * ATT_WIDTH + 2 * HGRN_WIDTH + 2 * HGRN_V_WIDTH + N_BRANCH * D_MODEL
D_FF = 2816
PLE_DIM = 256
ALPHA = (2 * DEPTH) ** 0.25
BETA = (8 * DEPTH) ** -0.25
LN_EPS = 1e-5
RMS_EPS = 1e-6

kernel_name = "hybrid_dilated_attn_hgrn2_macaron_deepnorm"

def _layer_norm(x, g, b):
    xf = x.astype(jnp.float32)
    mu = jnp.mean(xf, axis=-1, keepdims=True)
    var = jnp.mean(jnp.square(xf - mu), axis=-1, keepdims=True)
    y = (xf - mu) * lax.rsqrt(var + LN_EPS) * g.astype(jnp.float32) + b.astype(jnp.float32)
    return y.astype(x.dtype)

def _swiglu(x, w_in, w_out):
    a, u = jnp.split(x @ w_in, 2, axis=-1)
    return (jax.nn.silu(a) * u) @ w_out

def _partial_rope(x, positions):
    half = ROPE_DIM // 2
    inv_freq = jnp.exp(-math.log(ROPE_THETA) * jnp.arange(half, dtype=jnp.float32) * (2.0 / ROPE_DIM))
    ang = positions.astype(jnp.float32)[:, :, None] * inv_freq
    cos = jnp.cos(ang)[:, :, None, :]
    sin = jnp.sin(ang)[:, :, None, :]
    xr = x[..., :ROPE_DIM].astype(jnp.float32)
    x1, x2 = xr[..., :half], xr[..., half:]
    rot = jnp.concatenate([x1 * cos - x2 * sin, x2 * cos + x1 * sin], axis=-1).astype(x.dtype)
    return jnp.concatenate([rot, x[..., ROPE_DIM:]], axis=-1)

def _dilated_window_attention(q, k, v, window, dilation):
    b_, s_, h_, dh = q.shape
    sub_len = s_ // dilation
    w_sub = window // dilation
    blk = math.gcd(ATT_BLOCK, sub_len)
    nb = sub_len // blk

    def to_sub(t):
        return t.reshape(b_, sub_len, dilation, h_, dh).transpose(0, 2, 3, 1, 4)

    qs = (to_sub(q) * (dh ** -0.5)).reshape(b_, dilation, h_, nb, blk, dh)
    pad = ((0, 0), (0, 0), (0, 0), (w_sub, 0), (0, 0))
    ks = jnp.pad(to_sub(k), pad)
    vs = jnp.pad(to_sub(v), pad)
    kidx = jnp.arange(nb)[:, None] * blk + jnp.arange(blk + w_sub)[None, :]
    kb = ks[:, :, :, kidx, :]
    vb = vs[:, :, :, kidx, :]
    kpos = kidx - w_sub
    qpos = jnp.arange(nb)[:, None] * blk + jnp.arange(blk)[None, :]
    dist = qpos[:, :, None] - kpos[:, None, :]
    valid = (dist >= 0) & (dist <= w_sub) & (kpos[:, None, :] >= 0)
    s = jnp.einsum('bdhnqc,bdhnkc->bdhnqk', qs, kb, preferred_element_type=jnp.float32)
    s = jnp.where(valid, s, -jnp.inf)
    m = jnp.max(s, axis=-1, keepdims=True)
    e = jnp.exp(s - m)
    l = jnp.sum(e, axis=-1, keepdims=True)
    o = jnp.einsum('bdhnqk,bdhnkc->bdhnqc', e, vb.astype(jnp.float32)) / l
    lse = (m + jnp.log(l))[..., 0]
    o = o.reshape(b_, dilation, h_, sub_len, dh).transpose(0, 3, 1, 2, 4).reshape(b_, s_, h_, dh)
    lse = lse.reshape(b_, dilation, h_, sub_len).transpose(0, 3, 1, 2).reshape(b_, s_, h_)
    return o, lse

def _hgrn2_chunk_scan(q, k, v, log_f):
    b_, s_, h_, dk = q.shape
    dv = v.shape[-1]
    c = HGRN_CHUNK
    nc = s_ // c

    def chunks(t):
        return t.reshape(b_, nc, c, h_, t.shape[-1]).transpose(1, 0, 3, 2, 4)

    qc, kc, vc = chunks(q), chunks(k), chunks(v)
    bc = jnp.cumsum(chunks(log_f), axis=-2)
    causal = jnp.tril(jnp.ones((c, c), dtype=bool))[:, :, None]

    def step(state, inp):
        q_, k_, v_, b_c = inp
        diff = b_c[:, :, :, None, :] - b_c[:, :, None, :, :]
        decay = jnp.where(causal, jnp.exp(jnp.where(causal, diff, 0.0)), 0.0)
        att = jnp.einsum('bhtc,bhtsc,bhsc->bhts', q_, decay, k_)
        o = jnp.einsum('bhts,bhsv->bhtv', att, v_)
        o = o + jnp.einsum('bhtc,bhcv->bhtv', q_ * jnp.exp(b_c), state)
        b_last = b_c[:, :, -1:, :]
        state = (jnp.exp(b_last[:, :, 0, :])[..., None] * state
                 + jnp.einsum('bhsc,bhsv->bhcv', k_ * jnp.exp(b_last - b_c), v_))
        return state, o

    state0 = jnp.zeros((b_, h_, dk, dv), jnp.float32)
    _, o = lax.scan(step, state0, (qc, kc, vc, bc))
    return o.transpose(1, 0, 3, 2, 4).reshape(b_, s_, h_, dv)

def _token_mix(h, positions, w_in, lower_bound, norm_g, w_pa, w_pb, w_o):
    b_, s_, _ = h.shape
    z = h @ w_in
    sizes = [ATT_WIDTH, ATT_WIDTH, ATT_WIDTH, HGRN_WIDTH, HGRN_WIDTH, HGRN_V_WIDTH, HGRN_V_WIDTH]
    cuts = [int(c) for c in np.cumsum(sizes)]
    qa, ka, va, qh, fh, ih, gh, gates = jnp.split(z, cuts, axis=-1)

    qa = _partial_rope(qa.reshape(b_, s_, ATT_N_HEADS, ATT_HEAD_DIM), positions)
    ka = _partial_rope(ka.reshape(b_, s_, ATT_N_HEADS, ATT_HEAD_DIM), positions)
    va = va.reshape(b_, s_, ATT_N_HEADS, ATT_HEAD_DIM)
    outs, lses = [], []
    for gi, (window, dilation) in enumerate(ATT_GROUPS):
        sl = slice(gi * ATT_HEADS_PER_GROUP, (gi + 1) * ATT_HEADS_PER_GROUP)
        o_g, lse_g = _dilated_window_attention(qa[:, :, sl], ka[:, :, sl], va[:, :, sl], window, dilation)
        outs.append(o_g)
        lses.append(lse_g)
    wts = jax.nn.softmax(jnp.stack(lses, axis=0), axis=0)
    o_att = jnp.einsum('gbsh,gbshc->bshc', wts, jnp.stack(outs, axis=0))
    y_att = o_att.reshape(b_, s_, ATT_OUT_WIDTH).astype(h.dtype) @ w_pa

    q = jax.nn.silu(qh.astype(jnp.float32)).reshape(b_, s_, HGRN_HEADS, HGRN_KEY_DIM)
    lb = lower_bound.astype(jnp.float32).reshape(HGRN_HEADS, HGRN_KEY_DIM)
    f = lb + (1.0 - lb) * jax.nn.sigmoid(fh.astype(jnp.float32)).reshape(b_, s_, HGRN_HEADS, HGRN_KEY_DIM)
    v = ih.astype(jnp.float32).reshape(b_, s_, HGRN_HEADS, HGRN_VAL_DIM)
    o = _hgrn2_chunk_scan(q, 1.0 - f, v, jnp.log(f))
    o = o * lax.rsqrt(jnp.mean(jnp.square(o), axis=-1, keepdims=True) + RMS_EPS)
    o = o * norm_g.astype(jnp.float32).reshape(HGRN_HEADS, HGRN_VAL_DIM)
    o = o.reshape(b_, s_, HGRN_V_WIDTH) * jax.nn.silu(gh.astype(jnp.float32))
    y_hgrn = o.astype(h.dtype) @ w_pb

    g_att, g_hgrn = jnp.split(jax.nn.sigmoid(gates), N_BRANCH, axis=-1)
    return (g_att * y_att + g_hgrn * y_hgrn) @ w_o

def setup_inputs(seed: int = 0) -> dict:
    key = jax.random.key(seed)
    ks = jax.random.split(key, 24)
    f32 = jnp.float32

    def nrm(k, shape, scale):
        return jax.random.normal(k, shape, f32) * scale

    def gain(k, shape):
        return 1.0 + 0.05 * jax.random.normal(k, shape, f32)

    def bias(k, shape):
        return 0.02 * jax.random.normal(k, shape, f32)

    x = jax.random.normal(ks[0], (BATCH, SEQ, D_MODEL), f32)
    p = jax.random.normal(ks[1], (DEPTH, BATCH, SEQ, PLE_DIM), f32)
    start = jax.random.randint(ks[2], (BATCH, 1), 0, 4096, dtype=jnp.int32)
    positions = start + jnp.arange(SEQ, dtype=jnp.int32)[None, :]
    return {
        "x": x,
        "p": p,
        "positions": positions,
        "ffn1_w_in": nrm(ks[3], (DEPTH, D_MODEL, 2 * D_FF), D_MODEL ** -0.5),
        "ffn1_w_out": nrm(ks[4], (DEPTH, D_FF, D_MODEL), BETA * D_FF ** -0.5),
        "ln1_g": gain(ks[5], (DEPTH, D_MODEL)),
        "ln1_b": bias(ks[6], (DEPTH, D_MODEL)),
        "w_mix_in": nrm(ks[7], (DEPTH, D_MODEL, MIX_IN_WIDTH), D_MODEL ** -0.5),
        "hgrn_lb_logits": nrm(ks[8], (DEPTH + 1, HGRN_WIDTH), 0.5),
        "hgrn_norm_g": gain(ks[9], (DEPTH, HGRN_V_WIDTH)),
        "w_proj_attn": nrm(ks[10], (DEPTH, ATT_OUT_WIDTH, D_MODEL), ATT_OUT_WIDTH ** -0.5),
        "w_proj_hgrn": nrm(ks[11], (DEPTH, HGRN_V_WIDTH, D_MODEL), HGRN_V_WIDTH ** -0.5),
        "w_mix_out": nrm(ks[12], (DEPTH, D_MODEL, D_MODEL), BETA * D_MODEL ** -0.5),
        "ln2_g": gain(ks[13], (DEPTH, D_MODEL)),
        "ln2_b": bias(ks[14], (DEPTH, D_MODEL)),
        "ffn2_w_in": nrm(ks[15], (DEPTH, D_MODEL, 2 * D_FF), D_MODEL ** -0.5),
        "ffn2_w_out": nrm(ks[16], (DEPTH, D_FF, D_MODEL), BETA * D_FF ** -0.5),
        "ln3_g": gain(ks[17], (DEPTH, D_MODEL)),
        "ln3_b": bias(ks[18], (DEPTH, D_MODEL)),
        "ple_w_proj": nrm(ks[19], (DEPTH, PLE_DIM, D_MODEL), BETA * PLE_DIM ** -0.5),
        "ple_w_gate": nrm(ks[20], (DEPTH, D_MODEL, D_MODEL), D_MODEL ** -0.5),
    }

def reference(x, p, positions, ffn1_w_in, ffn1_w_out, ln1_g, ln1_b, w_mix_in, hgrn_lb_logits,
              hgrn_norm_g, w_proj_attn, w_proj_hgrn, w_mix_out, ln2_g, ln2_b, ffn2_w_in, ffn2_w_out,
              ln3_g, ln3_b, ple_w_proj, ple_w_gate):
    lower_bounds = jnp.cumsum(jax.nn.softmax(hgrn_lb_logits.astype(jnp.float32), axis=0), axis=0)
    h = x
    for i in range(DEPTH):
        h = _layer_norm(ALPHA * h + 0.5 * _swiglu(h, ffn1_w_in[i], ffn1_w_out[i]), ln1_g[i], ln1_b[i])
        mix = _token_mix(h, positions, w_mix_in[i], lower_bounds[i], hgrn_norm_g[i],
                         w_proj_attn[i], w_proj_hgrn[i], w_mix_out[i])
        h = _layer_norm(ALPHA * h + mix, ln2_g[i], ln2_b[i])
        h = _layer_norm(ALPHA * h + 0.5 * _swiglu(h, ffn2_w_in[i], ffn2_w_out[i]), ln3_g[i], ln3_b[i])
        h = h + jax.nn.sigmoid(h @ ple_w_gate[i]) * (p[i] @ ple_w_proj[i])
    return h


_drawn_inputs = setup_inputs


def setup_inputs(seed=0):
    import zlib

    import numpy as np

    out = dict(_drawn_inputs(seed))
    spreads = {}
    factors = {'hgrn_lb_logits': 6.108, 'hgrn_norm_g': 7.347, 'ln2_b': 2.962, 'ln3_b': 3.028}
    for name, (base, spread) in spreads.items():
        noise = np.random.default_rng([zlib.crc32(name.encode()), seed]).standard_normal(out[name].shape)
        drawn = base * np.exp(spread * noise) if base else spread * noise
        out[name] = __import__('jax').numpy.asarray(drawn.astype(out[name].dtype))
    for name, factor in factors.items():
        out[name] = (out[name] * factor).astype(out[name].dtype)
    return out
```

```python
import math

import numpy as np

import concourse.bass as bass
from concourse import mybir
from contextlib import ExitStack

F32 = mybir.dt.float32
F32R = mybir.dt.float32r
I32 = mybir.dt.int32
U8 = mybir.dt.uint8
ACT = mybir.ActivationFunctionType
ALU = mybir.AluOpType

P = 128
SEQ = 1024
DM = 1024
HALF = 512
KT = DM // P
TT = SEQ // P
D_FF = 2816
FT = D_FF // P
FFN_STEPS = FT // 2
ALPHA = 2.0 ** 0.25
LN_EPS = 1e-5
RMS_EPS = 1e-6

GROUPS = 3
PAIRS = 4
DH = 64
ROPE_DIM = 16
ROPE_THETA = 500000.0
ATT_SCALE = DH ** -0.5
HEADS = 8
CHUNK = 128
CHUNKS = SEQ // CHUNK
LEVELS = [1, 2, 4, 8, 16, 32, 64]
PLE_DIM = 256

FFN_UNITS = 6 * FFN_STEPS
ATT_UNITS = 12 * PAIRS
GATE_UNITS = 4
HGRN_UNITS = 4 * HEADS
MERGE_UNITS = 5 * 4
PLE_UNITS = 10
FFN1_BASE = 0
ATT_BASE = FFN1_BASE + FFN_UNITS
GATE_BASE = ATT_BASE + ATT_UNITS
HGRN_BASE = GATE_BASE + GATE_UNITS
MERGE_BASE = HGRN_BASE + HGRN_UNITS
FFN2_BASE = MERGE_BASE + MERGE_UNITS
PLE_BASE = FFN2_BASE + FFN_UNITS
UNITS = PLE_BASE + PLE_UNITS

RAW_SLOTS = 2
SLOTS = 4
FFN_SLOT = [0, 1, 2, 0, 3, 2]


class Step:

    def __init__(self, sem):
        self.sem, self.count = sem, 0

    def after(self, eng, instruction):
        self.count += 1
        instruction.then_inc(self.sem, 1)
        eng.wait_ge(self.sem, self.count)


class Weights:

    def __init__(self, nc, ctx, dram):
        self.dram = dram
        self.raw = ctx.enter_context(nc.sbuf_tensor("w_raw", [P, RAW_SLOTS, DM], F32))
        self.hi = ctx.enter_context(nc.sbuf_tensor("w_hi", [P, SLOTS, DM], F32R))
        self.lo = ctx.enter_context(nc.sbuf_tensor("w_lo", [P, SLOTS, DM], F32R))
        self.raw_ready = [ctx.enter_context(nc.semaphore(f"w_raw_ready{s}")) for s in range(RAW_SLOTS)]
        self.hi_ready = ctx.enter_context(nc.semaphore("w_hi_ready"))
        self.ready = ctx.enter_context(nc.semaphore("w_ready"))
        self.used = ctx.enter_context(nc.semaphore("w_used"))

    def load(self, sp, base, j, i=0, per=0):
        u = base + j + per * i
        sp.wait_ge(self.ready, u + 1)
        sp.dma_start(self.raw[:, j % 2, :], self.dram[u, :, :]).then_inc(self.raw_ready[j % 2], 16)

    def split_hi(self, act, slot, base, j, i=0, per=0, reuse=3):
        u = base + j + per * i
        act.wait_ge(self.raw_ready[j % 2], 16 * (base // 2 + j // 2 + 1) + 8 * per * i)
        act.wait_ge(self.used, u - reuse + 1 + SLOTS)
        act.activation(self.hi[:, slot, :], self.raw[:, j % 2, :], ACT.Copy).then_inc(self.hi_ready, 1)

    def split_lo(self, dve, slot, base, j, i=0, per=0):
        u = base + j + per * i
        dve.wait_ge(self.hi_ready, u + 1)
        dve.tensor_tensor(self.lo[:, slot, :], self.raw[:, j % 2, :], self.hi[:, slot, :].bitcast(F32),
                          ALU.subtract).then_inc(self.ready, 1)

    def wait(self, pe, base, j, i=0, per=0):
        pe.wait_ge(self.ready, base + j + per * i + 1 + RAW_SLOTS)


class Core:

    def past_waits(self, eng):
        eng.sem_inc(self.passed[eng.engine], 1)


def product(pe, out, pairs, start=True, stop=True):
    n = len(pairs)
    for x, (s_hi, s_lo, m_hi, m_lo) in enumerate(pairs):
        pe.matmul(out, s_hi, m_hi, start=start and x == 0, stop=False)
        pe.matmul(out, s_hi, m_lo, start=False, stop=False)
        last = pe.matmul(out, s_lo, m_hi, start=False, stop=stop and x == n - 1)
    return last


def out_product(pe, K, slots, hi, lo, ready, free, done, i):
    W = K.W
    for t in range(0, TT, 2):
        for f in range(2):
            if t in (0, TT // 2):
                pe.wait_ge(ready, 4 * i + 2 * f + (1 if t == 0 else 2))
            for tt in (t, t + 1):
                for c in range(2):
                    bank = K.ps[4 + 2 * (tt % 2) + c][:, :]
                    if f == 0:
                        pe.wait_ge(free, 16 * i + 2 * tt + c + 1)
                    st_hi, st_lo = (x[:, f, tt * P:(tt + 1) * P] for x in (hi, lo))
                    m_hi, m_lo = (w[:, slots[f], c * HALF:(c + 1) * HALF] for w in (W.hi, W.lo))
                    last = product(pe, bank, [(st_hi, st_lo, m_hi, m_lo)], start=(f == 0), stop=(f == 1))
                    if f == 1:
                        last.then_inc(done, 1)
    pe.wait_ge(done, 16 * i + 16)
    pe.sem_inc(W.used, 2)


def ffn_block(nc, K, name, base, presplit, first, ln, res_out=None):
    W, ps, hT_hi, hT_lo, ident = K.W, K.ps, K.hT_hi, K.hT_lo, K.ident
    with ExitStack() as ctx:
        def sb(n, shape, dt=F32):
            return ctx.enter_context(nc.sbuf_tensor(f"{name}_{n}", shape, dt))

        def sem(n):
            return ctx.enter_context(nc.semaphore(f"{name}_{n}"))

        acc = K.acc
        silu = sb("silu", [P, 2, HALF])
        g = sb("g", [P, 2, HALF])
        g_hi = sb("g_hi", [P, 2, SEQ], F32R)
        g_lo = sb("g_lo", [P, 2, SEQ], F32R)
        stage = sb("stage", [P, 2, SEQ]) if first else None
        a_done, u_done, out_done = sem("a_done"), sem("u_done"), sem("out_done")
        a_silu, g_mul, g_high, g_ready, out_free = sem("a_silu"), sem("g_mul"), sem("g_high"), sem("g_ready"), sem("out_free")
        in_ready = [sem(f"in_ready{s}") for s in range(2)]
        acc_ready, x_high, x_ready = sem("acc_ready"), sem("x_high"), sem("x_ready")
        L = LayerNorm(nc, ctx, K, name, ln, res_out)
        block = ctx.enter_context(nc.Block())

        @block.sync
        def _(sp):
            if first:
                sp.dma_start(ident[:, :], K.ident_dram).then_inc(K.const_ready, 16)
                for k in range(KT):
                    if k >= 2:
                        sp.wait_ge(x_ready, k - 1)
                    sp.dma_start(stage[:, k % 2, :], K.xT_dram[k, :, :]).then_inc(in_ready[k % 2], 16)
                    if k < 2:
                        W.load(sp, base, k)
                sp.dma_start(acc[:, :, :], K.x_dram).then_inc(acc_ready, 16)
            L.loads(sp)
            with sp.Fori(0, FFN_STEPS) as i:
                for j in range(6):
                    W.load(sp, base + 2, j, i, 6)
            L.stores(sp)

        @block.scalar
        def _(act):
            if first:
                for k in range(KT):
                    act.wait_ge(in_ready[k % 2], 16 * (k // 2 + 1))
                    act.activation(hT_hi[:, k, :], stage[:, k % 2, :], ACT.Copy).then_inc(x_high, 1)
                    if k == 1:
                        W.split_hi(act, 0, base, 0)
                    if k == 2:
                        W.split_hi(act, 1, base, 1)
            elif presplit == 1:
                W.split_hi(act, 1, base, 1)
            with act.Fori(0, FFN_STEPS) as i:
                def silus(f):
                    for h in range(2):
                        n = 2 * f + h
                        act.wait_ge(a_done, 4 * i + n + 1)
                        act.wait_ge(g_mul, 4 * i + n + 1)
                        act.activation(silu[:, h, :], ps[h][:, :], ACT.Silu).then_inc(a_silu, 1)

                def highs(f):
                    for h in range(2):
                        n = 2 * f + h
                        act.wait_ge(g_mul, 4 * i + n + 3)
                        act.activation(g_hi[:, f, h * HALF:(h + 1) * HALF], g[:, h, :], ACT.Copy).then_inc(g_high, 1)

                W.split_hi(act, FFN_SLOT[2], base, 2, i, 6)
                silus(0)
                W.split_hi(act, FFN_SLOT[3], base, 3, i, 6)
                highs(0)
                W.split_hi(act, FFN_SLOT[4], base, 4, i, 6)
                silus(1)
                W.split_hi(act, FFN_SLOT[5], base, 5, i, 6)
                highs(1)
                W.split_hi(act, 0, base, 6, i, 6)
                W.split_hi(act, 1, base, 7, i, 6, reuse=4)
            L.scalar(act)

        @block.vector
        def _(dve):
            if first:
                dve.sem_inc(W.ready, RAW_SLOTS)
                for k in range(KT):
                    dve.wait_ge(x_high, k + 1)
                    dve.tensor_tensor(hT_lo[:, k, :], stage[:, k % 2, :], hT_hi[:, k, :].bitcast(F32),
                                      ALU.subtract).then_inc(x_ready, 1)
                    if k == 1:
                        W.split_lo(dve, 0, base, 0)
                    if k == 2:
                        W.split_lo(dve, 1, base, 1)
                dve.wait_ge(acc_ready, 16)
                for t in range(TT):
                    dve.tensor_scalar(acc[:, t, :], acc[:, t, :], ALPHA, None, ALU.mult).then_inc(acc_ready, 1)
                dve.wait_ge(acc_ready, 16 + TT)
            elif presplit == 1:
                W.split_lo(dve, 1, base, 1)
            dve.sem_inc(g_mul, 2)
            dve.sem_inc(out_free, 4)
            with dve.Fori(0, FFN_STEPS) as i:
                def gates(f):
                    for h in range(2):
                        n = 2 * f + h
                        dve.wait_ge(u_done, 4 * i + n + 1)
                        dve.wait_ge(a_silu, 4 * i + n + 3)
                        dve.tensor_tensor(g[:, h, :], silu[:, h, :], ps[2 + h][:, :], ALU.mult).then_inc(g_mul, 1)
                        dve.wait_ge(g_high, 4 * i + n + 1)
                        dve.tensor_tensor(g_lo[:, f, h * HALF:(h + 1) * HALF], g[:, h, :],
                                          g_hi[:, f, h * HALF:(h + 1) * HALF].bitcast(F32),
                                          ALU.subtract).then_inc(g_ready, 1)

                W.split_lo(dve, FFN_SLOT[2], base, 2, i, 6)
                W.split_lo(dve, FFN_SLOT[3], base, 3, i, 6)
                gates(0)
                W.split_lo(dve, FFN_SLOT[4], base, 4, i, 6)
                W.split_lo(dve, FFN_SLOT[5], base, 5, i, 6)
                gates(1)
                W.split_lo(dve, 0, base, 6, i, 6)
                W.split_lo(dve, 1, base, 7, i, 6)
                for t in range(TT):
                    for c in range(2):
                        dve.wait_ge(out_done, 16 * i + 2 * t + c + 1)
                        a = acc[:, t, c * HALF:(c + 1) * HALF]
                        dve.scalar_tensor_tensor(a, ps[4 + 2 * (t % 2) + c][:, :], 0.5, a,
                                                 ALU.mult, ALU.add).then_inc(out_free, 1)
            dve.wait_ge(out_free, 16 * FFN_STEPS + 4)
            L.vector(dve)

        @block.tensor
        def _(pe):
            if first:
                pe.sem_inc(W.used, SLOTS)
                pe.wait_ge(x_ready, KT)
            pe.sem_inc(a_silu, 2)
            with pe.Fori(0, FFN_STEPS) as i:
                for f in range(2):
                    for kind in range(2):
                        j = 2 * f + kind
                        W.wait(pe, base, j, i, 6)
                        s = FFN_SLOT[j]
                        for h in range(2):
                            n = 2 * f + h
                            pe.wait_ge((a_silu, g_mul)[kind], 4 * i + n + 1)
                            last = product(pe, ps[2 * kind + h][:, :], [
                                (W.hi[:, s, k * P:(k + 1) * P], W.lo[:, s, k * P:(k + 1) * P],
                                 hT_hi[:, k, h * HALF:(h + 1) * HALF], hT_lo[:, k, h * HALF:(h + 1) * HALF])
                                for k in range(KT)])
                            last.then_inc((a_done, u_done)[kind], 1)
                        pe.wait_ge((a_done, u_done)[kind], 4 * i + 2 * f + 2)
                        pe.sem_inc(W.used, 1)
                W.wait(pe, base, 4, i, 6)
                W.wait(pe, base, 5, i, 6)
                out_product(pe, K, FFN_SLOT[4:], g_hi, g_lo, g_ready, out_free, out_done, i)
            L.tensor(pe)


class LayerNorm:

    def __init__(self, nc, ctx, K, name, index, res_out):
        def sb(n, shape, dt=F32):
            return ctx.enter_context(nc.sbuf_tensor(f"{name}_{n}", shape, dt))

        def sem(n):
            return ctx.enter_context(nc.semaphore(f"{name}_ln_{n}"))

        self.K, self.index, self.res_out = K, index, res_out
        self.scale = ALPHA if index < 2 else 1.0
        self.stats = sb("stats", [P, TT, 2, 6])
        self.mean_var = sb("mean_var", [P, TT, 2])
        self.std = sb("std", [P, TT])
        self.rstd = sb("rstd", [P, TT])
        self.eps = sb("eps", [P, 1])
        self.xn = sb("xn", [P, 4, DM])
        self.y = sb("y", [P, 2, HALF])
        self.cols = sb("cols", [P, 2, KT])
        self.rows = sb("rows", [P, 2, DM])
        self.step = Step(sem("step"))
        self.loaded, self.var_ready, self.std_ready, self.xn_ready = sem("loaded"), sem("var_ready"), sem("std_ready"), sem("xn_ready")
        self.turned, self.y_ready, self.high, self.res_ready, self.stored = sem("turned"), sem("y_ready"), sem("high"), sem("res_ready"), sem("stored")

    def loads(self, sp):
        sp.dma_start(self.cols[:, :, :], self.K.ln_cols_dram[self.index, :, :, :]).then_inc(self.loaded, 16)
        sp.dma_start(self.rows[:, :, :], self.K.ln_rows_dram[self.index, :, :, :].broadcast_to([P, 2, DM])).then_inc(self.loaded, 16)

    def stores(self, sp):
        if self.res_out is not None:
            sp.wait_ge(self.res_ready, TT)
            sp.dma_start(self.res_out, self.K.acc[:, :, :]).then_inc(self.stored, 16)
            sp.wait_ge(self.stored, 16)

    def vector(self, dve):
        acc, step, K = self.K.acc, self.step, self.K
        dve.memset(self.eps[:, :], LN_EPS)
        for half in range(2):
            tiles = range(4 * half, 4 * half + 4)
            for t in tiles:
                for c in range(2):
                    ins = dve.bn_stats(self.stats[:, t, c, :], acc[:, t, c * HALF:(c + 1) * HALF])
            step.after(dve, ins)
            for t in tiles:
                ins = dve.bn_aggr(self.mean_var[:, t, :], self.stats[:, t, :, :].rearrange("p a b -> p (a b)"))
            ins.then_inc(self.var_ready, 1)
        for half in range(2):
            dve.wait_ge(self.std_ready, half + 1)
            tiles = range(4 * half, 4 * half + 4)
            step.after(dve, dve.reciprocal(self.rstd[:, 4 * half:4 * half + 4], self.std[:, 4 * half:4 * half + 4]))
            if half == 1:
                dve.wait_ge(self.turned, KT)
            for t in tiles:
                dve.tensor_scalar(self.xn[:, t % 4, :], acc[:, t, :], self.mean_var[:, t, 0:1], self.rstd[:, t:t + 1],
                                  ALU.subtract, ALU.mult).then_inc(self.xn_ready, 1)
            dve.wait_ge(self.loaded, 32)
            for k in range(KT):
                n = KT * half + k
                if n >= 2:
                    dve.wait_ge(self.high, n - 1)
                dve.wait_ge(self.turned, n + 1)
                dve.tensor_scalar(self.y[:, n % 2, :], K.ps[k][:, :], self.cols[:, 0, k:k + 1], self.cols[:, 1, k:k + 1],
                                  ALU.mult, ALU.add).then_inc(self.y_ready, 1)
                dve.wait_ge(self.high, n + 1)
                part = slice(half * HALF, (half + 1) * HALF)
                dve.tensor_tensor(K.hT_lo[:, k, part], self.y[:, n % 2, :], K.hT_hi[:, k, part].bitcast(F32), ALU.subtract)
            for t in tiles:
                step.after(dve, dve.scalar_tensor_tensor(acc[:, t, :], self.xn[:, t % 4, :], self.scale, self.rows[:, 0, :],
                                                         ALU.mult, ALU.mult))
                dve.scalar_tensor_tensor(acc[:, t, :], self.rows[:, 1, :], self.scale, acc[:, t, :],
                                         ALU.mult, ALU.add).then_inc(self.res_ready, 1)
        dve.wait_ge(self.res_ready, TT)

    def scalar(self, act):
        K = self.K
        for half in range(2):
            act.wait_ge(self.var_ready, half + 1)
            tiles = slice(4 * half, 4 * half + 4)
            act.activation(self.std[:, tiles], self.mean_var[:, tiles, 1], ACT.Sqrt, bias=self.eps[:, :]).then_inc(self.std_ready, 1)
        for n in range(2 * KT):
            act.wait_ge(self.y_ready, n + 1)
            half, k = n // KT, n % KT
            act.activation(K.hT_hi[:, k, half * HALF:(half + 1) * HALF], self.y[:, n % 2, :], ACT.Copy).then_inc(self.high, 1)

    def tensor(self, pe):
        K = self.K
        pe.wait_ge(K.const_ready, 16)
        for half in range(2):
            pe.wait_ge(self.xn_ready, 4 * half + 4)
            for k in range(KT):
                if half:
                    pe.wait_ge(self.y_ready, k + 1)
                for t in range(4):
                    last = pe.transpose(K.ps[k][:, t * P:(t + 1) * P], self.xn[:, t, k * P:(k + 1) * P], K.ident[:, :])
                last.then_inc(self.turned, 1)


JOBS = 8
MAIN_BANKS, SCORE_BANKS, TURN_BANK, OUT_BANKS = (0, 1, 2), (3, 4), 5, (6, 7)
POSITIONS = 24
JOB_POS = [5, 6, 7, 8, 8, 9, 10, 10]
NEG = -3.0e38
TWO_PI_PARTS = (6.28125, 0.001934051513671875, 1.2554228305816650390625e-06)
SWAP_ROPE_HALVES = list(range(8, 16)) + list(range(8)) + list(range(16, 32))


def query_tokens(g, dj):
    if g == 0:
        return slice(dj * P, (dj + 1) * P)
    if g == 1:
        first = dj // 2 + 4 * P * (dj % 2)
        return slice(first, first + 4 * (P - 1) + 1, 4)
    return slice(dj, dj + 8 * (P - 1) + 1, 8)


def key_tiles(g, dj):
    return 1 if g == 2 or (g == 0 and dj == 0) or (g == 1 and dj % 2 == 0) else 2


def key_tokens(g, dj):
    if key_tiles(g, dj) == 1:
        return query_tokens(g, dj)
    if g == 0:
        return slice((dj - 1) * P, (dj + 1) * P)
    return slice(dj // 2, dj // 2 + 4 * (2 * P - 1) + 1, 4)


def token_order(ap, g, x):
    if g == 0:
        return ap[:, x * HALF:(x + 1) * HALF].rearrange("p (r j) -> p r j", r=2)
    r = 4 if g == 1 else 8
    v = ap.rearrange("p (j r) -> p r j", r=r)
    return v[:, x * r // 2:(x + 1) * r // 2, :]


def tile_order(ap, g):
    return ap.rearrange("p (r j) -> p r j", r=4 if g == 2 else 2)


def score_uses():
    order = []
    for pos in range(POSITIONS + 1):
        for g in range(GROUPS):
            if pos == 6 * g + 12:
                order.append(("spread", g))
        for g in range(GROUPS):
            order += [("job", g, dj) for dj in range(JOBS) if JOB_POS[dj] + 6 * g == pos]
    return {key: n for n, key in enumerate(order)}


def at_position(pos, lag):
    return [(g, dj) for g in range(GROUPS) for dj in range(JOBS) if JOB_POS[dj] + 6 * g + lag == pos]


def attention_block(nc, K):
    W, ps, hT_hi, hT_lo, ident = K.W, K.ps, K.hT_hi, K.hT_lo, K.ident
    USE = score_uses()
    N_USE = len(USE)
    base = ATT_BASE
    with ExitStack() as ctx:
        def sb(n, shape, dt=F32):
            return ctx.enter_context(nc.sbuf_tensor(f"att_{n}", shape, dt))

        def sem(n):
            return ctx.enter_context(nc.semaphore(f"att_{n}"))

        qT = [sb(f"qT{s}", [P, SEQ]) for s in range(2)]
        kT = [sb(f"kT{s}", [P, SEQ]) for s in range(2)]
        V = [sb(f"V{s}", [P, JOBS, P]) for s in range(2)]
        vT = sb("vT", [P, SEQ])
        cos, sin = sb("cos", [P, SEQ]), sb("sin", [P, SEQ])
        rope_cols = sb("rope_cols", [P, 2])
        mask2, mask3 = sb("mask2", [P, 2 * P]), sb("mask3", [P, P])
        z, swapped = sb("z", [P, 2, HALF]), sb("swapped", [P, 2, HALF])
        prob, probT = sb("prob", [P, 2, 2, 2 * P]), sb("probT", [P, 2, 4, P])
        gate = sb("gate", [P, 2, HALF])
        O = [sb(f"O{g}", [P, SEQ]) for g in range(GROUPS)]
        lse = [sb(f"lse{g}", [P, SEQ]) for g in range(GROUPS)]
        total = sb("total", [P, SEQ])
        spread = sb("spread", [P, JOBS, 2, DH])
        row_max, row_sum = sb("row_max", [P, GROUPS, JOBS, 2]), sb("row_sum", [P, GROUPS, JOBS, 2])
        neg_max, inv_sum = sb("neg_max", [P, 2, 2]), sb("inv_sum", [P, 2, 2])
        log_sum, row_lse = sb("log_sum", [P, JOBS * 2]), sb("row_lse", [P, JOBS * 2])

        setup, pos_ready, sin_ready = Step(sem("setup")), sem("pos_ready"), sem("sin_ready")
        main_done, main_free = sem("main_done"), sem("main_free")
        z_swapped, rope_part, rope_done = sem("z_swapped"), sem("rope_part"), sem("rope_done")
        vt_turned = sem("vt_turned")
        turn_free = sem("turn_free")
        score_done, score_free = sem("score_done"), sem("score_free")
        negmax_done, exp_done, inv_done, prob_done = sem("negmax_done"), sem("exp_done"), sem("inv_done"), sem("prob_done")
        prob_turned = sem("prob_turned")
        pv_done, out_free = sem("pv_done"), sem("out_free")
        log_done, lse_done, spread_done, spread_turned = sem("log_done"), sem("lse_done"), sem("spread_done"), sem("spread_turned")
        merge, weights_ready, weighted = sem("merge"), sem("weights_ready"), sem("weighted")
        merged, att_stored = sem("merged"), sem("att_stored")
        gate_stored = [sem(f"gate_stored{h}") for h in range(2)]
        MERGE_STEPS = 11
        block = ctx.enter_context(nc.Block())

        @block.sync
        def _(sp):
            sp.dma_start(vT[:, :].bitcast(I32), K.positions_dram.broadcast_to([P, SEQ])).then_inc(pos_ready, 16)
            sp.dma_start(rope_cols[:, :], K.rope_cols_dram).then_inc(pos_ready, 16)
            sp.dma_start(mask2[:, :], K.mask2_dram).then_inc(pos_ready, 16)
            sp.dma_start(mask3[:, :], K.mask3_dram).then_inc(pos_ready, 16)
            for h in range(2):
                sp.sem_inc(gate_stored[h], 16)
            sp.sem_inc(att_stored, 16)
            W.load(sp, base + 2, 0)
            with sp.Fori(0, PAIRS) as i:
                for j in range(1, 13):
                    W.load(sp, base + 2, j, i, 12)
                for n in range(3):
                    for h in range(2):
                        sp.wait_ge(main_free, POSITIONS * i + 18 + 2 * n + h + 1 + 3)
                        sp.dma_start(K.gates_scratch[3 * i + n, :, h * HALF:(h + 1) * HALF], gate[:, h, :])\
                          .then_inc(gate_stored[h], 16)
                sp.wait_ge(merged, i + 1)
                sp.dma_start(K.att_scratch[i, :, :], O[0][:, :]).then_inc(att_stored, 16)
            for h in range(2):
                sp.wait_ge(gate_stored[h], 16 * (3 * PAIRS + 1))
            sp.wait_ge(att_stored, 16 * (PAIRS + 1))

        @block.scalar
        def _(act):
            act.wait_ge(sin_ready, 1)
            act.activation(sin[:, :], total[:, :], ACT.Sin).then_inc(sin_ready, 1)
            act.activation(cos[:, :], O[0][:, :], ACT.Sin).then_inc(sin_ready, 1)
            W.split_hi(act, 2, base, 2)
            act.sem_inc(main_free, 3)
            with act.Fori(0, PAIRS) as i:
                def evacuate(hx):
                    unit, h = hx // 2, hx % 2
                    act.wait_ge(main_done, POSITIONS * i + hx + 1)
                    if unit >= 9:
                        act.wait_ge(gate_stored[h], 16 * (unit - 9) + 16 + 48 * i)
                        out = gate[:, h, :]
                    elif unit % 3 == 2:
                        act.wait_ge(vt_turned, 2 * (unit // 3) + 6 * i + 2)
                        out = vT[:, h * HALF:(h + 1) * HALF]
                    else:
                        rn = 4 * (unit // 3) + 2 * (unit % 3) + h
                        act.wait_ge(rope_done, 12 * i + rn + 1)
                        out = z[:, h, :]
                    act.activation(out, ps[MAIN_BANKS[hx % 3]][:, :], ACT.Copy).then_inc(main_free, 1)

                for pos in range(POSITIONS + 1):
                    if pos >= 1:
                        evacuate(pos - 1)
                    if pos % 2 == 0 and 2 <= pos < POSITIONS:
                        j = pos // 2 + 2
                        W.split_hi(act, j % SLOTS, base, j, i, 12)
                    for g in range(GROUPS):
                        if pos == 6 * g + 11:
                            act.wait_ge(lse_done, 3 * i + g + 1)
                            act.wait_ge(exp_done, 24 * i + 8 * g + 8)
                            act.activation(log_sum[:, :], row_sum[:, g, :, :].rearrange("p a b -> p (a b)"), ACT.Ln)\
                               .then_inc(log_done, 1)
                    for g, dj in at_position(pos, 1):
                        jn = 24 * i + 8 * g + dj
                        nk = key_tiles(g, dj)
                        act.wait_ge(prob_turned, jn + 3)
                        act.wait_ge(pv_done, jn + 23)
                        src = ps[TURN_BANK][:, :].rearrange("p (h k q) -> p h k q", h=2, k=2)[:, :, 2 - nk:2, :]
                        dst = probT[:, dj % 2, :, :].rearrange("p (h k) q -> p h k q", h=2)[:, :, 2 - nk:2, :]
                        act.activation(dst, src, ACT.Copy).then_inc(turn_free, 1)
                    for g, dj in at_position(pos, 0):
                        jn = 24 * i + 8 * g + dj
                        first = 2 * P - P * key_tiles(g, dj)
                        act.wait_ge(negmax_done, jn + 1)
                        for h in range(2):
                            s = prob[:, dj % 2, h, first:2 * P]
                            ins = act.activation(s, s, ACT.Exp, bias=neg_max[:, dj % 2, h:h + 1], scale=ATT_SCALE,
                                                 accum_out=row_sum[:, g, dj, h:h + 1])
                        ins.then_inc(exp_done, 1)
                W.split_hi(act, 2, base, 14, i, 12)
                for g in range(GROUPS):
                    act.wait_ge(merge, MERGE_STEPS * i + 3 + g)
                    act.activation(lse[g][:, :], lse[g][:, :], ACT.Exp).then_inc(weights_ready, 1)

        @block.gpsimd
        def _(pool):
            pool.sem_inc(rope_done, 2)
            pool.wait_ge(sin_ready, 4)
            with pool.Fori(0, PAIRS) as i:
                def rope(g, part, h):
                    rn = 4 * g + 2 * part + h
                    hx = 6 * g + 2 * part + h
                    cols = slice(h * HALF, (h + 1) * HALF)
                    dst = (qT, kT)[part][g % 2][:, cols]
                    if h == 0:
                        pool.wait_ge(score_done, 24 * i + (24, 16, 32)[g])
                    pool.wait_ge(main_free, POSITIONS * i + hx + 4)
                    pool.tensor_tensor(dst, z[:, h, :], cos[:, cols], ALU.mult).then_inc(rope_part, 1)
                    pool.wait_ge(z_swapped, 12 * i + rn + 1)
                    pool.tensor_tensor(swapped[:, h, :], swapped[:, h, :], sin[:, cols], ALU.mult).then_inc(rope_part, 1)
                    pool.wait_ge(rope_part, 24 * i + 2 * rn + 2)
                    pool.tensor_tensor(dst, dst, swapped[:, h, :], ALU.add).then_inc(rope_done, 1)

                def spread_lse(g):
                    pool.wait_ge(lse_done, 3 * i + g + 2)
                    pool.wait_ge(spread_turned, 6 * i + 2 * g + 2)
                    K.past_waits(pool)
                    pool.tensor_copy(spread[:, :, :, :], row_lse[:, :].rearrange("p (a b) -> p a b", b=2)
                                     .unsqueeze(3).broadcast_to([P, JOBS, 2, DH])).then_inc(spread_done, 1)

                for g in range(GROUPS):
                    for part in range(2):
                        for h in range(2):
                            rope(g, part, h)
                    if g >= 1:
                        spread_lse(g - 1)
                spread_lse(2)
                for g in range(GROUPS):
                    pool.wait_ge(weights_ready, 3 * i + g + 1)
                    pool.wait_ge(out_free, 6 * (i + 1) + 2)
                    pool.tensor_tensor(O[g][:, :], O[g][:, :], lse[g][:, :], ALU.mult).then_inc(weighted, 1)

        @block.vector
        def _(dve):
            angle, turns, x, y = total[:, :], O[1][:, :], O[0][:, :], O[2][:, :]
            dve.wait_ge(pos_ready, 64)
            setup.after(dve, dve.tensor_copy(angle, vT[:, :].bitcast(I32)))
            setup.after(dve, dve.tensor_scalar(angle, angle, rope_cols[:, 0:1], None, ALU.mult))
            setup.after(dve, dve.tensor_scalar(turns, angle, 1.0 / (2 * math.pi), 12582912.0, ALU.mult, ALU.add))
            setup.after(dve, dve.tensor_scalar(turns, turns, 12582912.0, None, ALU.subtract))
            for part in TWO_PI_PARTS:
                setup.after(dve, dve.scalar_tensor_tensor(angle, turns, -part, angle, ALU.mult, ALU.add))
            setup.after(dve, dve.tensor_scalar(angle, angle, -3.1415925, 3.1415925, ALU.max, ALU.min))
            setup.after(dve, dve.scalar_tensor_tensor(x, angle, -1.0, angle, ALU.mult, ALU.max))
            setup.after(dve, dve.tensor_scalar(x, x, -1.0, math.pi / 2, ALU.mult, ALU.add))
            dve.sem_inc(sin_ready, 1)
            W.split_lo(dve, 2, base, 2)
            dve.wait_ge(sin_ready, 3)
            dve.tensor_scalar(sin[:, :], sin[:, :], rope_cols[:, 1:2], None, ALU.mult).then_inc(sin_ready, 1)
            dve.sem_inc(turn_free, 1)
            dve.sem_inc(score_free, 2)
            dve.sem_inc(out_free, 2)
            dve.sem_inc(lse_done, 1)
            with dve.Fori(0, PAIRS) as i:
                for pos in range(POSITIONS + 1):
                    if pos % 2 == 0 and 2 <= pos < POSITIONS:
                        j = pos // 2 + 2
                        W.split_lo(dve, j % SLOTS, base, j, i, 12)
                    hx = pos - 1
                    if pos >= 1 and hx // 2 < 9 and (hx // 2) % 3 < 2:
                        rn = 4 * (hx // 6) + 2 * ((hx // 2) % 3) + hx % 2
                        dve.wait_ge(main_free, POSITIONS * i + hx + 4)
                        dve.wait_ge(rope_done, 12 * i + rn + 1)
                        K.past_waits(dve)
                        dve.stream_shuffle(swapped[:, hx % 2, :], z[:, hx % 2, :], SWAP_ROPE_HALVES).then_inc(z_swapped, 1)
                    for g in range(GROUPS):
                        if pos == 6 * g + 6:
                            dve.wait_ge(pv_done, 24 * i + (24, 16, 32)[g])
                            for x2 in range(2):
                                dve.wait_ge(vt_turned, 6 * i + 2 * g + x2 + 3)
                                dve.tensor_copy(V[g % 2][:, 4 * x2:4 * x2 + 4, :],
                                                ps[TURN_BANK][:, :].rearrange("p (k c) -> p k c", k=4)).then_inc(turn_free, 1)
                        if pos == 6 * g + 11:
                            dve.wait_ge(log_done, 3 * i + g + 1)
                            dve.wait_ge(spread_done, 3 * i + g + 1)
                            dve.scalar_tensor_tensor(row_lse[:, :], row_max[:, g, :, :].rearrange("p a b -> p (a b)"),
                                                     ATT_SCALE, log_sum[:, :], ALU.mult, ALU.add).then_inc(lse_done, 1)
                        if pos == 6 * g + 12:
                            for x2 in range(2):
                                dve.wait_ge(spread_turned, 6 * i + 2 * g + x2 + 3)
                                dve.tensor_copy(token_order(lse[g][:, :], g, x2), tile_order(ps[SCORE_BANKS[x2]][:, :], g))\
                                   .then_inc(score_free, 1)
                    for g, dj in at_position(pos, 0):
                        jn = 24 * i + 8 * g + dj
                        nk = key_tiles(g, dj)
                        mask = mask3[:, :] if g == 2 else mask2[:, 2 * P - nk * P:2 * P]
                        dve.wait_ge(score_done, jn + 25)
                        dve.wait_ge(prob_turned, jn + 1)
                        K.past_waits(dve)
                        for h in range(2):
                            dve.tensor_tensor_reduce(
                                prob[:, dj % 2, h, 2 * P - nk * P:2 * P], ps[SCORE_BANKS[h]][:, 0:nk * P], mask,
                                1.0, NEG, ALU.add, ALU.max, row_max[:, g, dj, h:h + 1]).then_inc(score_free, 1)
                        dve.wait_ge(score_free, 2 * N_USE * i + 2 * USE["job", g, dj] + 4)
                        dve.tensor_scalar(neg_max[:, dj % 2, :], row_max[:, g, dj, :], -ATT_SCALE, None, ALU.mult)\
                           .then_inc(negmax_done, 1)
                    for g, dj in at_position(pos, 0):
                        jn = 24 * i + 8 * g + dj
                        first = 2 * P - P * key_tiles(g, dj)
                        dve.wait_ge(exp_done, jn + 1)
                        dve.reciprocal(inv_sum[:, dj % 2, :], row_sum[:, g, dj, :]).then_inc(inv_done, 1)
                        dve.wait_ge(inv_done, jn + 1)
                        for h in range(2):
                            s = prob[:, dj % 2, h, first:2 * P]
                            ins = dve.tensor_scalar(s, s, inv_sum[:, dj % 2, h:h + 1], None, ALU.mult)
                        ins.then_inc(prob_done, 1)
                    for g, dj in at_position(pos, 2):
                        if dj % 4 == 3:
                            jn = 24 * i + 8 * g + dj
                            dve.wait_ge(pv_done, jn + 25)
                            if g == 0 and dj == 3:
                                dve.wait_ge(att_stored, 16 * i + 16)
                            dve.tensor_copy(token_order(O[g][:, :], g, dj // 4),
                                            tile_order(ps[OUT_BANKS[dj // 4]][:, :], g)).then_inc(out_free, 1)
                W.split_lo(dve, 2, base, 14, i, 12)
                steps = 0

                def step(ins):
                    nonlocal steps
                    steps += 1
                    ins.then_inc(merge, 1)
                    dve.wait_ge(merge, MERGE_STEPS * i + steps)

                dve.wait_ge(score_free, 2 * N_USE * (i + 1) + 2)
                step(dve.tensor_tensor(total[:, :], lse[0][:, :], lse[1][:, :], ALU.max))
                step(dve.tensor_tensor(total[:, :], total[:, :], lse[2][:, :], ALU.max))
                for g in range(GROUPS):
                    step(dve.tensor_tensor(lse[g][:, :], lse[g][:, :], total[:, :], ALU.subtract))
                dve.wait_ge(weights_ready, 3 * i + 3)
                step(dve.tensor_tensor(total[:, :], lse[0][:, :], lse[1][:, :], ALU.add))
                step(dve.tensor_tensor(total[:, :], total[:, :], lse[2][:, :], ALU.add))
                step(dve.reciprocal(total[:, :], total[:, :]))
                dve.wait_ge(weighted, 3 * i + 3)
                step(dve.tensor_tensor(O[1][:, :], O[1][:, :], O[2][:, :], ALU.add))
                step(dve.tensor_tensor(O[0][:, :], O[0][:, :], O[1][:, :], ALU.add))
                step(dve.tensor_tensor(O[0][:, :], O[0][:, :], total[:, :], ALU.mult))
                dve.sem_inc(merged, 1)
                assert steps == MERGE_STEPS

        @block.tensor
        def _(pe):
            pe.sem_inc(vt_turned, 2)
            pe.sem_inc(score_done, 24)
            pe.sem_inc(prob_turned, 2)
            pe.sem_inc(pv_done, 24)
            pe.sem_inc(spread_turned, 2)
            pe.sem_inc(spread_done, 1)
            with pe.Fori(0, PAIRS) as i:
                for pos in range(POSITIONS + 1):
                    for g in range(GROUPS):
                        if pos == 6 * g + 12:
                            pe.wait_ge(spread_done, 3 * i + g + 2)
                            for x2 in range(2):
                                pe.wait_ge(score_free, 2 * N_USE * i + 2 * USE["spread", g] + x2 + 1)
                                for q in range(4):
                                    ins = pe.transpose(ps[SCORE_BANKS[x2]][:, q * P:(q + 1) * P],
                                                       spread[:, 4 * x2 + q, :, :].rearrange("p a b -> p (a b)"), ident[:, :])
                                ins.then_inc(spread_turned, 1)

                    def scores(g, dj):
                        nk = key_tiles(g, dj)
                        if dj == 0:
                            pe.wait_ge(rope_done, 12 * i + 4 * (g + 1) + 2)
                        for h in range(2):
                            pe.wait_ge(score_free, 2 * N_USE * i + 2 * USE["job", g, dj] + h + 1)
                            rows = slice(h * DH, (h + 1) * DH)
                            ins = pe.matmul(ps[SCORE_BANKS[h]][:, 0:nk * P],
                                            qT[g % 2][rows, query_tokens(g, dj)], kT[g % 2][rows, key_tokens(g, dj)],
                                            start=True, stop=True)
                        ins.then_inc(score_done, 1)

                    def turn_v(g, x2):
                        pe.wait_ge(turn_free, 30 * i + 10 * g + x2 + 1)
                        for q in range(4):
                            ins = pe.transpose(ps[TURN_BANK][:, q * P:(q + 1) * P], vT[:, query_tokens(g, 4 * x2 + q)], ident[:, :])
                        ins.then_inc(vt_turned, 1)

                    for g in range(GROUPS):
                        if pos == 6 * g + 6:
                            pe.wait_ge(main_free, POSITIONS * i + 6 * g + 6 + 3)
                            turn_v(g, 0)
                    jobs = at_position(pos, 0)
                    if jobs:
                        scores(*jobs[0])
                    for g in range(GROUPS):
                        if pos == 6 * g + 6:
                            turn_v(g, 1)
                    for g, dj in at_position(pos, 1):
                        nk = key_tiles(g, dj)
                        pe.wait_ge(prob_done, 24 * i + 8 * g + dj + 1)
                        pe.wait_ge(turn_free, 30 * i + 10 * g + 2 + dj + 1)
                        for h in range(2):
                            for kt in range(2 - nk, 2):
                                ins = pe.transpose(ps[TURN_BANK][:, (2 * h + kt) * P:(2 * h + kt + 1) * P],
                                                   prob[:, dj % 2, h, kt * P:(kt + 1) * P], ident[:, :])
                        ins.then_inc(prob_turned, 1)
                    for g, dj in at_position(pos, 2):
                        nk = key_tiles(g, dj)
                        pe.wait_ge(turn_free, 30 * i + 10 * g + 2 + dj + 2)
                        if dj % 4 == 0:
                            pe.wait_ge(out_free, 6 * i + 2 * g + dj // 4 + 1)
                        for h in range(2):
                            cols = slice(h * DH, (h + 1) * DH)
                            for kt in range(2 - nk, 2):
                                ins = pe.matmul(ps[OUT_BANKS[dj // 4]][cols, (dj % 4) * P:(dj % 4 + 1) * P],
                                                V[g % 2][:, dj - 1 + kt, cols], probT[:, dj % 2, 2 * h + kt, :],
                                                start=(kt == 2 - nk), stop=(kt == 1))
                        ins.then_inc(pv_done, 1)
                    if pos < POSITIONS:
                        j, h = pos // 2, pos % 2
                        if h == 0:
                            W.wait(pe, base, j, i, 12)
                        pe.wait_ge(main_free, POSITIONS * i + pos + 1)
                        s = j % SLOTS
                        terms = [(W.hi[:, s, k * P:(k + 1) * P], W.lo[:, s, k * P:(k + 1) * P],
                                  hT_hi[:, k, h * HALF:(h + 1) * HALF], hT_lo[:, k, h * HALF:(h + 1) * HALF])
                                 for k in range(KT)]
                        product(pe, ps[MAIN_BANKS[pos % 3]][:, :], terms[:KT // 2], stop=False)
                        if len(jobs) == 2:
                            scores(*jobs[1])
                        product(pe, ps[MAIN_BANKS[pos % 3]][:, :], terms[KT // 2:], start=False).then_inc(main_done, 1)
                        if h == 1:
                            pe.wait_ge(main_done, POSITIONS * i + pos + 1)
                            pe.sem_inc(W.used, 1)


CHAIN = 43
AFTER_KEYS, AFTER_DIAGONAL, AFTER_STATES = 1, 5, 39


def after_level(l):
    return AFTER_DIAGONAL + 4 * l + 2


def rights(ap, m):
    return ap.rearrange("p (b two m) -> p b two m", two=2, m=m)[:, :, 1, :]


def lefts(ap, m):
    return ap.rearrange("p (b two m) -> p b two m", two=2, m=m)[:, :, 0, :]


def hgrn_block(nc, K):
    W, ps, hT_hi, hT_lo, ident = K.W, K.ps, K.hT_hi, K.hT_lo, K.ident
    MAIN, LEVEL, TURN, OUT, MEAN = (0, 1), (2, 3), 4, (5, 6), 7
    with ExitStack() as ctx:
        def sb(n, shape, dt=F32):
            return ctx.enter_context(nc.sbuf_tensor(f"hg_{n}", shape, dt))

        def sem(n):
            return ctx.enter_context(nc.semaphore(f"hg_{n}"))

        Q = [sb(f"Q{s}", [P, SEQ]) for s in range(2)]
        F = [sb(f"F{s}", [P, SEQ]) for s in range(2)]
        G = [sb(f"G{s}", [P, SEQ]) for s in range(2)]
        keys, prods, vT = sb("keys", [P, SEQ]), sb("prods", [P, SEQ]), sb("vT", [P, SEQ])
        V, keysT = sb("V", [P, CHUNKS, P]), sb("keysT", [P, CHUNKS, P])
        att = sb("att", [P, CHUNKS, P])
        state = sb("state", [P, CHUNKS, P])
        z, sig = sb("z", [P, 2, HALF]), sb("sig", [P, 2, HALF])
        sq, rms, o = sb("sq", [P, 2, HALF]), sb("rms", [P, 2, HALF]), sb("o", [P, SEQ])
        masks = sb("masks", [P, len(LEVELS), CHUNK // 2], I32)
        logits, lb, one_minus_lb = sb("logits", [P, 2, HEADS]), sb("lb", [P, HEADS]), sb("one_minus_lb", [P, HEADS])
        lb_tmp, lb_exp = sb("lb_tmp", [P, HEADS]), sb("lb_exp", [P, 2, HEADS])
        norm_g, mean_w, eps = sb("norm_g", [P, HEADS]), sb("mean_w", [P, P]), sb("eps", [P, 1])

        setup, loaded, lb_ready, lb_expd = Step(sem("setup")), sem("loaded"), sem("lb_ready"), sem("lb_expd")
        main_done, main_read = sem("main_done"), sem("main_read")
        pool_used, dve_used = sem("pool_used"), sem("dve_used")
        v_turned, v_ready, k_turned, k_ready = sem("v_turned"), sem("v_ready"), sem("k_turned"), sem("k_ready")
        level_done, update_done, chain = sem("level_done"), sem("update_done"), sem("chain")
        o_done, squared, mean_done, rms_done = sem("o_done"), sem("squared"), sem("mean_done"), sem("rms_done")
        gated, stored = sem("gated"), sem("stored")
        gate_stored = [sem(f"gate_stored{h}") for h in range(2)]
        block = ctx.enter_context(nc.Block())

        def passes(eng, body):
            body(None, 0, 0, True)
            with eng.Fori(0, (HEADS - 2) // 2) as it:
                for a in range(2):
                    body(it, a, 1, True)
            body(0, HEADS - 2, 0, True)
            body(0, HEADS - 1, 0, False)

        def which(it, a, looped):
            if it is None:
                return None, None, 0, (0, 0)
            n = 2 * it + a if looped else a
            return n, a % 2, n + 1, ((4 * (a + 1), it) if looped else (4 * (a + 1), 0))

        @block.sync
        def _(sp):
            sp.dma_start(masks[:, :, :], K.level_masks_dram).then_inc(loaded, 16)
            sp.dma_start(logits[:, :, :], K.lb_logits_dram).then_inc(loaded, 16)
            sp.dma_start(norm_g[:, :], K.norm_g_dram).then_inc(loaded, 16)
            sp.sem_inc(stored, 16)
            W.load(sp, GATE_BASE, 3)
            for j in range(2):
                W.load(sp, HGRN_BASE, j)
            for n in range(GATE_UNITS):
                for h in range(2):
                    sp.wait_ge(main_read, 2 * n + h + 3)
                    sp.dma_start(K.gates_scratch[3 * PAIRS + n, :, h * HALF:(h + 1) * HALF], z[:, h, :]).then_inc(gate_stored[h], 16)
                if n < 2:
                    W.load(sp, HGRN_BASE, n + 2)
            for j in range(4, 8):
                W.load(sp, HGRN_BASE, j)

            def store(n):
                sp.wait_ge(gated, 2 * n + 2)
                sp.dma_start(K.hgrn_scratch[n, :, :], o[:, :]).then_inc(stored, 16)

            with sp.Fori(0, (HEADS - 2) // 2) as it:
                for a in range(2):
                    for j in range(4):
                        W.load(sp, HGRN_BASE, 4 * (a + 2) + j, it, 8)
                    store(2 * it + a)
            for j in range(2):
                W.load(sp, MERGE_BASE, j)
            store(HEADS - 2)
            store(HEADS - 1)
            sp.wait_ge(stored, 16 * (HEADS + 1))
            for h in range(2):
                sp.wait_ge(gate_stored[h], 16 * GATE_UNITS)

        @block.scalar
        def _(act):
            act.wait_ge(lb_ready, 1)
            act.activation(lb_exp[:, :, :], logits[:, :, :], ACT.Exp).then_inc(lb_expd, 1)
            act.sem_inc(main_read, 2)
            act.sem_inc(k_ready, 1)
            act.sem_inc(rms_done, 1)
            for n in range(GATE_UNITS):
                if n >= 1:
                    W.split_hi(act, (n + 2) % SLOTS, GATE_BASE, n + 2)
                for h in range(2):
                    act.wait_ge(main_done, 2 * n + h + 1)
                    if n:
                        act.wait_ge(gate_stored[h], 16 * n)
                    act.activation(z[:, h, :], ps[MAIN[h]][:, :], ACT.Copy).then_inc(main_read, 1)
            for h in range(2):
                act.wait_ge(gate_stored[h], 16 * GATE_UNITS)

            def body(it, a, looped, projecting):
                n, par, nxt, (first, w_it) = which(it, a, looped)

                def evacuate(k):
                    if not projecting:
                        return
                    unit, h = k // 2, k % 2
                    act.wait_ge(main_done, 8 + 8 * nxt + k + 1)
                    bank = ps[MAIN[k % 2]][:, :]
                    if unit == 2:
                        act.wait_ge(v_turned, 2 * nxt + 2)
                        act.activation(vT[:, h * HALF:(h + 1) * HALF], bank, ACT.Copy).then_inc(main_read, 1)
                        return
                    if unit == 0:
                        act.wait_ge(pool_used, 4 * nxt + h + 1)
                    elif unit == 1:
                        act.wait_ge(pool_used, 4 * nxt + h + 3)
                    else:
                        act.wait_ge(dve_used, 2 * nxt + h + 1)
                    if unit != 1:
                        act.activation(z[:, h, :], bank, ACT.Copy)
                    act.activation(sig[:, h, :], bank, ACT.Sigmoid).then_inc(main_read, 1)

                def split(j):
                    if projecting and not (n == HEADS - 2 and j == 3 if not looped else False):
                        act_first = first + j + 2
                        W.split_hi(act, (j + 2) % SLOTS, HGRN_BASE, act_first, w_it, 8 if looped else 0)

                split(0)
                if n is not None:
                    for x in range(2):
                        act.wait_ge(v_turned, 2 * n + x + 3)
                        act.activation(V[:, 4 * x:4 * x + 4, :], ps[TURN][:, :].rearrange("p (c v) -> p c v", c=4), ACT.Copy)\
                           .then_inc(v_ready, 1)
                evacuate(0)
                evacuate(1)
                split(1)
                evacuate(2)
                evacuate(3)
                split(2)
                evacuate(4)
                if n is not None:
                    for x in range(2):
                        act.wait_ge(k_turned, 2 * n + x + 3)
                        act.activation(keysT[:, 4 * x:4 * x + 4, :], ps[TURN][:, :].rearrange("p (c v) -> p c v", c=4), ACT.Copy)\
                           .then_inc(k_ready, 1)
                        if x == 0:
                            evacuate(5)
                            split(3)
                    evacuate(6)
                    for x in range(2):
                        act.wait_ge(o_done, 2 * n + x + 2)
                        act.activation(sq[:, x, :], ps[OUT[x]][:, :], ACT.Square).then_inc(squared, 1)
                    for x in range(2):
                        act.wait_ge(mean_done, 2 * n + x + 1)
                        act.activation(rms[:, x, :], ps[MEAN][:, :], ACT.Sqrt, bias=eps[:, :]).then_inc(rms_done, 1)
                else:
                    evacuate(5)
                    split(3)
                    evacuate(6)
                evacuate(7)

            passes(act, body)

        @block.gpsimd
        def _(pool):
            pool.memset(mean_w[:, :], 1.0 / P).then_inc(setup.sem, 1)
            pool.memset(eps[:, :], RMS_EPS).then_inc(setup.sem, 1)
            pool.sem_inc(pool_used, 2)

            def body(it, a, looped, projecting):
                n, par, nxt, _ = which(it, a, looped)
                other = 0 if n is None else 1 - par

                def gate(dst, unit, h):
                    pool.wait_ge(main_read, 8 + 8 * nxt + 2 * unit + h + 3)
                    if unit == 0 and h == 0 and n is not None:
                        pool.wait_ge(o_done, 2 * n + 1)
                    pool.tensor_tensor(dst[:, h * HALF:(h + 1) * HALF], z[:, h, :], sig[:, h, :], ALU.mult).then_inc(pool_used, 1)

                if projecting:
                    for h in range(2):
                        gate(Q[other], 0, h)
                    for h in range(2):
                        gate(G[other], 3, h)
                if n is not None:
                    for x in range(2):
                        pool.wait_ge(chain, CHAIN * n + 42 + x)
                        part = o[:, x * HALF:(x + 1) * HALF]
                        pool.tensor_tensor(part, part, G[par][:, x * HALF:(x + 1) * HALF], ALU.mult).then_inc(gated, 1)

            passes(pool, body)

        @block.vector
        def _(dve):
            dve.wait_ge(loaded, 48)
            setup.count = 2
            setup.after(dve, dve.tensor_tensor(lb_tmp[:, :], logits[:, 0, :], logits[:, 1, :], ALU.max))
            for r in range(2):
                setup.after(dve, dve.tensor_tensor(logits[:, r, :], logits[:, r, :], lb_tmp[:, :], ALU.subtract))
            dve.sem_inc(lb_ready, 1)
            dve.wait_ge(lb_expd, 1)
            setup.after(dve, dve.tensor_tensor(lb_tmp[:, :], lb_exp[:, 0, :], lb_exp[:, 1, :], ALU.add))
            setup.after(dve, dve.reciprocal(lb_tmp[:, :], lb_tmp[:, :]))
            setup.after(dve, dve.tensor_tensor(lb[:, :], lb_exp[:, 0, :], lb_tmp[:, :], ALU.mult))
            setup.after(dve, dve.tensor_scalar(one_minus_lb[:, :], lb[:, :], -1.0, 1.0, ALU.mult, ALU.add))
            for n in range(1, GATE_UNITS):
                W.split_lo(dve, (n + 2) % SLOTS, GATE_BASE, n + 2)

            def body(it, a, looped, projecting):
                n, par, nxt, (first, w_it) = which(it, a, looped)
                other = 0 if n is None else 1 - par
                steps = 0

                def step(ins, wait=False):
                    nonlocal steps
                    steps += 1
                    ins.then_inc(chain, 1)
                    if wait:
                        dve.wait_ge(chain, CHAIN * n + steps)

                def split(j):
                    if projecting and not (n == HEADS - 2 and j == 3 if not looped else False):
                        W.split_lo(dve, (j + 2) % SLOTS, HGRN_BASE, first + j + 2, w_it, 8 if looped else 0)

                def decay(h):
                    if not projecting:
                        return
                    dve.wait_ge(main_read, 8 + 8 * nxt + 2 + h + 3)
                    head = slice(nxt, nxt + 1) if isinstance(nxt, int) else bass.ds(nxt, 1)
                    dve.tensor_scalar(F[other][:, h * HALF:(h + 1) * HALF], sig[:, h, :], one_minus_lb[:, head], lb[:, head],
                                      ALU.mult, ALU.add).then_inc(dve_used, 1)

                split(0)
                if n is None:
                    split(1)
                    decay(0)
                    decay(1)
                    split(2)
                    split(3)
                    return
                Qn, Fn = Q[par], F[par]
                tp = {1: Fn[:, :]}
                at = 0
                for m in LEVELS:
                    tp[2 * m] = prods[:, at:at + SEQ // (2 * m)]
                    at += SEQ // (2 * m)

                def pairs(m, side):
                    return tp[m].rearrange("p (b two) -> p b two", two=2)[:, :, side]

                def block_product(m):
                    return dve.tensor_tensor(tp[2 * m], pairs(m, 0), pairs(m, 1), ALU.mult)

                def level(l):
                    m = LEVELS[l]
                    dve.wait_ge(level_done, 9 * n + 2 + l + 1)
                    blocks = SEQ // (2 * m)
                    spread = [pairs(m, side).unsqueeze(2).broadcast_to([P, blocks, m]) for side in range(2)]
                    step(dve.tensor_tensor(rights(Qn[:, :], m), rights(Qn[:, :], m), spread[0], ALU.mult))
                    step(dve.tensor_tensor(lefts(keys[:, :], m), lefts(keys[:, :], m), spread[1], ALU.mult))
                    dve.wait_ge(chain, CHAIN * n + steps - 2)
                    if l < len(LEVELS) - 1:
                        step(block_product(2 * m))
                    out = att[:, :, :].rearrange("p c (b two m) -> p c b two m", two=2, m=m)[:, :, :, 1, :]
                    pick = masks[:, l, :].rearrange("p (b m) -> p b m", m=m).unsqueeze(1).broadcast_to([P, CHUNKS, 64 // m, m])
                    data = ps[LEVEL[l % 2]][:, :].rearrange("p (c b m) -> p c b m", c=CHUNKS, m=m)
                    if m == 1:
                        out, pick, data = out.squeeze(3), pick.squeeze(3), data.squeeze(3)
                    elif m == 64:
                        out, pick, data = out.squeeze(2), pick.squeeze(2), data.squeeze(2)
                    K.past_waits(dve)
                    step(dve.copy_predicated(out, pick, data))

                dve.wait_ge(dve_used, 2 * n + 2)
                dve.wait_ge(k_turned, 2 * n + 2)
                step(dve.tensor_scalar(keys[:, :], Fn[:, :], -1.0, 1.0, ALU.mult, ALU.add))
                step(block_product(1))
                for x in range(2):
                    dve.wait_ge(level_done, 9 * n + x + 1)
                    step(dve.tensor_tensor(att[:, 4 * x:4 * x + 4, :], ps[LEVEL[x]][:, :].rearrange("p (c t) -> p c t", c=4),
                                           ident[:, :].unsqueeze(1).broadcast_to([P, 4, P]), ALU.mult))
                step(dve.tensor_tensor(Qn[:, :], Qn[:, :], Fn[:, :], ALU.mult))
                assert steps == AFTER_DIAGONAL
                level(0)
                level(1)
                split(1)
                level(2)
                level(3)
                decay(0)
                level(4)
                split(2)
                decay(1)
                level(5)
                level(6)
                split(3)
                dve.wait_ge(update_done, 2 * n + 1)
                step(dve.tensor_copy(state[:, 1, :], ps[LEVEL[0]][:, 0:P]), wait=True)
                for c in range(1, CHUNKS - 1):
                    if c == 4:
                        dve.wait_ge(update_done, 2 * n + 2)
                    step(dve.scalar_tensor_tensor(state[:, c + 1, :], state[:, c, :], tp[CHUNK][:, c:c + 1],
                                                  ps[LEVEL[c // 4]][:, (c % 4) * P:(c % 4 + 1) * P], ALU.mult, ALU.add), wait=True)
                assert steps == AFTER_STATES
                for x in range(2):
                    dve.wait_ge(rms_done, 2 * n + x + 2)
                    step(dve.reciprocal(rms[:, x, :], rms[:, x, :]), wait=True)
                dve.wait_ge(stored, 16 * n + 16)
                head = slice(n, n + 1) if isinstance(n, int) else bass.ds(n, 1)
                for x in range(2):
                    step(dve.scalar_tensor_tensor(o[:, x * HALF:(x + 1) * HALF], ps[OUT[x]][:, :], norm_g[:, head], rms[:, x, :],
                                                  ALU.mult, ALU.mult))
                assert steps == CHAIN

            passes(dve, body)

        @block.tensor
        def _(pe):
            pe.sem_inc(v_turned, 2)
            pe.sem_inc(k_turned, 2)
            pe.sem_inc(o_done, 1)
            for n in range(GATE_UNITS):
                W.wait(pe, GATE_BASE, n)
                s = n % SLOTS
                for h in range(2):
                    pe.wait_ge(main_read, 2 * n + h + 1)
                    product(pe, ps[MAIN[h]][:, :], [
                        (W.hi[:, s, k * P:(k + 1) * P], W.lo[:, s, k * P:(k + 1) * P],
                         hT_hi[:, k, h * HALF:(h + 1) * HALF], hT_lo[:, k, h * HALF:(h + 1) * HALF])
                        for k in range(KT)]).then_inc(main_done, 1)
                pe.wait_ge(main_done, 2 * n + 2)
                pe.sem_inc(W.used, 1)
            pe.wait_ge(setup.sem, 2)

            def body(it, a, looped, projecting):
                n, par, nxt, (first, w_it) = which(it, a, looped)

                def project(piece):
                    k, third = piece // 3, piece % 3
                    j, h = k // 2, k % 2
                    s = j % SLOTS
                    if third == 0:
                        if h == 0:
                            W.wait(pe, HGRN_BASE, first + j, w_it, 8 if looped else 0)
                        pe.wait_ge(main_read, 8 + 8 * nxt + k + 1)
                    out = ps[MAIN[h]][:, :]
                    for x in range(8 * third, 8 * third + 8):
                        kt, part = x // 3, x % 3
                        cols = slice(kt * P, (kt + 1) * P)
                        toks = slice(h * HALF, (h + 1) * HALF)
                        st = (W.lo if part == 2 else W.hi)[:, s, cols]
                        mv = (hT_lo if part == 1 else hT_hi)[:, kt, toks]
                        ins = pe.matmul(out, st, mv, start=(x == 0), stop=(x == 23))
                    if third == 2:
                        ins.then_inc(main_done, 1)
                        if h == 1:
                            pe.wait_ge(main_done, 8 + 8 * nxt + k + 1)
                            pe.sem_inc(W.used, 1)

                def chunk(c):
                    return slice(c * CHUNK, (c + 1) * CHUNK)

                def turn(src, x, done):
                    for q in range(4):
                        ins = pe.transpose(ps[TURN][:, q * P:(q + 1) * P], src[:, chunk(4 * x + q)], ident[:, :])
                    ins.then_inc(done, 1)

                def steps(pos):
                    if pos == 0:
                        pe.wait_ge(main_read, 8 + 8 * n + 6 + 2)
                        pe.wait_ge(k_ready, 2 * n + 1)
                        turn(vT, 0, v_turned)
                        pe.wait_ge(chain, CHAIN * n + AFTER_KEYS)
                        pe.wait_ge(pool_used, 4 * n + 2 + 2)
                        for x in range(2):
                            for c in range(4):
                                ins = pe.matmul(ps[LEVEL[x]][:, c * P:(c + 1) * P], keys[:, chunk(4 * x + c)],
                                                Q[par][:, chunk(4 * x + c)], start=True, stop=True)
                            ins.then_inc(level_done, 1)
                    if pos == 1:
                        pe.wait_ge(v_ready, 2 * n + 1)
                        turn(vT, 1, v_turned)
                    if pos >= 3 and pos % 2 == 1 and pos <= 15:
                        l = (pos - 3) // 2
                        m = LEVELS[l]
                        pe.wait_ge(chain, CHAIN * n + (after_level(l - 1) if l else AFTER_DIAGONAL))
                        for c in range(CHUNKS):
                            mv = rights(Q[par][:, chunk(c)], m)
                            ins = pe.matmul(ps[LEVEL[l % 2]][:, c * 64:(c + 1) * 64].rearrange("p (b m) -> p b m", m=m),
                                            keys[:, chunk(c)], mv, start=True, stop=True)
                        ins.then_inc(level_done, 1)
                    if pos == 17:
                        pe.wait_ge(v_ready, 2 * n + 2)
                        pe.wait_ge(chain, CHAIN * n + after_level(6))
                        turn(keys, 0, k_turned)
                    if pos == 18:
                        pe.wait_ge(k_ready, 2 * n + 2)
                        turn(keys, 1, k_turned)
                    if pos == 19:
                        pe.wait_ge(k_ready, 2 * n + 3)
                        pe.wait_ge(chain, CHAIN * n + after_level(6) + 1)
                        for x in range(2):
                            for c in range(4 * x, min(4 * x + 4, CHUNKS - 1)):
                                ins = pe.matmul(ps[LEVEL[x]][:, (c % 4) * P:(c % 4 + 1) * P], keysT[:, c, :], V[:, c, :],
                                                start=True, stop=True)
                            ins.then_inc(update_done, 1)
                    if pos == 21:
                        pe.wait_ge(chain, CHAIN * n + AFTER_STATES)
                        for c in range(CHUNKS):
                            out = ps[OUT[c // 4]][:, (c % 4) * P:(c % 4 + 1) * P]
                            ins = pe.matmul(out, V[:, c, :], att[:, c, :], start=True, stop=(c == 0))
                            if c:
                                ins = pe.matmul(out, state[:, c, :], Q[par][:, chunk(c)], start=False, stop=True)
                            if c % 4 == 3:
                                ins.then_inc(o_done, 1)
                    if pos in (22, 23):
                        x = pos - 22
                        pe.wait_ge(squared, 2 * n + x + 1)
                        pe.wait_ge(rms_done, 2 * n + x + 1)
                        pe.matmul(ps[MEAN][:, :], mean_w[:, :], sq[:, x, :], start=True, stop=True).then_inc(mean_done, 1)

                for pos in range(24):
                    if n is not None:
                        steps(pos)
                    if projecting:
                        project(pos)

            passes(pe, body)


def constants():
    q, k = np.arange(P)[:, None], np.arange(P)[None, :]
    half = ROPE_DIM // 2
    freq = np.exp(np.float32(-math.log(ROPE_THETA)) * np.arange(half, dtype=np.float32) * np.float32(2.0 / ROPE_DIM))
    rope = np.zeros((P, 2), np.float32)
    for h in range(2):
        for part, sign in ((0, -1.0), (1, 1.0)):
            rows = slice(h * DH + part * half, h * DH + (part + 1) * half)
            rope[rows, 0], rope[rows, 1] = freq, sign
    level = []
    for m in LEVELS:
        t = np.concatenate([np.arange(b + m, b + 2 * m) for b in range(0, CHUNK, 2 * m)])[None, :]
        level.append((q // (2 * m) == t // (2 * m)) & (q % (2 * m) < m))
    return {
        "ident": np.eye(P, dtype=np.float32),
        "rope_cols": rope,
        "mask2": np.where(np.concatenate([k >= q, k <= q], axis=1), 0.0, NEG).astype(np.float32),
        "mask3": np.where((k <= q) & ((q - k) % 2 == 0), 0.0, NEG).astype(np.float32),
        "level_masks": np.stack(level, axis=1).astype(np.int32),
    }


MERGE_SLOT = [0, 1, 2, 3, 1]
MERGE_STEPS = KT // 2


def merge_block(nc, K):
    W, ps, hT_hi, hT_lo = K.W, K.ps, K.hT_hi, K.hT_lo
    base = MERGE_BASE
    with ExitStack() as ctx:
        def sb(n, shape, dt=F32):
            return ctx.enter_context(nc.sbuf_tensor(f"mg_{n}", shape, dt))

        def sem(n):
            return ctx.enter_context(nc.semaphore(f"mg_{n}"))

        acc = K.acc
        aT_hi, aT_lo = sb("aT_hi", [P, PAIRS, SEQ], F32R), sb("aT_lo", [P, PAIRS, SEQ], F32R)
        m_hi, m_lo = sb("m_hi", [P, 2, SEQ], F32R), sb("m_lo", [P, 2, SEQ], F32R)
        gate, m = sb("gate", [P, 2, SEQ]), sb("m", [P, 2, SEQ])
        in_ready = [sem(f"in_ready{x}") for x in range(2)]
        acc_ready, in_high, in_split = sem("acc_ready"), sem("in_high"), sem("in_split")
        gate_ready = [sem(f"gate_ready{x}") for x in range(2)]
        gate_sig = sem("gate_sig")
        y_done, y_read = sem("y_done"), sem("y_read")
        m_sum, m_high, m_ready = sem("m_sum"), sem("m_high"), sem("m_ready")
        out_done, out_free = sem("out_done"), sem("out_free")
        block = ctx.enter_context(nc.Block())

        def branch(x):
            if x < 4:
                return hT_hi[:, 2 * x:2 * x + 2, :], hT_lo[:, 2 * x:2 * x + 2, :]
            return aT_hi[:, 2 * x - 8:2 * x - 6, :], aT_lo[:, 2 * x - 8:2 * x - 6, :]

        def two_tiles(dram, x):
            return dram[2 * x:2 * x + 2, :, :].rearrange("k p n -> p k n")

        @block.sync
        def _(sp):
            sp.sem_inc(y_read, 4)
            sp.sem_inc(m_sum, 4)
            for x in range(6):
                src = two_tiles(K.hgrn_scratch, x) if x < 4 else two_tiles(K.att_scratch, x - 4)
                if x >= 2:
                    sp.wait_ge(in_split, x - 1)
                sp.dma_start((m, gate)[x % 2][:, :, :], src).then_inc(in_ready[x % 2], 16)
            sp.dma_start(acc[:, :, :], K.res_scratch).then_inc(acc_ready, 16)
            with sp.Fori(0, MERGE_STEPS // 2) as it:
                for a in range(2):
                    i = 2 * it + a

                    def load_gate(q):
                        sp.wait_ge(*((m_sum, 4 * i + 2 * q + 2) if q < 2 else (y_read, 8 * i + 2 * q + 2)))
                        tile = (KT if q < 2 else 0) + 2 * i + q % 2
                        sp.dma_start(gate[:, q % 2, :], K.gates_scratch[tile, :, :]).then_inc(gate_ready[q % 2], 16)

                    if a == 0:
                        sp.wait_ge(in_split, 6)
                    load_gate(0)
                    load_gate(1)
                    W.load(sp, base + 2, 5 * a, it, 10)
                    W.load(sp, base + 2, 5 * a + 1, it, 10)
                    load_gate(2)
                    W.load(sp, base + 2, 5 * a + 2, it, 10)
                    load_gate(3)
                    W.load(sp, base + 2, 5 * a + 3, it, 10)
                    W.load(sp, base + 2, 5 * a + 4, it, 10)

        @block.scalar
        def _(act):
            for x in range(6):
                act.wait_ge(in_ready[x % 2], 16 * (x // 2 + 1))
                act.activation(branch(x)[0], (m, gate)[x % 2][:, :, :], ACT.Copy).then_inc(in_high, 1)
            with act.Fori(0, MERGE_STEPS // 2) as it:
                for a in range(2):
                    i = 2 * it + a

                    def sigmoid(q):
                        act.wait_ge(gate_ready[q % 2], 32 * i + 16 * (q // 2) + 16)
                        act.activation(gate[:, q % 2, :], gate[:, q % 2, :], ACT.Sigmoid).then_inc(gate_sig, 1)

                    W.split_hi(act, 1, base, 5 * a + 1, it, 10, reuse=2)
                    W.split_hi(act, 2, base, 5 * a + 2, it, 10)
                    sigmoid(0)
                    sigmoid(1)
                    W.split_hi(act, 3, base, 5 * a + 3, it, 10)
                    sigmoid(2)
                    W.split_hi(act, 1, base, 5 * a + 4, it, 10)
                    sigmoid(3)
                    for n in range(4):
                        d, h = n // 2, n % 2
                        act.wait_ge(m_sum, 4 * i + n + 5)
                        part = slice(h * HALF, (h + 1) * HALF)
                        act.activation(m_hi[:, d, part], m[:, d, part], ACT.Copy).then_inc(m_high, 1)
                    W.split_hi(act, 0, base, 5 * a + 5, it, 10)

        @block.vector
        def _(dve):
            for x in range(6):
                dve.wait_ge(in_high, x + 1)
                hi, lo = branch(x)
                dve.tensor_tensor(lo, (m, gate)[x % 2][:, :, :], hi.bitcast(F32), ALU.subtract).then_inc(in_split, 1)
            dve.wait_ge(acc_ready, 16)
            dve.sem_inc(out_free, 4)
            with dve.Fori(0, MERGE_STEPS // 2) as it:
                for a in range(2):
                    i = 2 * it + a

                    def weigh(q):
                        for h in range(2):
                            part = slice(h * HALF, (h + 1) * HALF)
                            dve.wait_ge(y_done, 8 * i + 2 * q + h + 1)
                            dve.wait_ge(gate_sig, 4 * i + q + 1)
                            g = gate[:, q % 2, part]
                            dve.tensor_tensor(m[:, q, part] if q < 2 else g, g, ps[2 * (q % 2) + h][:, :], ALU.mult).then_inc(y_read, 1)

                    def merge(d):
                        for h in range(2):
                            n, part = 2 * d + h, slice(h * HALF, (h + 1) * HALF)
                            dve.wait_ge(y_read, 8 * i + n + 9)
                            dve.tensor_tensor(m[:, d, part], m[:, d, part], gate[:, d, part], ALU.add).then_inc(m_sum, 1)
                        for h in range(2):
                            n, part = 2 * d + h, slice(h * HALF, (h + 1) * HALF)
                            dve.wait_ge(m_high, 4 * i + n + 1)
                            dve.tensor_tensor(m_lo[:, d, part], m[:, d, part], m_hi[:, d, part].bitcast(F32), ALU.subtract)\
                               .then_inc(m_ready, 1)

                    W.split_lo(dve, 1, base, 5 * a + 1, it, 10)
                    W.split_lo(dve, 2, base, 5 * a + 2, it, 10)
                    weigh(0)
                    W.split_lo(dve, 3, base, 5 * a + 3, it, 10)
                    weigh(1)
                    W.split_lo(dve, 1, base, 5 * a + 4, it, 10)
                    weigh(2)
                    merge(0)
                    weigh(3)
                    merge(1)
                    W.split_lo(dve, 0, base, 5 * a + 5, it, 10)
                    for n in range(2 * TT):
                        t, c = n // 2, n % 2
                        dve.wait_ge(out_done, 16 * i + n + 1)
                        part = acc[:, t, c * HALF:(c + 1) * HALF]
                        dve.tensor_tensor(part, ps[4 + 2 * (t % 2) + c][:, :], part, ALU.add).then_inc(out_free, 1)
            dve.wait_ge(out_free, 16 * MERGE_STEPS + 4)

        @block.tensor
        def _(pe):
            pe.wait_ge(in_split, 4)
            with pe.Fori(0, MERGE_STEPS // 2) as it:
                for a in range(2):
                    i = 2 * it + a

                    def branch_product(q, stationary, hi, lo, tiles):
                        for h in range(2):
                            part = slice(h * HALF, (h + 1) * HALF)
                            pe.wait_ge(y_read, 8 * i + 2 * q + h + 1)
                            product(pe, ps[2 * (q % 2) + h][:, :], [
                                (*stationary(k), hi[:, k, part], lo[:, k, part]) for k in range(tiles)]).then_inc(y_done, 1)

                    def columns(slot, first=0):
                        return lambda k: (W.hi[:, slot, first + k * P:first + (k + 1) * P], W.lo[:, slot, first + k * P:first + (k + 1) * P])

                    for q in range(2):
                        W.wait(pe, base, 5 * a + q, it, 10)
                        branch_product(q, columns(MERGE_SLOT[q]), hT_hi, hT_lo, KT)
                        pe.wait_ge(y_done, 8 * i + 2 * q + 2)
                        pe.sem_inc(W.used, 1)
                    W.wait(pe, base, 5 * a + 2, it, 10)
                    if a == 0:
                        pe.wait_ge(in_split, 6)
                    for q in (2, 3):
                        branch_product(q, columns(MERGE_SLOT[2], (q - 2) * PAIRS * P), aT_hi, aT_lo, PAIRS)
                    pe.wait_ge(y_done, 8 * i + 8)
                    pe.sem_inc(W.used, 1)
                    W.wait(pe, base, 5 * a + 3, it, 10)
                    W.wait(pe, base, 5 * a + 4, it, 10)
                    out_product(pe, K, MERGE_SLOT[3:], m_hi, m_lo, m_ready, out_free, out_done, i)

    with ExitStack() as ctx:
        L = LayerNorm(nc, ctx, K, "ln2", 1, None)
        block = ctx.enter_context(nc.Block())
        block.sync(L.loads)
        block.scalar(L.scalar)
        block.vector(L.vector)
        block.tensor(L.tensor)


def ple_block(nc, K, out):
    W, ps, hT_hi, hT_lo, acc = K.W, K.ps, K.hT_hi, K.hT_lo, K.acc
    base, tiles = PLE_BASE, PLE_DIM // P
    with ExitStack() as ctx:
        def sb(n, shape, dt=F32):
            return ctx.enter_context(nc.sbuf_tensor(f"ple_{n}", shape, dt))

        def sem(n):
            return ctx.enter_context(nc.semaphore(f"ple_{n}"))

        pT, pT_hi, pT_lo = sb("pT", [P, tiles, SEQ]), sb("pT_hi", [P, tiles, SEQ], F32R), sb("pT_lo", [P, tiles, SEQ], F32R)
        emb, gate = sb("emb", [P, TT, HALF]), sb("gate", [P, TT, HALF])
        p_in, p_high, p_split = sem("p_in"), sem("p_high"), sem("p_split")
        done, read = sem("done"), sem("read")
        scaled, summed, stored = sem("scaled"), sem("summed"), sem("stored")
        block = ctx.enter_context(nc.Block())

        @block.sync
        def _(sp):
            sp.dma_start(pT[:, :, :], K.pT_dram.rearrange("k p n -> p k n")).then_inc(p_in, 16)
            for j in range(2, 6):
                W.load(sp, base, j)

            def store(n):
                t, c = n % TT, n // TT
                sp.wait_ge(summed, n + 1)
                sp.dma_start(out[t, :, c * HALF:(c + 1) * HALF], acc[:, t, c * HALF:(c + 1) * HALF]).then_inc(stored, 16)

            for j in range(6, PLE_UNITS):
                W.load(sp, base, j)
            for n in range(2 * TT):
                store(n)
            sp.wait_ge(stored, 16 * 2 * TT)

        @block.scalar
        def _(act):
            act.wait_ge(p_in, 16)
            act.activation(pT_hi[:, :, :], pT[:, :, :], ACT.Copy).then_inc(p_high, 1)
            for c in range(2):
                for x in range(5):
                    j = 5 * c + x + 2
                    if j < PLE_UNITS:
                        W.split_hi(act, j % SLOTS, base, j, reuse=4)
                    if x == 0:
                        for t in range(TT):
                            act.wait_ge(done, 16 * c + t + 1)
                            if c:
                                act.wait_ge(scaled, t + 1)
                            act.activation(emb[:, t, :], ps[t][:, :], ACT.Copy).then_inc(read, 1)
                for t in range(TT):
                    act.wait_ge(done, 16 * c + TT + t + 1)
                    if c:
                        act.wait_ge(summed, t + 1)
                    act.activation(gate[:, t, :], ps[t][:, :], ACT.Sigmoid).then_inc(read, 1)

        @block.vector
        def _(dve):
            dve.wait_ge(p_high, 1)
            dve.tensor_tensor(pT_lo[:, :, :], pT[:, :, :], pT_hi[:, :, :].bitcast(F32), ALU.subtract).then_inc(p_split, 1)
            for c in range(2):
                for x in range(5):
                    j = 5 * c + x + 2
                    if j < PLE_UNITS:
                        W.split_lo(dve, j % SLOTS, base, j)
                for t in range(TT):
                    n = TT * c + t
                    dve.wait_ge(read, 16 * c + TT + t + 1)
                    dve.tensor_tensor(gate[:, t, :], gate[:, t, :], emb[:, t, :], ALU.mult).then_inc(scaled, 1)
                    dve.wait_ge(scaled, n + 1)
                    part = acc[:, t, c * HALF:(c + 1) * HALF]
                    dve.tensor_tensor(part, part, gate[:, t, :], ALU.add).then_inc(summed, 1)

        @block.tensor
        def _(pe):
            pe.wait_ge(p_split, 1)
            for c in range(2):
                for x in range(5):
                    j = 5 * c + x
                    s = j % SLOTS
                    W.wait(pe, base, j)
                    hi, lo = (pT_hi, pT_lo) if x == 0 else (hT_hi, hT_lo)
                    for t in range(TT):
                        if x < 2 and j:
                            pe.wait_ge(read, TT * (2 * c + x - 1) + t + 1)
                        last = product(pe, ps[t][:, :], [
                            (hi[:, k, t * P:(t + 1) * P], lo[:, k, t * P:(t + 1) * P],
                             W.hi[:, s, (k % 2) * HALF:(k % 2 + 1) * HALF], W.lo[:, s, (k % 2) * HALF:(k % 2 + 1) * HALF])
                            for k in ((0, 1) if x == 0 else (2 * x - 2, 2 * x - 1))], start=(x < 2), stop=(x in (0, 4)))
                        if x in (0, 4):
                            last.then_inc(done, 1)
                        elif t == TT - 1:
                            last.then_inc(W.used, 1)
                    if x in (0, 4):
                        pe.wait_ge(done, TT * (2 * c + (x == 4)) + TT)
                        pe.sem_inc(W.used, 1)


def decoder_layer(nc, drams, out):
    with ExitStack() as ctx:
        K = Core()
        K.W = Weights(nc, ctx, drams["units"])
        K.ps = [ctx.enter_context(nc.psum_tensor(f"bank{b}", [P, HALF], F32)) for b in range(8)]
        K.hT_hi = ctx.enter_context(nc.sbuf_tensor("hT_hi", [P, KT, SEQ], F32R))
        K.hT_lo = ctx.enter_context(nc.sbuf_tensor("hT_lo", [P, KT, SEQ], F32R))
        K.ident = ctx.enter_context(nc.sbuf_tensor("ident", [P, P], F32))
        K.const_ready = ctx.enter_context(nc.semaphore("const_ready"))
        K.passed = {e.engine: ctx.enter_context(nc.semaphore(f"passed_{n}")) for n, e in (("dve", nc.vector), ("pool", nc.gpsimd))}
        K.ident_dram, K.xT_dram, K.x_dram, K.pT_dram = drams["ident"], drams["xT"], drams["x"], drams["pT"]
        K.ln_cols_dram, K.ln_rows_dram = drams["ln_cols"], drams["ln_rows"]
        K.positions_dram, K.rope_cols_dram = drams["positions"], drams["rope_cols"]
        K.mask2_dram, K.mask3_dram = drams["mask2"], drams["mask3"]
        K.level_masks_dram, K.lb_logits_dram, K.norm_g_dram = drams["level_masks"], drams["lb_logits"], drams["norm_g"]

        def scratch(name, shape):
            return nc.dram_tensor(name, shape, F32, kind="Internal").ap()

        K.res_scratch = scratch("res_scratch", (P, TT, DM))
        K.gates_scratch = scratch("gates_scratch", (2 * KT, P, SEQ))
        K.att_scratch = scratch("att_scratch", (PAIRS, P, SEQ))
        K.hgrn_scratch = scratch("hgrn_scratch", (HEADS, P, SEQ))

        with nc.sbuf_tensor("acc1", [P, TT, DM], F32) as K.acc:
            ffn_block(nc, K, "ffn1", FFN1_BASE, presplit=0, first=True, ln=0, res_out=K.res_scratch)
        attention_block(nc, K)
        hgrn_block(nc, K)
        with nc.sbuf_tensor("acc2", [P, TT, DM], F32) as K.acc:
            merge_block(nc, K)
            ffn_block(nc, K, "ffn2", FFN2_BASE, presplit=1, first=False, ln=2)
            ple_block(nc, K, out)


def kernel(**inputs):
    import numpy as _np
    import concourse.bacc as _bacc
    from concourse import mybir as _mybir
    from concourse.bass_utils import run_bass_kernel_spmd as _run

    given = {n: _np.asarray(a) for n, a in inputs.items()}

    def columns(w, first, n=P):
        return w[:, first:first + n].reshape(-1, P, n).transpose(1, 0, 2).reshape(P, -1)

    def slab(w, row, first, tiles):
        width = DM // tiles
        return w[row:row + tiles * P, first:first + width].reshape(tiles, P, width).transpose(1, 0, 2).reshape(P, -1)

    units = _np.empty((UNITS, P, DM), _np.float32)
    at = 0

    def put(unit):
        nonlocal at
        units[at] = unit
        at += 1

    def put_ffn(w_in, w_out):
        for step in range(FFN_STEPS):
            for f in (2 * step, 2 * step + 1):
                put(columns(w_in, f * P))
                put(columns(w_in, D_FF + f * P))
            for f in (2 * step, 2 * step + 1):
                put(slab(w_out, f * P, 0, 1))

    w_mix = given["w_mix_in"][0]
    att, hgrn = 3 * DM // 2, DM
    gates = 3 * att + 4 * hgrn
    put_ffn(given["ffn1_w_in"][0], given["ffn1_w_out"][0])
    for pair in range(PAIRS):
        for group in range(GROUPS):
            for part in range(3):
                put(columns(w_mix, part * att + (group * PAIRS + pair) * P))
        for n in range(3):
            put(columns(w_mix, gates + (3 * pair + n) * P))
    for n in range(3 * PAIRS, 2 * KT):
        put(columns(w_mix, gates + n * P))
    for head in range(HEADS):
        for part in range(4):
            put(columns(w_mix, 3 * att + part * hgrn + head * P))
    w_pa, w_pb, w_o = given["w_proj_attn"][0], given["w_proj_hgrn"][0], given["w_mix_out"][0]
    for j in range(0, KT, 2):
        put(columns(w_pb, j * P))
        put(columns(w_pb, (j + 1) * P))
        put(_np.concatenate([columns(w_pa, j * P), columns(w_pa, (j + 1) * P)], axis=1))
        put(slab(w_o, j * P, 0, 1))
        put(slab(w_o, (j + 1) * P, 0, 1))
    put_ffn(given["ffn2_w_in"][0], given["ffn2_w_out"][0])
    for c in range(2):
        put(slab(given["ple_w_proj"][0], 0, c * HALF, 2))
        for k in range(0, KT, 2):
            put(slab(given["ple_w_gate"][0], k * P, c * HALF, 2))
    assert at == UNITS

    def tiles_of_rows(a):
        return a.reshape(-1, P, a.shape[-1])

    x = given["x"][0]
    arrays = {
        "units": units,
        "xT": tiles_of_rows(x.T),
        "x": tiles_of_rows(x).transpose(1, 0, 2),
        "pT": tiles_of_rows(given["p"][0, 0].T),
        "positions": given["positions"],
        "ln_cols": _np.stack([_np.stack([given[f"ln{i}_{s}"][0].reshape(KT, P).T for s in "gb"], axis=1) for i in (1, 2, 3)]),
        "ln_rows": _np.stack([_np.stack([given[f"ln{i}_{s}"] for s in "gb"], axis=1) for i in (1, 2, 3)]),
        "lb_logits": given["hgrn_lb_logits"].reshape(2, HEADS, P).transpose(2, 0, 1),
        "norm_g": given["hgrn_norm_g"][0].reshape(HEADS, P).T,
        **constants(),
    }
    arrays = {n: _np.ascontiguousarray(a) for n, a in arrays.items()}
    nc = _bacc.Bacc("TRN2", target_bir_lowering=False, num_devices=1)
    drams = {n: nc.dram_tensor(f"in_{n}", a.shape, _mybir.dt.from_np(a.dtype), kind="ExternalInput").ap()
             for n, a in arrays.items()}
    out = nc.dram_tensor("out_0", (TT, P, DM), F32, kind="ExternalOutput").ap()
    decoder_layer(nc, drams, out)
    result = _run(nc, [{f"in_{n}": a for n, a in arrays.items()}], core_ids=[0])
    return result.results[0]["out_0"].reshape(1, SEQ, DM)
```

```python
import math

import numpy as np

import concourse.bass as bass
from concourse import mybir
from contextlib import ExitStack

F32 = mybir.dt.float32
F32R = mybir.dt.float32r
I32 = mybir.dt.int32
U8 = mybir.dt.uint8
ACT = mybir.ActivationFunctionType
ALU = mybir.AluOpType

P = 128
SEQ = 1024
DM = 1024
HALF = 512
KT = DM // P
TT = SEQ // P
D_FF = 2816
FT = D_FF // P
FFN_STEPS = FT // 2
ALPHA = 2.0 ** 0.25
LN_EPS = 1e-5
RMS_EPS = 1e-6

GROUPS = 3
PAIRS = 4
DH = 64
ROPE_DIM = 16
ROPE_THETA = 500000.0
ATT_SCALE = DH ** -0.5
HEADS = 8
CHUNK = 128
CHUNKS = SEQ // CHUNK
LEVELS = [1, 2, 4, 8, 16, 32, 64]
PLE_DIM = 256

FFN_UNITS = 6 * FFN_STEPS
ATT_UNITS = 12 * PAIRS
GATE_UNITS = 4
HGRN_UNITS = 4 * HEADS
MERGE_UNITS = 5 * 4
PLE_UNITS = 10
FFN1_BASE = 0
ATT_BASE = FFN1_BASE + FFN_UNITS
GATE_BASE = ATT_BASE + ATT_UNITS
HGRN_BASE = GATE_BASE + GATE_UNITS
MERGE_BASE = HGRN_BASE + HGRN_UNITS
FFN2_BASE = MERGE_BASE + MERGE_UNITS
PLE_BASE = FFN2_BASE + FFN_UNITS
UNITS = PLE_BASE + PLE_UNITS

RAW_SLOTS = 2
SLOTS = 4
FFN_SLOT = [0, 1, 2, 0, 3, 2]


class Step:

    def __init__(self, sem):
        self.sem, self.count = sem, 0

    def after(self, eng, instruction):
        self.count += 1
        instruction.then_inc(self.sem, 1)
        eng.wait_ge(self.sem, self.count)


class Weights:

    def __init__(self, nc, ctx, dram):
        self.dram = dram
        self.raw = ctx.enter_context(nc.sbuf_tensor("w_raw", [P, RAW_SLOTS, DM], F32))
        self.hi = ctx.enter_context(nc.sbuf_tensor("w_hi", [P, SLOTS, DM], F32R))
        self.lo = ctx.enter_context(nc.sbuf_tensor("w_lo", [P, SLOTS, DM], F32R))
        self.raw_ready = [ctx.enter_context(nc.semaphore(f"w_raw_ready{s}")) for s in range(RAW_SLOTS)]
        self.hi_ready = ctx.enter_context(nc.semaphore("w_hi_ready"))
        self.ready = ctx.enter_context(nc.semaphore("w_ready"))
        self.used = ctx.enter_context(nc.semaphore("w_used"))

    def load(self, sp, base, j, i=0, per=0):
        u = base + j + per * i
        sp.wait_ge(self.ready, u + 1)
        sp.dma_start(self.raw[:, j % 2, :], self.dram[u, :, :]).then_inc(self.raw_ready[j % 2], 16)

    def split_hi(self, act, slot, base, j, i=0, per=0, reuse=3):
        u = base + j + per * i
        act.wait_ge(self.raw_ready[j % 2], 16 * (base // 2 + j // 2 + 1) + 8 * per * i)
        act.wait_ge(self.used, u - reuse + 1 + SLOTS)
        act.activation(self.hi[:, slot, :], self.raw[:, j % 2, :], ACT.Copy).then_inc(self.hi_ready, 1)

    def split_lo(self, dve, slot, base, j, i=0, per=0):
        u = base + j + per * i
        dve.wait_ge(self.hi_ready, u + 1)
        dve.tensor_tensor(self.lo[:, slot, :], self.raw[:, j % 2, :], self.hi[:, slot, :].bitcast(F32),
                          ALU.subtract).then_inc(self.ready, 1)

    def done(self, eng, base, j, i=0, per=0):
        eng.wait_ge(self.used, base + j + per * i + 1 + SLOTS)

    def wait(self, pe, base, j, i=0, per=0):
        pe.wait_ge(self.ready, base + j + per * i + 1 + RAW_SLOTS)


class Core:

    def past_waits(self, eng):
        eng.sem_inc(self.passed[eng.engine], 1)


def product(pe, out, pairs, start=True, stop=True):
    n = len(pairs)
    for x, (s_hi, s_lo, m_hi, m_lo) in enumerate(pairs):
        pe.matmul(out, s_hi, m_hi, start=start and x == 0, stop=False)
        pe.matmul(out, s_hi, m_lo, start=False, stop=False)
        last = pe.matmul(out, s_lo, m_hi, start=False, stop=stop and x == n - 1)
    return last


def out_product(pe, K, slots, hi, lo, ready, free, done, step):
    W = K.W
    for t in range(0, TT, 2):
        for f in range(2):
            if t in (0, TT // 2):
                pe.wait_ge(ready, 4 * step + 2 * f + (1 if t == 0 else 2))
            for tt in (t, t + 1):
                for c in range(2):
                    bank = K.ps[4 + 2 * (tt % 2) + c][:, :]
                    if f == 0:
                        pe.wait_ge(free, 16 * step + 2 * tt + c + 1)
                    st_hi, st_lo = (x[:, f, tt * P:(tt + 1) * P] for x in (hi, lo))
                    m_hi, m_lo = (w[:, slots[f], c * HALF:(c + 1) * HALF] for w in (W.hi, W.lo))
                    last = product(pe, bank, [(st_hi, st_lo, m_hi, m_lo)], start=(f == 0), stop=(f == 1))
                    if f == 1:
                        if (tt, c) == (TT - 1, 1):
                            last.then_inc(W.used, 2)
                        else:
                            last.then_inc(done, 1)


def add_out(dve, K, done, free, res_ready, step, unit, factor, L=None):
    for t in range(TT):
        for c in range(2):
            if (t, c) == (TT - 1, 1):
                K.W.done(dve, *unit)
            else:
                dve.wait_ge(done, 15 * step + 2 * t + c + 1)
            if c == 0:
                dve.wait_ge(res_ready, t + 1)
            a = K.acc[:, t, c * HALF:(c + 1) * HALF]
            dve.scalar_tensor_tensor(a, K.ps[4 + 2 * (t % 2) + c][:, :], factor, a, ALU.mult, ALU.add).then_inc(free, 1)
        if L is not None:
            if t >= 1:
                dve.wait_ge(free, 16 * step + 2 * t + 4)
                L.statistics(dve, t - 1)
            if t == 5:
                L.scales(dve, 0)
            if t == 4:
                L.moments(dve, 0)
    if L is not None:
        dve.wait_ge(free, 16 * step + 2 * TT + 4)
        L.statistics(dve, TT - 1)
        L.moments(dve, 1)
        L.scales(dve, 1)
        L.columns(dve)


class Residual:

    def __init__(self, nc, ctx, K, name, index, rows=2):
        self.K, self.index, self.rows = K, index, rows
        self.scale = 1.0 if index == 2 else ALPHA
        self.row = None if index is None else ctx.enter_context(nc.sbuf_tensor(f"{name}_res_row", [P, rows, DM], F32))
        self.ready = ctx.enter_context(nc.semaphore(f"{name}_res_ready"))
        if index is not None:
            self.loaded, self.scaled, self.gained = (
                ctx.enter_context(nc.semaphore(f"{name}_res_{n}")) for n in ("loaded", "scaled", "gained"))

    def load(self, eng, first, rows):
        eng.dma_start(self.row[:, 0:rows, :], self.K.ln_rows_dram[self.index, :, first:first + rows, :].broadcast_to([P, rows, DM]))\
           .then_inc(self.loaded, 16)

    def loads(self, sp):
        if self.index is not None and self.rows == 2:
            self.load(sp, 0, 2)

    def make(self, pool):
        acc = self.K.acc
        if self.index is None:
            for t in range(TT):
                pool.tensor_scalar(acc[:, t, :], acc[:, t, :], self.scale, None, ALU.mult).then_inc(self.ready, 1)
            return
        for r, op in ((0, ALU.mult), (1, ALU.add)):
            if r:
                pool.wait_ge(self.gained, TT)
            if self.rows == 1:
                self.load(pool, r, 1)
            pool.wait_ge(self.loaded, 16 * (r + 1) if self.rows == 1 else 16)
            row = self.row[:, r % self.rows, :]
            if self.scale != 1.0:
                pool.tensor_scalar(row, row, self.scale, None, ALU.mult).then_inc(self.scaled, 1)
                pool.wait_ge(self.scaled, r + 1)
            for t in range(TT):
                pool.tensor_tensor(acc[:, t, :], acc[:, t, :], row, op).then_inc((self.gained, self.ready)[r], 1)


class LayerNorm:

    def __init__(self, nc, ctx, K, name, index):
        def sb(n, shape, dt=F32):
            return ctx.enter_context(nc.sbuf_tensor(f"{name}_{n}", shape, dt))

        def sem(n):
            return ctx.enter_context(nc.semaphore(f"{name}_ln_{n}"))

        self.K, self.index = K, index
        self.stats = sb("stats", [P, TT, 2, 6])
        self.mean_var = sb("mean_var", [P, TT, 2])
        self.std, self.rstd, self.shift = sb("std", [P, TT]), sb("rstd", [P, TT]), sb("shift", [P, TT])
        self.eps = sb("eps", [P, 1])
        self.y = sb("y", [P, 4, HALF])
        self.cols = sb("cols", [P, 2, KT])
        self.step = Step(sem("step"))
        self.loaded, self.var_ready, self.std_ready, self.scale_ready, self.xn_ready = (
            sem(n) for n in ("loaded", "var_ready", "std_ready", "scale_ready", "xn_ready"))
        self.turned, self.y_ready, self.high = (sem(n) for n in ("turned", "y_ready", "high"))
        self.low = sem("low_even"), sem("low_odd")
        self.stored = sem("stored") if index == 0 else None

    def loads(self, sp):
        sp.dma_start(self.cols[:, :, :], self.K.ln_cols_dram[self.index, :, :, :]).then_inc(self.loaded, 16)

    def store(self, sp, dram):
        for half in range(2):
            sp.wait_ge(self.xn_ready, 4 * half + 4)
            tiles = slice(4 * half, 4 * half + 4)
            sp.dma_start(dram[:, tiles, :], self.K.acc[:, tiles, :]).then_inc(self.stored, 16)
        sp.wait_ge(self.stored, 32)

    def statistics(self, dve, t):
        if t == 0:
            dve.memset(self.eps[:, :], LN_EPS)
        for c in range(2):
            ins = dve.bn_stats(self.stats[:, t, c, :], self.K.acc[:, t, c * HALF:(c + 1) * HALF])
        self.step.count += 1
        ins.then_inc(self.step.sem, 1)

    def moments(self, dve, half):
        dve.wait_ge(self.step.sem, self.step.count)
        for t in range(4 * half, 4 * half + 4):
            ins = dve.bn_aggr(self.mean_var[:, t, :], self.stats[:, t, :, :].rearrange("p a b -> p (a b)"))
        ins.then_inc(self.var_ready, 1)

    def scales(self, dve, half):
        tiles = slice(4 * half, 4 * half + 4)
        dve.wait_ge(self.std_ready, half + 1)
        self.step.after(dve, dve.reciprocal(self.rstd[:, tiles], self.std[:, tiles]))
        dve.scalar_tensor_tensor(self.shift[:, tiles], self.mean_var[:, tiles, 0], -1.0, self.rstd[:, tiles],
                                 ALU.mult, ALU.mult).then_inc(self.scale_ready, 1)

    def part(self, n):
        return (slice(None), n % KT, slice(n // KT * HALF, (n // KT + 1) * HALF))

    def low_part(self, eng, n):
        eng.wait_ge(self.high, n + 1)
        eng.tensor_tensor(self.K.hT_lo[self.part(n)], self.y[:, n % 4, :], self.K.hT_hi[self.part(n)].bitcast(F32),
                          ALU.subtract).then_inc(self.low[n % 2], 1)

    def columns(self, dve):
        dve.wait_ge(self.loaded, 16)
        for n in range(2 * KT):
            if n >= 4:
                dve.wait_ge(self.low[n % 2], n // 2 - 1)
            dve.wait_ge(self.turned, n + 1)
            k = n % KT
            dve.tensor_scalar(self.y[:, n % 4, :], self.K.ps[k][:, :], self.cols[:, 0, k:k + 1], self.cols[:, 1, k:k + 1],
                              ALU.mult, ALU.add).then_inc(self.y_ready, 1)
            if n % 2 == 0 and n:
                dve.wait_ge(self.y_ready, n)
                self.low_part(dve, n - 1)
        dve.wait_ge(self.y_ready, 2 * KT)
        self.low_part(dve, 2 * KT - 1)

    def gpsimd(self, pool):
        for n in range(0, 2 * KT, 2):
            pool.wait_ge(self.y_ready, n + 1)
            self.low_part(pool, n)

    def scalar(self, act):
        K = self.K

        def rows(half):
            tiles = slice(4 * half, 4 * half + 4)
            act.wait_ge(self.var_ready, half + 1)
            act.activation(self.std[:, tiles], self.mean_var[:, tiles, 1], ACT.Sqrt, bias=self.eps[:, :]).then_inc(self.std_ready, 1)
            act.wait_ge(self.scale_ready, half + 1)
            for t in range(4 * half, 4 * half + 4):
                act.activation(K.acc[:, t, :], K.acc[:, t, :], ACT.Identity, bias=self.shift[:, t:t + 1],
                               scale=self.rstd[:, t:t + 1]).then_inc(self.xn_ready, 1)

        def highs():
            for n in range(2 * KT):
                act.wait_ge(self.y_ready, n + 1)
                act.activation(K.hT_hi[self.part(n)], self.y[:, n % 4, :], ACT.Copy).then_inc(self.high, 1)

        rows(0)
        rows(1)
        highs()

    def tensor(self, pe, free, end):
        K = self.K
        pe.wait_ge(K.const_ready, 16)
        for n in range(2 * KT):
            half, k = n // KT, n % KT
            if k == 0:
                pe.wait_ge(self.xn_ready, 4 * half + 4)
            if n == 4:
                pe.wait_ge(free, end)
            if half:
                pe.wait_ge(self.y_ready, k + 1)
            for t in range(4 * half, 4 * half + 4):
                last = pe.transpose(K.ps[k][:, (t % 4) * P:(t % 4 + 1) * P], K.acc[:, t, k * P:(k + 1) * P], K.ident[:, :])
            last.then_inc(self.turned, 1)


def ffn_block(nc, K, name, base, presplit, first, ln, res_out=None):
    W, ps, hT_hi, hT_lo, ident = K.W, K.ps, K.hT_hi, K.hT_lo, K.ident
    with ExitStack() as ctx:
        def sb(n, shape, dt=F32):
            return ctx.enter_context(nc.sbuf_tensor(f"{name}_{n}", shape, dt))

        def sem(n):
            return ctx.enter_context(nc.semaphore(f"{name}_{n}"))

        acc = K.acc
        silu = sb("silu", [P, 2, HALF])
        g = sb("g", [P, 2, HALF])
        g_hi = sb("g_hi", [P, 2, SEQ], F32R)
        g_lo = sb("g_lo", [P, 2, SEQ], F32R)
        a_done, u_done, out_done = sem("a_done"), sem("u_done"), sem("out_done")
        a_silu, g_mul, g_high, g_ready, out_free = sem("a_silu"), sem("g_mul"), sem("g_high"), sem("g_ready"), sem("out_free")
        if first:
            in_ready = [sem(f"in_ready{s}") for s in range(4)]
            acc_ready, x_high, x_ready = sem("acc_ready"), sem("x_high"), sem("x_ready")
        R = Residual(nc, ctx, K, name, None if first else ln - 1)
        L = LayerNorm(nc, ctx, K, name, ln)
        side = K.ffn_side[name](nc, ctx, K)
        block = ctx.enter_context(nc.Block())

        def staged(x):
            return slice(None), slice(x % 2 * 4, x % 2 * 4 + 4), slice(x // 2 * HALF, (x // 2 + 1) * HALF)

        def steps(eng, body):
            with eng.Fori(0, FFN_STEPS - 1) as i:
                body(i, False)
            body(FFN_STEPS - 1, True)

        @block.sync
        def _(sp):
            if first:
                def load_x(x):
                    _, tiles, tokens = staged(x)
                    sp.dma_start(acc[staged(x)], K.xT_dram[tiles, :, tokens].rearrange("k p n -> p k n")).then_inc(in_ready[x], 16)

                W.load(sp, base, 0)
                load_x(0)
                load_x(1)
                W.load(sp, base, 1)
                load_x(2)
                load_x(3)
                sp.dma_start(ident[:, :], K.ident_dram).then_inc(K.const_ready, 16)
            R.loads(sp)
            L.loads(sp)
            side.loads(sp)
            with sp.Fori(0, FFN_STEPS) as i:
                for j in range(6):
                    W.load(sp, base + 2, j, i, 6)
            if res_out is not None:
                L.store(sp, res_out)

        @block.scalar
        def _(act):
            if first:
                W.split_hi(act, 0, base, 0)
                for x in range(4):
                    act.wait_ge(in_ready[x], 16)
                    act.activation(hT_hi[staged(x)], acc[staged(x)], ACT.Copy).then_inc(x_high, 1)
                    if x == 1:
                        W.split_hi(act, 1, base, 1)
                act.wait_ge(x_ready, 4)
                act.dma_start(acc[:, :, :], K.x_dram).then_inc(acc_ready, 16)
            elif presplit == 1:
                W.split_hi(act, 1, base, 1)

            def body(i, last):
                if last:
                    side.scalar(act)

                def silus(f):
                    for h in range(2):
                        n = 2 * f + h
                        if h == 0:
                            act.wait_ge(a_done, 2 * i + f + 1)
                        else:
                            W.done(act, base, 2 * f, i, 6)
                        act.wait_ge(g_mul, 4 * i + n + 1)
                        act.activation(silu[:, h, :], ps[h][:, :], ACT.Silu).then_inc(a_silu, 1)

                def highs(f):
                    for h in range(2):
                        n = 2 * f + h
                        act.wait_ge(g_mul, 4 * i + n + 3)
                        act.activation(g_hi[:, f, h * HALF:(h + 1) * HALF], g[:, h, :], ACT.Copy).then_inc(g_high, 1)

                W.split_hi(act, FFN_SLOT[2], base, 2, i, 6)
                silus(0)
                W.split_hi(act, FFN_SLOT[3], base, 3, i, 6)
                highs(0)
                W.split_hi(act, FFN_SLOT[4], base, 4, i, 6)
                silus(1)
                W.split_hi(act, FFN_SLOT[5], base, 5, i, 6)
                highs(1)
                W.split_hi(act, 0, base, 6, i, 6)
                W.split_hi(act, 1, base, 7, i, 6, reuse=4)

            steps(act, body)
            L.scalar(act)

        @block.gpsimd
        def _(pool):
            if first:
                pool.wait_ge(acc_ready, 16)
            R.make(pool)
            side.gpsimd(pool)
            L.gpsimd(pool)

        @block.vector
        def _(dve):
            if first:
                dve.sem_inc(W.ready, RAW_SLOTS)
                W.split_lo(dve, 0, base, 0)
                for x in range(4):
                    dve.wait_ge(x_high, x + 1)
                    dve.tensor_tensor(hT_lo[staged(x)], acc[staged(x)], hT_hi[staged(x)].bitcast(F32),
                                      ALU.subtract).then_inc(x_ready, 1)
                    if x == 1:
                        W.split_lo(dve, 1, base, 1)
            elif presplit == 1:
                W.split_lo(dve, 1, base, 1)
            side.vector(dve)
            dve.sem_inc(g_mul, 2)
            dve.sem_inc(out_free, 4)

            def body(i, last):
                def gates(f):
                    for h in range(2):
                        n = 2 * f + h
                        if h == 0:
                            dve.wait_ge(u_done, 2 * i + f + 1)
                        else:
                            W.done(dve, base, 2 * f + 1, i, 6)
                        dve.wait_ge(a_silu, 4 * i + n + 3)
                        dve.tensor_tensor(g[:, h, :], silu[:, h, :], ps[2 + h][:, :], ALU.mult).then_inc(g_mul, 1)
                        dve.wait_ge(g_high, 4 * i + n + 1)
                        dve.tensor_tensor(g_lo[:, f, h * HALF:(h + 1) * HALF], g[:, h, :],
                                          g_hi[:, f, h * HALF:(h + 1) * HALF].bitcast(F32),
                                          ALU.subtract).then_inc(g_ready, 1)

                W.split_lo(dve, FFN_SLOT[2], base, 2, i, 6)
                W.split_lo(dve, FFN_SLOT[3], base, 3, i, 6)
                gates(0)
                W.split_lo(dve, FFN_SLOT[4], base, 4, i, 6)
                W.split_lo(dve, FFN_SLOT[5], base, 5, i, 6)
                gates(1)
                W.split_lo(dve, 0, base, 6, i, 6)
                W.split_lo(dve, 1, base, 7, i, 6)
                add_out(dve, K, out_done, out_free, R.ready, i, (base, 5, i, 6), 0.5, L if last else None)

            steps(dve, body)

        @block.tensor
        def _(pe):
            if first:
                pe.sem_inc(W.used, SLOTS)
            pe.sem_inc(a_silu, 2)

            def body(i, last):
                for f in range(2):
                    for kind in range(2):
                        j = 2 * f + kind
                        W.wait(pe, base, j, i, 6)
                        s = FFN_SLOT[j]
                        for h in range(2):
                            n = 2 * f + h
                            if first and j == 0:
                                pe.wait_ge(x_ready, 2 * h + 2)
                            pe.wait_ge((a_silu, g_mul)[kind], 4 * i + n + 1)
                            ins = product(pe, ps[2 * kind + h][:, :], [
                                (W.hi[:, s, k * P:(k + 1) * P], W.lo[:, s, k * P:(k + 1) * P],
                                 hT_hi[:, k, h * HALF:(h + 1) * HALF], hT_lo[:, k, h * HALF:(h + 1) * HALF])
                                for k in range(KT)])
                            ins.then_inc(W.used if h else (a_done, u_done)[kind], 1)
                W.wait(pe, base, 4, i, 6)
                W.wait(pe, base, 5, i, 6)
                out_product(pe, K, FFN_SLOT[4:], g_hi, g_lo, g_ready, out_free, out_done, i)

            steps(pe, body)
            L.tensor(pe, out_free, 16 * FFN_STEPS + 4)


class NoSide:

    def __init__(self, nc, ctx, K):
        pass

    def loads(self, sp):
        pass

    scalar = vector = gpsimd = loads


JOBS = 8
MAIN_BANKS, SCORE_BANKS, TURN_BANK, OUT_BANKS = (0, 1, 2), (3, 4), 5, (6, 7)
POSITIONS = 24
JOB_POS = [5, 6, 7, 8, 8, 9, 10, 10]
NEG = -3.0e38
TWO_PI_PARTS = (6.28125, 0.001934051513671875, 1.2554228305816650390625e-06)
SWAP_ROPE_HALVES = list(range(8, 16)) + list(range(8)) + list(range(16, 32))


def query_tokens(g, dj):
    if g == 0:
        return slice(dj * P, (dj + 1) * P)
    if g == 1:
        first = dj // 2 + 4 * P * (dj % 2)
        return slice(first, first + 4 * (P - 1) + 1, 4)
    return slice(dj, dj + 8 * (P - 1) + 1, 8)


def key_tiles(g, dj):
    return 1 if g == 2 or (g == 0 and dj == 0) or (g == 1 and dj % 2 == 0) else 2


def key_tokens(g, dj):
    if key_tiles(g, dj) == 1:
        return query_tokens(g, dj)
    if g == 0:
        return slice((dj - 1) * P, (dj + 1) * P)
    return slice(dj // 2, dj // 2 + 4 * (2 * P - 1) + 1, 4)


def token_order(ap, g, x):
    if g == 0:
        return ap[:, x * HALF:(x + 1) * HALF].rearrange("p (r j) -> p r j", r=2)
    r = 4 if g == 1 else 8
    v = ap.rearrange("p (j r) -> p r j", r=r)
    return v[:, x * r // 2:(x + 1) * r // 2, :]


def tile_order(ap, g):
    return ap.rearrange("p (r j) -> p r j", r=4 if g == 2 else 2)


def score_uses():
    order = []
    for pos in range(POSITIONS + 1):
        for g in range(GROUPS):
            if pos == 6 * g + 12:
                order.append(("spread", g))
        for g in range(GROUPS):
            order += [("job", g, dj) for dj in range(JOBS) if JOB_POS[dj] + 6 * g == pos]
    return {key: n for n, key in enumerate(order)}


def at_position(pos, lag):
    return [(g, dj) for g in range(GROUPS) for dj in range(JOBS) if JOB_POS[dj] + 6 * g + lag == pos]


def attention_block(nc, K):
    W, ps, hT_hi, hT_lo, ident = K.W, K.ps, K.hT_hi, K.hT_lo, K.ident
    USE = score_uses()
    N_USE = len(USE)
    base = ATT_BASE
    with ExitStack() as ctx:
        def sb(n, shape, dt=F32):
            return ctx.enter_context(nc.sbuf_tensor(f"att_{n}", shape, dt))

        def sem(n):
            return ctx.enter_context(nc.semaphore(f"att_{n}"))

        qT = [sb(f"qT{s}", [P, SEQ]) for s in range(2)]
        kT = [sb(f"kT{s}", [P, SEQ]) for s in range(2)]
        V = [sb(f"V{s}", [P, JOBS, P]) for s in range(2)]
        vT = sb("vT", [P, SEQ])
        cos, sin = sb("cos", [P, SEQ]), sb("sin", [P, SEQ])
        rope_cols = sb("rope_cols", [P, 2])
        mask2, mask3 = sb("mask2", [P, 2 * P]), sb("mask3", [P, P])
        z, swapped = sb("z", [P, 2, HALF]), sb("swapped", [P, 2, HALF])
        prob, probT = sb("prob", [P, 2, 2, 2 * P]), sb("probT", [P, 2, 4, P])
        gate = sb("gate", [P, 2, HALF])
        O = [sb(f"O{g}", [P, SEQ]) for g in range(GROUPS)]
        lse = [sb(f"lse{g}", [P, SEQ]) for g in range(GROUPS)]
        total = sb("total", [P, SEQ])
        spread = sb("spread", [P, JOBS, 2, DH])
        row_max, row_sum = sb("row_max", [P, GROUPS, JOBS, 2]), sb("row_sum", [P, GROUPS, JOBS, 2])
        neg_max, inv_sum = sb("neg_max", [P, 2, 2]), sb("inv_sum", [P, 2, 2])
        log_sum, row_lse = sb("log_sum", [P, JOBS * 2]), sb("row_lse", [P, JOBS * 2])

        setup, pos_ready, sin_ready = Step(sem("setup")), sem("pos_ready"), sem("sin_ready")
        main_done, main_free = sem("main_done"), sem("main_free")
        z_swapped, rope_part, rope_done = sem("z_swapped"), sem("rope_part"), sem("rope_done")
        vt_turned = sem("vt_turned")
        turn_free = sem("turn_free")
        score_done, score_free = sem("score_done"), sem("score_free")
        negmax_done, exp_done, inv_done, prob_done = sem("negmax_done"), sem("exp_done"), sem("inv_done"), sem("prob_done")
        prob_turned = sem("prob_turned")
        pv_done, out_free = sem("pv_done"), sem("out_free")
        log_done, lse_done, spread_done, spread_turned = sem("log_done"), sem("lse_done"), sem("spread_done"), sem("spread_turned")
        merge, weights_ready, weighted = sem("merge"), sem("weights_ready"), sem("weighted")
        merged, att_stored = sem("merged"), sem("att_stored")
        gate_stored = [sem(f"gate_stored{h}") for h in range(2)]
        MERGE_STEPS = 11
        block = ctx.enter_context(nc.Block())

        @block.sync
        def _(sp):
            sp.dma_start(vT[:, :].bitcast(I32), K.positions_dram.broadcast_to([P, SEQ])).then_inc(pos_ready, 16)
            sp.dma_start(rope_cols[:, :], K.rope_cols_dram).then_inc(pos_ready, 16)
            sp.dma_start(mask2[:, :], K.mask2_dram).then_inc(pos_ready, 16)
            sp.dma_start(mask3[:, :], K.mask3_dram).then_inc(pos_ready, 16)
            for h in range(2):
                sp.sem_inc(gate_stored[h], 16)
            sp.sem_inc(att_stored, 16)
            W.load(sp, base + 2, 0)
            with sp.Fori(0, PAIRS) as i:
                for j in range(1, 13):
                    W.load(sp, base + 2, j, i, 12)
                for n in range(3):
                    for h in range(2):
                        sp.wait_ge(main_free, POSITIONS * i + 18 + 2 * n + h + 1 + 3)
                        sp.dma_start(K.gates_scratch[3 * i + n, :, h * HALF:(h + 1) * HALF], gate[:, h, :])\
                          .then_inc(gate_stored[h], 16)
                sp.wait_ge(merged, i + 1)
                sp.dma_start(K.att_scratch[i, :, :], O[0][:, :]).then_inc(att_stored, 16)
            for h in range(2):
                sp.wait_ge(gate_stored[h], 16 * (3 * PAIRS + 1))
            sp.wait_ge(att_stored, 16 * (PAIRS + 1))

        @block.scalar
        def _(act):
            act.wait_ge(sin_ready, 1)
            act.activation(sin[:, :], total[:, :], ACT.Sin).then_inc(sin_ready, 1)
            act.activation(cos[:, :], O[0][:, :], ACT.Sin).then_inc(sin_ready, 1)
            W.split_hi(act, 2, base, 2)
            act.sem_inc(main_free, 3)
            with act.Fori(0, PAIRS) as i:
                def evacuate(hx):
                    unit, h = hx // 2, hx % 2
                    act.wait_ge(main_done, POSITIONS * i + hx + 1)
                    if unit >= 9:
                        act.wait_ge(gate_stored[h], 16 * (unit - 9) + 16 + 48 * i)
                        out = gate[:, h, :]
                    elif unit % 3 == 2:
                        act.wait_ge(vt_turned, 2 * (unit // 3) + 6 * i + 2)
                        out = vT[:, h * HALF:(h + 1) * HALF]
                    else:
                        rn = 4 * (unit // 3) + 2 * (unit % 3) + h
                        act.wait_ge(rope_done, 12 * i + rn + 1)
                        out = z[:, h, :]
                    act.activation(out, ps[MAIN_BANKS[hx % 3]][:, :], ACT.Copy).then_inc(main_free, 1)

                for pos in range(POSITIONS + 1):
                    if pos >= 1:
                        evacuate(pos - 1)
                    if pos % 2 == 0 and 2 <= pos < POSITIONS:
                        j = pos // 2 + 2
                        W.split_hi(act, j % SLOTS, base, j, i, 12)
                    for g in range(GROUPS):
                        if pos == 6 * g + 11:
                            act.wait_ge(lse_done, 3 * i + g + 1)
                            act.wait_ge(exp_done, 24 * i + 8 * g + 8)
                            act.activation(log_sum[:, :], row_sum[:, g, :, :].rearrange("p a b -> p (a b)"), ACT.Ln)\
                               .then_inc(log_done, 1)
                    for g, dj in at_position(pos, 1):
                        jn = 24 * i + 8 * g + dj
                        nk = key_tiles(g, dj)
                        act.wait_ge(prob_turned, jn + 3)
                        act.wait_ge(pv_done, jn + 23)
                        src = ps[TURN_BANK][:, :].rearrange("p (h k q) -> p h k q", h=2, k=2)[:, :, 2 - nk:2, :]
                        dst = probT[:, dj % 2, :, :].rearrange("p (h k) q -> p h k q", h=2)[:, :, 2 - nk:2, :]
                        act.activation(dst, src, ACT.Copy).then_inc(turn_free, 1)
                    for g, dj in at_position(pos, 0):
                        jn = 24 * i + 8 * g + dj
                        first = 2 * P - P * key_tiles(g, dj)
                        act.wait_ge(negmax_done, jn + 1)
                        for h in range(2):
                            s = prob[:, dj % 2, h, first:2 * P]
                            ins = act.activation(s, s, ACT.Exp, bias=neg_max[:, dj % 2, h:h + 1], scale=ATT_SCALE,
                                                 accum_out=row_sum[:, g, dj, h:h + 1])
                        ins.then_inc(exp_done, 1)
                W.split_hi(act, 2, base, 14, i, 12)
                for g in range(GROUPS):
                    act.wait_ge(merge, MERGE_STEPS * i + 3 + g)
                    act.activation(lse[g][:, :], lse[g][:, :], ACT.Exp).then_inc(weights_ready, 1)

        @block.gpsimd
        def _(pool):
            pool.sem_inc(rope_done, 2)
            pool.wait_ge(sin_ready, 4)
            with pool.Fori(0, PAIRS) as i:
                def rope(g, part, h):
                    rn = 4 * g + 2 * part + h
                    hx = 6 * g + 2 * part + h
                    cols = slice(h * HALF, (h + 1) * HALF)
                    dst = (qT, kT)[part][g % 2][:, cols]
                    if h == 0:
                        pool.wait_ge(score_done, 24 * i + (24, 16, 32)[g])
                    pool.wait_ge(main_free, POSITIONS * i + hx + 4)
                    pool.tensor_tensor(dst, z[:, h, :], cos[:, cols], ALU.mult).then_inc(rope_part, 1)
                    pool.wait_ge(z_swapped, 12 * i + rn + 1)
                    pool.tensor_tensor(swapped[:, h, :], swapped[:, h, :], sin[:, cols], ALU.mult).then_inc(rope_part, 1)
                    pool.wait_ge(rope_part, 24 * i + 2 * rn + 2)
                    pool.tensor_tensor(dst, dst, swapped[:, h, :], ALU.add).then_inc(rope_done, 1)

                def spread_lse(g):
                    pool.wait_ge(lse_done, 3 * i + g + 2)
                    pool.wait_ge(spread_turned, 6 * i + 2 * g + 2)
                    K.past_waits(pool)
                    pool.tensor_copy(spread[:, :, :, :], row_lse[:, :].rearrange("p (a b) -> p a b", b=2)
                                     .unsqueeze(3).broadcast_to([P, JOBS, 2, DH])).then_inc(spread_done, 1)

                for g in range(GROUPS):
                    for part in range(2):
                        for h in range(2):
                            rope(g, part, h)
                    if g >= 1:
                        spread_lse(g - 1)
                spread_lse(2)
                for g in range(GROUPS):
                    pool.wait_ge(weights_ready, 3 * i + g + 1)
                    pool.wait_ge(out_free, 6 * (i + 1) + 2)
                    pool.tensor_tensor(O[g][:, :], O[g][:, :], lse[g][:, :], ALU.mult).then_inc(weighted, 1)

        @block.vector
        def _(dve):
            angle, turns, x, y = total[:, :], O[1][:, :], O[0][:, :], O[2][:, :]
            dve.wait_ge(pos_ready, 64)
            setup.after(dve, dve.tensor_copy(angle, vT[:, :].bitcast(I32)))
            setup.after(dve, dve.tensor_scalar(angle, angle, rope_cols[:, 0:1], None, ALU.mult))
            setup.after(dve, dve.tensor_scalar(turns, angle, 1.0 / (2 * math.pi), 12582912.0, ALU.mult, ALU.add))
            setup.after(dve, dve.tensor_scalar(turns, turns, 12582912.0, None, ALU.subtract))
            for part in TWO_PI_PARTS:
                setup.after(dve, dve.scalar_tensor_tensor(angle, turns, -part, angle, ALU.mult, ALU.add))
            setup.after(dve, dve.tensor_scalar(angle, angle, -3.1415925, 3.1415925, ALU.max, ALU.min))
            setup.after(dve, dve.scalar_tensor_tensor(x, angle, -1.0, angle, ALU.mult, ALU.max))
            setup.after(dve, dve.tensor_scalar(x, x, -1.0, math.pi / 2, ALU.mult, ALU.add))
            dve.sem_inc(sin_ready, 1)
            W.split_lo(dve, 2, base, 2)
            dve.wait_ge(sin_ready, 3)
            dve.tensor_scalar(sin[:, :], sin[:, :], rope_cols[:, 1:2], None, ALU.mult).then_inc(sin_ready, 1)
            dve.sem_inc(turn_free, 1)
            dve.sem_inc(score_free, 2)
            dve.sem_inc(out_free, 2)
            dve.sem_inc(lse_done, 1)
            with dve.Fori(0, PAIRS) as i:
                for pos in range(POSITIONS + 1):
                    if pos % 2 == 0 and 2 <= pos < POSITIONS:
                        j = pos // 2 + 2
                        W.split_lo(dve, j % SLOTS, base, j, i, 12)
                    hx = pos - 1
                    if pos >= 1 and hx // 2 < 9 and (hx // 2) % 3 < 2:
                        rn = 4 * (hx // 6) + 2 * ((hx // 2) % 3) + hx % 2
                        dve.wait_ge(main_free, POSITIONS * i + hx + 4)
                        dve.wait_ge(rope_done, 12 * i + rn + 1)
                        K.past_waits(dve)
                        dve.stream_shuffle(swapped[:, hx % 2, :], z[:, hx % 2, :], SWAP_ROPE_HALVES).then_inc(z_swapped, 1)
                    for g in range(GROUPS):
                        if pos == 6 * g + 6:
                            dve.wait_ge(pv_done, 24 * i + (24, 16, 32)[g])
                            for x2 in range(2):
                                dve.wait_ge(vt_turned, 6 * i + 2 * g + x2 + 3)
                                dve.tensor_copy(V[g % 2][:, 4 * x2:4 * x2 + 4, :],
                                                ps[TURN_BANK][:, :].rearrange("p (k c) -> p k c", k=4)).then_inc(turn_free, 1)
                        if pos == 6 * g + 11:
                            dve.wait_ge(log_done, 3 * i + g + 1)
                            dve.wait_ge(spread_done, 3 * i + g + 1)
                            dve.scalar_tensor_tensor(row_lse[:, :], row_max[:, g, :, :].rearrange("p a b -> p (a b)"),
                                                     ATT_SCALE, log_sum[:, :], ALU.mult, ALU.add).then_inc(lse_done, 1)
                        if pos == 6 * g + 12:
                            for x2 in range(2):
                                dve.wait_ge(spread_turned, 6 * i + 2 * g + x2 + 3)
                                dve.tensor_copy(token_order(lse[g][:, :], g, x2), tile_order(ps[SCORE_BANKS[x2]][:, :], g))\
                                   .then_inc(score_free, 1)
                    for g, dj in at_position(pos, 0):
                        jn = 24 * i + 8 * g + dj
                        nk = key_tiles(g, dj)
                        mask = mask3[:, :] if g == 2 else mask2[:, 2 * P - nk * P:2 * P]
                        dve.wait_ge(score_done, jn + 25)
                        dve.wait_ge(prob_turned, jn + 1)
                        K.past_waits(dve)
                        for h in range(2):
                            dve.tensor_tensor_reduce(
                                prob[:, dj % 2, h, 2 * P - nk * P:2 * P], ps[SCORE_BANKS[h]][:, 0:nk * P], mask,
                                1.0, NEG, ALU.add, ALU.max, row_max[:, g, dj, h:h + 1]).then_inc(score_free, 1)
                        dve.wait_ge(score_free, 2 * N_USE * i + 2 * USE["job", g, dj] + 4)
                        dve.tensor_scalar(neg_max[:, dj % 2, :], row_max[:, g, dj, :], -ATT_SCALE, None, ALU.mult)\
                           .then_inc(negmax_done, 1)
                    for g, dj in at_position(pos, 0):
                        jn = 24 * i + 8 * g + dj
                        first = 2 * P - P * key_tiles(g, dj)
                        dve.wait_ge(exp_done, jn + 1)
                        dve.reciprocal(inv_sum[:, dj % 2, :], row_sum[:, g, dj, :]).then_inc(inv_done, 1)
                        dve.wait_ge(inv_done, jn + 1)
                        for h in range(2):
                            s = prob[:, dj % 2, h, first:2 * P]
                            ins = dve.tensor_scalar(s, s, inv_sum[:, dj % 2, h:h + 1], None, ALU.mult)
                        ins.then_inc(prob_done, 1)
                    for g, dj in at_position(pos, 2):
                        if dj % 4 == 3:
                            jn = 24 * i + 8 * g + dj
                            dve.wait_ge(pv_done, jn + 25)
                            if g == 0 and dj == 3:
                                dve.wait_ge(att_stored, 16 * i + 16)
                            dve.tensor_copy(token_order(O[g][:, :], g, dj // 4),
                                            tile_order(ps[OUT_BANKS[dj // 4]][:, :], g)).then_inc(out_free, 1)
                W.split_lo(dve, 2, base, 14, i, 12)
                steps = 0

                def step(ins):
                    nonlocal steps
                    steps += 1
                    ins.then_inc(merge, 1)
                    dve.wait_ge(merge, MERGE_STEPS * i + steps)

                dve.wait_ge(score_free, 2 * N_USE * (i + 1) + 2)
                step(dve.tensor_tensor(total[:, :], lse[0][:, :], lse[1][:, :], ALU.max))
                step(dve.tensor_tensor(total[:, :], total[:, :], lse[2][:, :], ALU.max))
                for g in range(GROUPS):
                    step(dve.tensor_tensor(lse[g][:, :], lse[g][:, :], total[:, :], ALU.subtract))
                dve.wait_ge(weights_ready, 3 * i + 3)
                step(dve.tensor_tensor(total[:, :], lse[0][:, :], lse[1][:, :], ALU.add))
                step(dve.tensor_tensor(total[:, :], total[:, :], lse[2][:, :], ALU.add))
                step(dve.reciprocal(total[:, :], total[:, :]))
                dve.wait_ge(weighted, 3 * i + 3)
                step(dve.tensor_tensor(O[1][:, :], O[1][:, :], O[2][:, :], ALU.add))
                step(dve.tensor_tensor(O[0][:, :], O[0][:, :], O[1][:, :], ALU.add))
                step(dve.tensor_tensor(O[0][:, :], O[0][:, :], total[:, :], ALU.mult))
                dve.sem_inc(merged, 1)
                assert steps == MERGE_STEPS

        @block.tensor
        def _(pe):
            pe.sem_inc(vt_turned, 2)
            pe.sem_inc(score_done, 24)
            pe.sem_inc(prob_turned, 2)
            pe.sem_inc(pv_done, 24)
            pe.sem_inc(spread_turned, 2)
            pe.sem_inc(spread_done, 1)
            with pe.Fori(0, PAIRS) as i:
                for pos in range(POSITIONS + 1):
                    for g in range(GROUPS):
                        if pos == 6 * g + 12:
                            pe.wait_ge(spread_done, 3 * i + g + 2)
                            for x2 in range(2):
                                pe.wait_ge(score_free, 2 * N_USE * i + 2 * USE["spread", g] + x2 + 1)
                                for q in range(4):
                                    ins = pe.transpose(ps[SCORE_BANKS[x2]][:, q * P:(q + 1) * P],
                                                       spread[:, 4 * x2 + q, :, :].rearrange("p a b -> p (a b)"), ident[:, :])
                                ins.then_inc(spread_turned, 1)

                    def scores(g, dj):
                        nk = key_tiles(g, dj)
                        if dj == 0:
                            pe.wait_ge(rope_done, 12 * i + 4 * (g + 1) + 2)
                        for h in range(2):
                            pe.wait_ge(score_free, 2 * N_USE * i + 2 * USE["job", g, dj] + h + 1)
                            rows = slice(h * DH, (h + 1) * DH)
                            ins = pe.matmul(ps[SCORE_BANKS[h]][:, 0:nk * P],
                                            qT[g % 2][rows, query_tokens(g, dj)], kT[g % 2][rows, key_tokens(g, dj)],
                                            start=True, stop=True)
                        ins.then_inc(score_done, 1)

                    def turn_v(g, x2):
                        pe.wait_ge(turn_free, 30 * i + 10 * g + x2 + 1)
                        for q in range(4):
                            ins = pe.transpose(ps[TURN_BANK][:, q * P:(q + 1) * P], vT[:, query_tokens(g, 4 * x2 + q)], ident[:, :])
                        ins.then_inc(vt_turned, 1)

                    for g in range(GROUPS):
                        if pos == 6 * g + 6:
                            pe.wait_ge(main_free, POSITIONS * i + 6 * g + 6 + 3)
                            turn_v(g, 0)
                    jobs = at_position(pos, 0)
                    if jobs:
                        scores(*jobs[0])
                    for g in range(GROUPS):
                        if pos == 6 * g + 6:
                            turn_v(g, 1)
                    for g, dj in at_position(pos, 1):
                        nk = key_tiles(g, dj)
                        pe.wait_ge(prob_done, 24 * i + 8 * g + dj + 1)
                        pe.wait_ge(turn_free, 30 * i + 10 * g + 2 + dj + 1)
                        for h in range(2):
                            for kt in range(2 - nk, 2):
                                ins = pe.transpose(ps[TURN_BANK][:, (2 * h + kt) * P:(2 * h + kt + 1) * P],
                                                   prob[:, dj % 2, h, kt * P:(kt + 1) * P], ident[:, :])
                        ins.then_inc(prob_turned, 1)
                    for g, dj in at_position(pos, 2):
                        nk = key_tiles(g, dj)
                        pe.wait_ge(turn_free, 30 * i + 10 * g + 2 + dj + 2)
                        if dj % 4 == 0:
                            pe.wait_ge(out_free, 6 * i + 2 * g + dj // 4 + 1)
                        for h in range(2):
                            cols = slice(h * DH, (h + 1) * DH)
                            for kt in range(2 - nk, 2):
                                ins = pe.matmul(ps[OUT_BANKS[dj // 4]][cols, (dj % 4) * P:(dj % 4 + 1) * P],
                                                V[g % 2][:, dj - 1 + kt, cols], probT[:, dj % 2, 2 * h + kt, :],
                                                start=(kt == 2 - nk), stop=(kt == 1))
                        ins.then_inc(pv_done, 1)
                    if pos < POSITIONS:
                        j, h = pos // 2, pos % 2
                        if h == 0:
                            W.wait(pe, base, j, i, 12)
                        pe.wait_ge(main_free, POSITIONS * i + pos + 1)
                        s = j % SLOTS
                        terms = [(W.hi[:, s, k * P:(k + 1) * P], W.lo[:, s, k * P:(k + 1) * P],
                                  hT_hi[:, k, h * HALF:(h + 1) * HALF], hT_lo[:, k, h * HALF:(h + 1) * HALF])
                                 for k in range(KT)]
                        product(pe, ps[MAIN_BANKS[pos % 3]][:, :], terms[:KT // 2], stop=False)
                        if len(jobs) == 2:
                            scores(*jobs[1])
                        product(pe, ps[MAIN_BANKS[pos % 3]][:, :], terms[KT // 2:], start=False).then_inc(main_done, 1)
                        if h == 1:
                            pe.wait_ge(main_done, POSITIONS * i + pos + 1)
                            pe.sem_inc(W.used, 1)


CHAIN = 43
AFTER_KEYS, AFTER_DIAGONAL, AFTER_STATES = 1, 5, 39


def after_level(l):
    return AFTER_DIAGONAL + 4 * l + 2


def rights(ap, m):
    return ap.rearrange("p (b two m) -> p b two m", two=2, m=m)[:, :, 1, :]


def lefts(ap, m):
    return ap.rearrange("p (b two m) -> p b two m", two=2, m=m)[:, :, 0, :]


def hgrn_block(nc, K):
    W, ps, hT_hi, hT_lo, ident = K.W, K.ps, K.hT_hi, K.hT_lo, K.ident
    MAIN, LEVEL, TURN, OUT, MEAN = (0, 1), (2, 3), 4, (5, 6), 7
    with ExitStack() as ctx:
        def sb(n, shape, dt=F32):
            return ctx.enter_context(nc.sbuf_tensor(f"hg_{n}", shape, dt))

        def sem(n):
            return ctx.enter_context(nc.semaphore(f"hg_{n}"))

        Q = [sb(f"Q{s}", [P, SEQ]) for s in range(2)]
        F = [sb(f"F{s}", [P, SEQ]) for s in range(2)]
        G = [sb(f"G{s}", [P, SEQ]) for s in range(2)]
        keys, prods, vT = sb("keys", [P, SEQ]), sb("prods", [P, SEQ]), sb("vT", [P, SEQ])
        V, keysT = sb("V", [P, CHUNKS, P]), sb("keysT", [P, CHUNKS, P])
        att = sb("att", [P, CHUNKS, P])
        state = sb("state", [P, CHUNKS, P])
        z, sig = sb("z", [P, 2, HALF]), sb("sig", [P, 2, HALF])
        sq, rms, o = sb("sq", [P, 2, HALF]), sb("rms", [P, 2, HALF]), sb("o", [P, SEQ])
        masks = sb("masks", [P, len(LEVELS), CHUNK // 2], I32)
        logits, lb, one_minus_lb = sb("logits", [P, 2, HEADS]), sb("lb", [P, HEADS]), sb("one_minus_lb", [P, HEADS])
        lb_tmp, lb_exp = sb("lb_tmp", [P, HEADS]), sb("lb_exp", [P, 2, HEADS])
        norm_g, mean_w, eps = sb("norm_g", [P, HEADS]), sb("mean_w", [P, P]), sb("eps", [P, 1])

        setup, loaded, lb_ready, lb_expd = Step(sem("setup")), sem("loaded"), sem("lb_ready"), sem("lb_expd")
        main_done, main_read = sem("main_done"), sem("main_read")
        pool_used, dve_used = sem("pool_used"), sem("dve_used")
        v_turned, v_ready, k_turned, k_ready = sem("v_turned"), sem("v_ready"), sem("k_turned"), sem("k_ready")
        level_done, update_done, chain = sem("level_done"), sem("update_done"), sem("chain")
        o_done, squared, mean_done, rms_done = sem("o_done"), sem("squared"), sem("mean_done"), sem("rms_done")
        gated, stored = sem("gated"), sem("stored")
        gate_stored = [sem(f"gate_stored{h}") for h in range(2)]
        block = ctx.enter_context(nc.Block())

        def passes(eng, body):
            body(None, 0, 0, True)
            with eng.Fori(0, (HEADS - 2) // 2) as it:
                for a in range(2):
                    body(it, a, 1, True)
            body(0, HEADS - 2, 0, True)
            body(0, HEADS - 1, 0, False)

        def which(it, a, looped):
            if it is None:
                return None, None, 0, (0, 0)
            n = 2 * it + a if looped else a
            return n, a % 2, n + 1, ((4 * (a + 1), it) if looped else (4 * (a + 1), 0))

        @block.sync
        def _(sp):
            sp.dma_start(masks[:, :, :], K.level_masks_dram).then_inc(loaded, 16)
            sp.dma_start(logits[:, :, :], K.lb_logits_dram).then_inc(loaded, 16)
            sp.dma_start(norm_g[:, :], K.norm_g_dram).then_inc(loaded, 16)
            sp.sem_inc(stored, 16)
            W.load(sp, GATE_BASE, 3)
            for j in range(2):
                W.load(sp, HGRN_BASE, j)
            for n in range(GATE_UNITS):
                for h in range(2):
                    sp.wait_ge(main_read, 2 * n + h + 3)
                    sp.dma_start(K.gates_scratch[3 * PAIRS + n, :, h * HALF:(h + 1) * HALF], z[:, h, :]).then_inc(gate_stored[h], 16)
                if n < 2:
                    W.load(sp, HGRN_BASE, n + 2)
            for j in range(4, 8):
                W.load(sp, HGRN_BASE, j)

            def store(n):
                sp.wait_ge(gated, 2 * n + 2)
                sp.dma_start(K.hgrn_scratch[n, :, :], o[:, :]).then_inc(stored, 16)

            with sp.Fori(0, (HEADS - 2) // 2) as it:
                for a in range(2):
                    for j in range(4):
                        W.load(sp, HGRN_BASE, 4 * (a + 2) + j, it, 8)
                    store(2 * it + a)
            for j in range(2):
                W.load(sp, MERGE_BASE, j)
            store(HEADS - 2)
            store(HEADS - 1)
            sp.wait_ge(stored, 16 * (HEADS + 1))
            for h in range(2):
                sp.wait_ge(gate_stored[h], 16 * GATE_UNITS)

        @block.scalar
        def _(act):
            act.wait_ge(lb_ready, 1)
            act.activation(lb_exp[:, :, :], logits[:, :, :], ACT.Exp).then_inc(lb_expd, 1)
            act.sem_inc(main_read, 2)
            act.sem_inc(k_ready, 1)
            act.sem_inc(rms_done, 1)
            for n in range(GATE_UNITS):
                if n >= 1:
                    W.split_hi(act, (n + 2) % SLOTS, GATE_BASE, n + 2)
                for h in range(2):
                    act.wait_ge(main_done, 2 * n + h + 1)
                    if n:
                        act.wait_ge(gate_stored[h], 16 * n)
                    act.activation(z[:, h, :], ps[MAIN[h]][:, :], ACT.Copy).then_inc(main_read, 1)
            for h in range(2):
                act.wait_ge(gate_stored[h], 16 * GATE_UNITS)

            def body(it, a, looped, projecting):
                n, par, nxt, (first, w_it) = which(it, a, looped)

                def evacuate(k):
                    if not projecting:
                        return
                    unit, h = k // 2, k % 2
                    act.wait_ge(main_done, 8 + 8 * nxt + k + 1)
                    bank = ps[MAIN[k % 2]][:, :]
                    if unit == 2:
                        act.wait_ge(v_turned, 2 * nxt + 2)
                        act.activation(vT[:, h * HALF:(h + 1) * HALF], bank, ACT.Copy).then_inc(main_read, 1)
                        return
                    if unit == 0:
                        act.wait_ge(pool_used, 4 * nxt + h + 1)
                    elif unit == 1:
                        act.wait_ge(pool_used, 4 * nxt + h + 3)
                    else:
                        act.wait_ge(dve_used, 2 * nxt + h + 1)
                    if unit != 1:
                        act.activation(z[:, h, :], bank, ACT.Copy)
                    act.activation(sig[:, h, :], bank, ACT.Sigmoid).then_inc(main_read, 1)

                def split(j):
                    if projecting and not (n == HEADS - 2 and j == 3 if not looped else False):
                        act_first = first + j + 2
                        W.split_hi(act, (j + 2) % SLOTS, HGRN_BASE, act_first, w_it, 8 if looped else 0)

                split(0)
                if n is not None:
                    for x in range(2):
                        act.wait_ge(v_turned, 2 * n + x + 3)
                        act.activation(V[:, 4 * x:4 * x + 4, :], ps[TURN][:, :].rearrange("p (c v) -> p c v", c=4), ACT.Copy)\
                           .then_inc(v_ready, 1)
                evacuate(0)
                evacuate(1)
                split(1)
                evacuate(2)
                evacuate(3)
                split(2)
                evacuate(4)
                if n is not None:
                    for x in range(2):
                        act.wait_ge(k_turned, 2 * n + x + 3)
                        act.activation(keysT[:, 4 * x:4 * x + 4, :], ps[TURN][:, :].rearrange("p (c v) -> p c v", c=4), ACT.Copy)\
                           .then_inc(k_ready, 1)
                        if x == 0:
                            evacuate(5)
                            split(3)
                    evacuate(6)
                    for x in range(2):
                        act.wait_ge(o_done, 2 * n + x + 2)
                        act.activation(sq[:, x, :], ps[OUT[x]][:, :], ACT.Square).then_inc(squared, 1)
                    for x in range(2):
                        act.wait_ge(mean_done, 2 * n + x + 1)
                        act.activation(rms[:, x, :], ps[MEAN][:, :], ACT.Sqrt, bias=eps[:, :]).then_inc(rms_done, 1)
                else:
                    evacuate(5)
                    split(3)
                    evacuate(6)
                evacuate(7)

            passes(act, body)

        @block.gpsimd
        def _(pool):
            pool.memset(mean_w[:, :], 1.0 / P).then_inc(setup.sem, 1)
            pool.memset(eps[:, :], RMS_EPS).then_inc(setup.sem, 1)
            pool.sem_inc(pool_used, 2)

            def body(it, a, looped, projecting):
                n, par, nxt, _ = which(it, a, looped)
                other = 0 if n is None else 1 - par

                def gate(dst, unit, h):
                    pool.wait_ge(main_read, 8 + 8 * nxt + 2 * unit + h + 3)
                    if unit == 0 and h == 0 and n is not None:
                        pool.wait_ge(o_done, 2 * n + 1)
                    pool.tensor_tensor(dst[:, h * HALF:(h + 1) * HALF], z[:, h, :], sig[:, h, :], ALU.mult).then_inc(pool_used, 1)

                if projecting:
                    for h in range(2):
                        gate(Q[other], 0, h)
                    for h in range(2):
                        gate(G[other], 3, h)
                if n is not None:
                    for x in range(2):
                        pool.wait_ge(chain, CHAIN * n + 42 + x)
                        part = o[:, x * HALF:(x + 1) * HALF]
                        pool.tensor_tensor(part, part, G[par][:, x * HALF:(x + 1) * HALF], ALU.mult).then_inc(gated, 1)

            passes(pool, body)

        @block.vector
        def _(dve):
            dve.wait_ge(loaded, 48)
            setup.count = 2
            setup.after(dve, dve.tensor_tensor(lb_tmp[:, :], logits[:, 0, :], logits[:, 1, :], ALU.max))
            for r in range(2):
                setup.after(dve, dve.tensor_tensor(logits[:, r, :], logits[:, r, :], lb_tmp[:, :], ALU.subtract))
            dve.sem_inc(lb_ready, 1)
            dve.wait_ge(lb_expd, 1)
            setup.after(dve, dve.tensor_tensor(lb_tmp[:, :], lb_exp[:, 0, :], lb_exp[:, 1, :], ALU.add))
            setup.after(dve, dve.reciprocal(lb_tmp[:, :], lb_tmp[:, :]))
            setup.after(dve, dve.tensor_tensor(lb[:, :], lb_exp[:, 0, :], lb_tmp[:, :], ALU.mult))
            setup.after(dve, dve.tensor_scalar(one_minus_lb[:, :], lb[:, :], -1.0, 1.0, ALU.mult, ALU.add))
            for n in range(1, GATE_UNITS):
                W.split_lo(dve, (n + 2) % SLOTS, GATE_BASE, n + 2)

            def body(it, a, looped, projecting):
                n, par, nxt, (first, w_it) = which(it, a, looped)
                other = 0 if n is None else 1 - par
                steps = 0

                def step(ins, wait=False):
                    nonlocal steps
                    steps += 1
                    ins.then_inc(chain, 1)
                    if wait:
                        dve.wait_ge(chain, CHAIN * n + steps)

                def split(j):
                    if projecting and not (n == HEADS - 2 and j == 3 if not looped else False):
                        W.split_lo(dve, (j + 2) % SLOTS, HGRN_BASE, first + j + 2, w_it, 8 if looped else 0)

                def decay(h):
                    if not projecting:
                        return
                    dve.wait_ge(main_read, 8 + 8 * nxt + 2 + h + 3)
                    head = slice(nxt, nxt + 1) if isinstance(nxt, int) else bass.ds(nxt, 1)
                    dve.tensor_scalar(F[other][:, h * HALF:(h + 1) * HALF], sig[:, h, :], one_minus_lb[:, head], lb[:, head],
                                      ALU.mult, ALU.add).then_inc(dve_used, 1)

                split(0)
                if n is None:
                    split(1)
                    decay(0)
                    decay(1)
                    split(2)
                    split(3)
                    return
                Qn, Fn = Q[par], F[par]
                tp = {1: Fn[:, :]}
                at = 0
                for m in LEVELS:
                    tp[2 * m] = prods[:, at:at + SEQ // (2 * m)]
                    at += SEQ // (2 * m)

                def pairs(m, side):
                    return tp[m].rearrange("p (b two) -> p b two", two=2)[:, :, side]

                def block_product(m):
                    return dve.tensor_tensor(tp[2 * m], pairs(m, 0), pairs(m, 1), ALU.mult)

                def level(l):
                    m = LEVELS[l]
                    dve.wait_ge(level_done, 9 * n + 2 + l + 1)
                    blocks = SEQ // (2 * m)
                    spread = [pairs(m, side).unsqueeze(2).broadcast_to([P, blocks, m]) for side in range(2)]
                    step(dve.tensor_tensor(rights(Qn[:, :], m), rights(Qn[:, :], m), spread[0], ALU.mult))
                    step(dve.tensor_tensor(lefts(keys[:, :], m), lefts(keys[:, :], m), spread[1], ALU.mult))
                    dve.wait_ge(chain, CHAIN * n + steps - 2)
                    if l < len(LEVELS) - 1:
                        step(block_product(2 * m))
                    out = att[:, :, :].rearrange("p c (b two m) -> p c b two m", two=2, m=m)[:, :, :, 1, :]
                    pick = masks[:, l, :].rearrange("p (b m) -> p b m", m=m).unsqueeze(1).broadcast_to([P, CHUNKS, 64 // m, m])
                    data = ps[LEVEL[l % 2]][:, :].rearrange("p (c b m) -> p c b m", c=CHUNKS, m=m)
                    if m == 1:
                        out, pick, data = out.squeeze(3), pick.squeeze(3), data.squeeze(3)
                    elif m == 64:
                        out, pick, data = out.squeeze(2), pick.squeeze(2), data.squeeze(2)
                    K.past_waits(dve)
                    step(dve.copy_predicated(out, pick, data))

                dve.wait_ge(dve_used, 2 * n + 2)
                dve.wait_ge(k_turned, 2 * n + 2)
                step(dve.tensor_scalar(keys[:, :], Fn[:, :], -1.0, 1.0, ALU.mult, ALU.add))
                step(block_product(1))
                for x in range(2):
                    dve.wait_ge(level_done, 9 * n + x + 1)
                    step(dve.tensor_tensor(att[:, 4 * x:4 * x + 4, :], ps[LEVEL[x]][:, :].rearrange("p (c t) -> p c t", c=4),
                                           ident[:, :].unsqueeze(1).broadcast_to([P, 4, P]), ALU.mult))
                step(dve.tensor_tensor(Qn[:, :], Qn[:, :], Fn[:, :], ALU.mult))
                assert steps == AFTER_DIAGONAL
                level(0)
                level(1)
                split(1)
                level(2)
                level(3)
                decay(0)
                level(4)
                split(2)
                decay(1)
                level(5)
                level(6)
                split(3)
                dve.wait_ge(update_done, 2 * n + 1)
                step(dve.tensor_copy(state[:, 1, :], ps[LEVEL[0]][:, 0:P]), wait=True)
                for c in range(1, CHUNKS - 1):
                    if c == 4:
                        dve.wait_ge(update_done, 2 * n + 2)
                    step(dve.scalar_tensor_tensor(state[:, c + 1, :], state[:, c, :], tp[CHUNK][:, c:c + 1],
                                                  ps[LEVEL[c // 4]][:, (c % 4) * P:(c % 4 + 1) * P], ALU.mult, ALU.add), wait=True)
                assert steps == AFTER_STATES
                for x in range(2):
                    dve.wait_ge(rms_done, 2 * n + x + 2)
                    step(dve.reciprocal(rms[:, x, :], rms[:, x, :]), wait=True)
                dve.wait_ge(stored, 16 * n + 16)
                head = slice(n, n + 1) if isinstance(n, int) else bass.ds(n, 1)
                for x in range(2):
                    step(dve.scalar_tensor_tensor(o[:, x * HALF:(x + 1) * HALF], ps[OUT[x]][:, :], norm_g[:, head], rms[:, x, :],
                                                  ALU.mult, ALU.mult))
                assert steps == CHAIN

            passes(dve, body)

        @block.tensor
        def _(pe):
            pe.sem_inc(v_turned, 2)
            pe.sem_inc(k_turned, 2)
            pe.sem_inc(o_done, 1)
            for n in range(GATE_UNITS):
                W.wait(pe, GATE_BASE, n)
                s = n % SLOTS
                for h in range(2):
                    pe.wait_ge(main_read, 2 * n + h + 1)
                    product(pe, ps[MAIN[h]][:, :], [
                        (W.hi[:, s, k * P:(k + 1) * P], W.lo[:, s, k * P:(k + 1) * P],
                         hT_hi[:, k, h * HALF:(h + 1) * HALF], hT_lo[:, k, h * HALF:(h + 1) * HALF])
                        for k in range(KT)]).then_inc(main_done, 1)
                pe.wait_ge(main_done, 2 * n + 2)
                pe.sem_inc(W.used, 1)
            pe.wait_ge(setup.sem, 2)

            def body(it, a, looped, projecting):
                n, par, nxt, (first, w_it) = which(it, a, looped)

                def project(piece):
                    k, third = piece // 3, piece % 3
                    j, h = k // 2, k % 2
                    s = j % SLOTS
                    if third == 0:
                        if h == 0:
                            W.wait(pe, HGRN_BASE, first + j, w_it, 8 if looped else 0)
                        pe.wait_ge(main_read, 8 + 8 * nxt + k + 1)
                    out = ps[MAIN[h]][:, :]
                    for x in range(8 * third, 8 * third + 8):
                        kt, part = x // 3, x % 3
                        cols = slice(kt * P, (kt + 1) * P)
                        toks = slice(h * HALF, (h + 1) * HALF)
                        st = (W.lo if part == 2 else W.hi)[:, s, cols]
                        mv = (hT_lo if part == 1 else hT_hi)[:, kt, toks]
                        ins = pe.matmul(out, st, mv, start=(x == 0), stop=(x == 23))
                    if third == 2:
                        ins.then_inc(main_done, 1)
                        if h == 1:
                            pe.wait_ge(main_done, 8 + 8 * nxt + k + 1)
                            pe.sem_inc(W.used, 1)

                def chunk(c):
                    return slice(c * CHUNK, (c + 1) * CHUNK)

                def turn(src, x, done):
                    for q in range(4):
                        ins = pe.transpose(ps[TURN][:, q * P:(q + 1) * P], src[:, chunk(4 * x + q)], ident[:, :])
                    ins.then_inc(done, 1)

                def steps(pos):
                    if pos == 0:
                        pe.wait_ge(main_read, 8 + 8 * n + 6 + 2)
                        pe.wait_ge(k_ready, 2 * n + 1)
                        turn(vT, 0, v_turned)
                        pe.wait_ge(chain, CHAIN * n + AFTER_KEYS)
                        pe.wait_ge(pool_used, 4 * n + 2 + 2)
                        for x in range(2):
                            for c in range(4):
                                ins = pe.matmul(ps[LEVEL[x]][:, c * P:(c + 1) * P], keys[:, chunk(4 * x + c)],
                                                Q[par][:, chunk(4 * x + c)], start=True, stop=True)
                            ins.then_inc(level_done, 1)
                    if pos == 1:
                        pe.wait_ge(v_ready, 2 * n + 1)
                        turn(vT, 1, v_turned)
                    if pos >= 3 and pos % 2 == 1 and pos <= 15:
                        l = (pos - 3) // 2
                        m = LEVELS[l]
                        pe.wait_ge(chain, CHAIN * n + (after_level(l - 1) if l else AFTER_DIAGONAL))
                        for c in range(CHUNKS):
                            mv = rights(Q[par][:, chunk(c)], m)
                            ins = pe.matmul(ps[LEVEL[l % 2]][:, c * 64:(c + 1) * 64].rearrange("p (b m) -> p b m", m=m),
                                            keys[:, chunk(c)], mv, start=True, stop=True)
                        ins.then_inc(level_done, 1)
                    if pos == 17:
                        pe.wait_ge(v_ready, 2 * n + 2)
                        pe.wait_ge(chain, CHAIN * n + after_level(6))
                        turn(keys, 0, k_turned)
                    if pos == 18:
                        pe.wait_ge(k_ready, 2 * n + 2)
                        turn(keys, 1, k_turned)
                    if pos == 19:
                        pe.wait_ge(k_ready, 2 * n + 3)
                        pe.wait_ge(chain, CHAIN * n + after_level(6) + 1)
                        for x in range(2):
                            for c in range(4 * x, min(4 * x + 4, CHUNKS - 1)):
                                ins = pe.matmul(ps[LEVEL[x]][:, (c % 4) * P:(c % 4 + 1) * P], keysT[:, c, :], V[:, c, :],
                                                start=True, stop=True)
                            ins.then_inc(update_done, 1)
                    if pos == 21:
                        pe.wait_ge(chain, CHAIN * n + AFTER_STATES)
                        for c in range(CHUNKS):
                            out = ps[OUT[c // 4]][:, (c % 4) * P:(c % 4 + 1) * P]
                            ins = pe.matmul(out, V[:, c, :], att[:, c, :], start=True, stop=(c == 0))
                            if c:
                                ins = pe.matmul(out, state[:, c, :], Q[par][:, chunk(c)], start=False, stop=True)
                            if c % 4 == 3:
                                ins.then_inc(o_done, 1)
                    if pos in (22, 23):
                        x = pos - 22
                        pe.wait_ge(squared, 2 * n + x + 1)
                        pe.wait_ge(rms_done, 2 * n + x + 1)
                        pe.matmul(ps[MEAN][:, :], mean_w[:, :], sq[:, x, :], start=True, stop=True).then_inc(mean_done, 1)

                for pos in range(24):
                    if n is not None:
                        steps(pos)
                    if projecting:
                        project(pos)

            passes(pe, body)


def constants():
    q, k = np.arange(P)[:, None], np.arange(P)[None, :]
    half = ROPE_DIM // 2
    freq = np.exp(np.float32(-math.log(ROPE_THETA)) * np.arange(half, dtype=np.float32) * np.float32(2.0 / ROPE_DIM))
    rope = np.zeros((P, 2), np.float32)
    for h in range(2):
        for part, sign in ((0, -1.0), (1, 1.0)):
            rows = slice(h * DH + part * half, h * DH + (part + 1) * half)
            rope[rows, 0], rope[rows, 1] = freq, sign
    level = []
    for m in LEVELS:
        t = np.concatenate([np.arange(b + m, b + 2 * m) for b in range(0, CHUNK, 2 * m)])[None, :]
        level.append((q // (2 * m) == t // (2 * m)) & (q % (2 * m) < m))
    return {
        "ident": np.eye(P, dtype=np.float32),
        "rope_cols": rope,
        "mask2": np.where(np.concatenate([k >= q, k <= q], axis=1), 0.0, NEG).astype(np.float32),
        "mask3": np.where((k <= q) & ((q - k) % 2 == 0), 0.0, NEG).astype(np.float32),
        "level_masks": np.stack(level, axis=1).astype(np.int32),
    }


MERGE_SLOT = [0, 1, 2, 3, 1]
MERGE_STEPS = KT // 2


def merge_block(nc, K):
    W, ps, hT_hi, hT_lo = K.W, K.ps, K.hT_hi, K.hT_lo
    base = MERGE_BASE
    with ExitStack() as ctx:
        def sb(n, shape, dt=F32):
            return ctx.enter_context(nc.sbuf_tensor(f"mg_{n}", shape, dt))

        def sem(n):
            return ctx.enter_context(nc.semaphore(f"mg_{n}"))

        acc = K.acc
        aT_hi, aT_lo = sb("aT_hi", [P, PAIRS, SEQ], F32R), sb("aT_lo", [P, PAIRS, SEQ], F32R)
        m_hi, m_lo = sb("m_hi", [P, 2, SEQ], F32R), sb("m_lo", [P, 2, SEQ], F32R)
        gate, m = sb("gate", [P, 2, SEQ]), sb("m", [P, 2, SEQ])
        in_ready = [sem(f"in_ready{x}") for x in range(2)]
        acc_ready, in_high, in_split = sem("acc_ready"), sem("in_high"), sem("in_split")
        gate_ready = [sem(f"gate_ready{x}") for x in range(2)]
        gate_sig = sem("gate_sig")
        y_done, y_read = sem("y_done"), sem("y_read")
        m_sum, m_high, m_ready = sem("m_sum"), sem("m_high"), sem("m_ready")
        out_done, out_free = sem("out_done"), sem("out_free")
        R = Residual(nc, ctx, K, "mg", 0, rows=1)
        block = ctx.enter_context(nc.Block())

        def branch(x):
            if x < 4:
                return hT_hi[:, 2 * x:2 * x + 2, :], hT_lo[:, 2 * x:2 * x + 2, :]
            return aT_hi[:, 2 * x - 8:2 * x - 6, :], aT_lo[:, 2 * x - 8:2 * x - 6, :]

        def two_tiles(dram, x):
            return dram[2 * x:2 * x + 2, :, :].rearrange("k p n -> p k n")

        @block.sync
        def _(sp):
            sp.sem_inc(y_read, 4)
            sp.sem_inc(m_sum, 4)
            for x in range(6):
                src = two_tiles(K.hgrn_scratch, x) if x < 4 else two_tiles(K.att_scratch, x - 4)
                if x >= 2:
                    sp.wait_ge(in_split, x - 1)
                sp.dma_start((m, gate)[x % 2][:, :, :], src).then_inc(in_ready[x % 2], 16)
            sp.dma_start(acc[:, :, :], K.res_scratch).then_inc(acc_ready, 16)
            R.loads(sp)
            with sp.Fori(0, MERGE_STEPS // 2) as it:
                for a in range(2):
                    i = 2 * it + a

                    def load_gate(q):
                        sp.wait_ge(*((m_sum, 4 * i + 2 * q + 2) if q < 2 else (y_read, 8 * i + 2 * q + 2)))
                        tile = (KT if q < 2 else 0) + 2 * i + q % 2
                        sp.dma_start(gate[:, q % 2, :], K.gates_scratch[tile, :, :]).then_inc(gate_ready[q % 2], 16)

                    if a == 0:
                        sp.wait_ge(in_split, 6)
                    load_gate(0)
                    load_gate(1)
                    W.load(sp, base + 2, 5 * a, it, 10)
                    W.load(sp, base + 2, 5 * a + 1, it, 10)
                    load_gate(2)
                    W.load(sp, base + 2, 5 * a + 2, it, 10)
                    load_gate(3)
                    W.load(sp, base + 2, 5 * a + 3, it, 10)
                    W.load(sp, base + 2, 5 * a + 4, it, 10)

        @block.scalar
        def _(act):
            for x in range(6):
                act.wait_ge(in_ready[x % 2], 16 * (x // 2 + 1))
                act.activation(branch(x)[0], (m, gate)[x % 2][:, :, :], ACT.Copy).then_inc(in_high, 1)
            with act.Fori(0, MERGE_STEPS // 2) as it:
                for a in range(2):
                    i = 2 * it + a

                    def sigmoid(q):
                        act.wait_ge(gate_ready[q % 2], 32 * i + 16 * (q // 2) + 16)
                        act.activation(gate[:, q % 2, :], gate[:, q % 2, :], ACT.Sigmoid).then_inc(gate_sig, 1)

                    W.split_hi(act, 1, base, 5 * a + 1, it, 10, reuse=2)
                    W.split_hi(act, 2, base, 5 * a + 2, it, 10)
                    sigmoid(0)
                    sigmoid(1)
                    W.split_hi(act, 3, base, 5 * a + 3, it, 10)
                    sigmoid(2)
                    W.split_hi(act, 1, base, 5 * a + 4, it, 10)
                    sigmoid(3)
                    for n in range(4):
                        d, h = n // 2, n % 2
                        act.wait_ge(m_sum, 4 * i + n + 5)
                        part = slice(h * HALF, (h + 1) * HALF)
                        act.activation(m_hi[:, d, part], m[:, d, part], ACT.Copy).then_inc(m_high, 1)
                    W.split_hi(act, 0, base, 5 * a + 5, it, 10)

        @block.gpsimd
        def _(pool):
            pool.wait_ge(acc_ready, 16)
            R.make(pool)

        @block.vector
        def _(dve):
            for x in range(6):
                dve.wait_ge(in_high, x + 1)
                hi, lo = branch(x)
                dve.tensor_tensor(lo, (m, gate)[x % 2][:, :, :], hi.bitcast(F32), ALU.subtract).then_inc(in_split, 1)
            dve.sem_inc(out_free, 4)
            with dve.Fori(0, MERGE_STEPS // 2) as it:
                for a in range(2):
                    i = 2 * it + a

                    def weigh(q):
                        for h in range(2):
                            part = slice(h * HALF, (h + 1) * HALF)
                            if h and q != 2:
                                W.done(dve, base, 5 * a + min(q, 2), it, 10)
                            else:
                                dve.wait_ge(y_done, 5 * i + (1, 2, 3, 5)[q] + h)
                            dve.wait_ge(gate_sig, 4 * i + q + 1)
                            g = gate[:, q % 2, part]
                            dve.tensor_tensor(m[:, q, part] if q < 2 else g, g, ps[2 * (q % 2) + h][:, :], ALU.mult).then_inc(y_read, 1)

                    def merge(d):
                        for h in range(2):
                            n, part = 2 * d + h, slice(h * HALF, (h + 1) * HALF)
                            dve.wait_ge(y_read, 8 * i + n + 9)
                            dve.tensor_tensor(m[:, d, part], m[:, d, part], gate[:, d, part], ALU.add).then_inc(m_sum, 1)
                        for h in range(2):
                            n, part = 2 * d + h, slice(h * HALF, (h + 1) * HALF)
                            dve.wait_ge(m_high, 4 * i + n + 1)
                            dve.tensor_tensor(m_lo[:, d, part], m[:, d, part], m_hi[:, d, part].bitcast(F32), ALU.subtract)\
                               .then_inc(m_ready, 1)

                    W.split_lo(dve, 1, base, 5 * a + 1, it, 10)
                    W.split_lo(dve, 2, base, 5 * a + 2, it, 10)
                    weigh(0)
                    W.split_lo(dve, 3, base, 5 * a + 3, it, 10)
                    weigh(1)
                    W.split_lo(dve, 1, base, 5 * a + 4, it, 10)
                    weigh(2)
                    merge(0)
                    weigh(3)
                    merge(1)
                    W.split_lo(dve, 0, base, 5 * a + 5, it, 10)
                    add_out(dve, K, out_done, out_free, R.ready, i, (base, 5 * a + 4, it, 10), 1.0)

        @block.tensor
        def _(pe):
            pe.wait_ge(in_split, 4)
            with pe.Fori(0, MERGE_STEPS // 2) as it:
                for a in range(2):
                    i = 2 * it + a

                    def branch_product(q, stationary, hi, lo, tiles):
                        for h in range(2):
                            part = slice(h * HALF, (h + 1) * HALF)
                            pe.wait_ge(y_read, 8 * i + 2 * q + h + 1)
                            product(pe, ps[2 * (q % 2) + h][:, :], [
                                (*stationary(k), hi[:, k, part], lo[:, k, part]) for k in range(tiles)])\
                                .then_inc(W.used if h and q != 2 else y_done, 1)

                    def columns(slot, first=0):
                        return lambda k: (W.hi[:, slot, first + k * P:first + (k + 1) * P], W.lo[:, slot, first + k * P:first + (k + 1) * P])

                    for q in range(2):
                        W.wait(pe, base, 5 * a + q, it, 10)
                        branch_product(q, columns(MERGE_SLOT[q]), hT_hi, hT_lo, KT)
                    W.wait(pe, base, 5 * a + 2, it, 10)
                    if a == 0:
                        pe.wait_ge(in_split, 6)
                    for q in (2, 3):
                        branch_product(q, columns(MERGE_SLOT[2], (q - 2) * PAIRS * P), aT_hi, aT_lo, PAIRS)
                    W.wait(pe, base, 5 * a + 3, it, 10)
                    W.wait(pe, base, 5 * a + 4, it, 10)
                    out_product(pe, K, MERGE_SLOT[3:], m_hi, m_lo, m_ready, out_free, out_done, i)

    with ExitStack() as ctx:
        L = LayerNorm(nc, ctx, K, "ln2", 1)
        block = ctx.enter_context(nc.Block())
        block.sync(L.loads)
        block.scalar(L.scalar)
        block.gpsimd(L.gpsimd)

        @block.vector
        def _(dve):
            for half in range(2):
                for t in range(4 * half, 4 * half + 4):
                    L.statistics(dve, t)
                L.moments(dve, half)
                if half:
                    L.scales(dve, 0)
            L.scales(dve, 1)
            L.columns(dve)

        @block.tensor
        def _(pe):
            L.tensor(pe, L.xn_ready, 1)


def ple_block(nc, K, out):
    W, ps, hT_hi, hT_lo, acc = K.W, K.ps, K.hT_hi, K.hT_lo, K.acc
    base, tiles = PLE_BASE, PLE_DIM // P
    with ExitStack() as ctx:
        def sb(n, shape, dt=F32):
            return ctx.enter_context(nc.sbuf_tensor(f"ple_{n}", shape, dt))

        def sem(n):
            return ctx.enter_context(nc.semaphore(f"ple_{n}"))

        pT, pT_hi, pT_lo = sb("pT", [P, tiles, SEQ]), sb("pT_hi", [P, tiles, SEQ], F32R), sb("pT_lo", [P, tiles, SEQ], F32R)
        emb, gate = sb("emb", [P, TT, HALF]), sb("gate", [P, TT, HALF])
        p_in, p_high, p_split = sem("p_in"), sem("p_high"), sem("p_split")
        done, read = sem("done"), sem("read")
        scaled, summed, stored = sem("scaled"), sem("summed"), sem("stored")
        R = Residual(nc, ctx, K, "ple", 2)
        block = ctx.enter_context(nc.Block())

        @block.sync
        def _(sp):
            sp.dma_start(pT[:, :, :], K.pT_dram.rearrange("k p n -> p k n")).then_inc(p_in, 16)
            R.loads(sp)
            for j in range(2, 6):
                W.load(sp, base, j)

            def store(n):
                t, c = n % TT, n // TT
                sp.wait_ge(summed, n + 1)
                sp.dma_start(out[t, :, c * HALF:(c + 1) * HALF], acc[:, t, c * HALF:(c + 1) * HALF]).then_inc(stored, 16)

            for j in range(6, PLE_UNITS):
                W.load(sp, base, j)
            for n in range(2 * TT):
                store(n)
            sp.wait_ge(stored, 16 * 2 * TT)

        def bank_done(eng, c, x, t):
            if t == TT - 1:
                W.done(eng, base, 5 * c + x)
            else:
                eng.wait_ge(done, (TT - 1) * (2 * c + (x == 4)) + t + 1)

        @block.scalar
        def _(act):
            act.wait_ge(p_in, 16)
            act.activation(pT_hi[:, :, :], pT[:, :, :], ACT.Copy).then_inc(p_high, 1)
            for c in range(2):
                for x in range(5):
                    j = 5 * c + x + 2
                    if j < PLE_UNITS:
                        W.split_hi(act, j % SLOTS, base, j, reuse=4)
                    if x == 0:
                        for t in range(TT):
                            bank_done(act, c, 0, t)
                            if c:
                                act.wait_ge(scaled, t + 1)
                            act.activation(emb[:, t, :], ps[t][:, :], ACT.Copy).then_inc(read, 1)
                for t in range(TT):
                    bank_done(act, c, 4, t)
                    if c:
                        act.wait_ge(summed, t + 1)
                    act.activation(gate[:, t, :], ps[t][:, :], ACT.Sigmoid).then_inc(read, 1)

        block.gpsimd(R.make)

        @block.vector
        def _(dve):
            dve.wait_ge(p_high, 1)
            dve.tensor_tensor(pT_lo[:, :, :], pT[:, :, :], pT_hi[:, :, :].bitcast(F32), ALU.subtract).then_inc(p_split, 1)
            for c in range(2):
                for x in range(5):
                    j = 5 * c + x + 2
                    if j < PLE_UNITS:
                        W.split_lo(dve, j % SLOTS, base, j)
                for t in range(TT):
                    n = TT * c + t
                    dve.wait_ge(read, 16 * c + TT + t + 1)
                    dve.tensor_tensor(gate[:, t, :], gate[:, t, :], emb[:, t, :], ALU.mult).then_inc(scaled, 1)
                    dve.wait_ge(scaled, n + 1)
                    dve.wait_ge(R.ready, t + 1)
                    part = acc[:, t, c * HALF:(c + 1) * HALF]
                    dve.tensor_tensor(part, part, gate[:, t, :], ALU.add).then_inc(summed, 1)

        @block.tensor
        def _(pe):
            pe.wait_ge(p_split, 1)
            for c in range(2):
                for x in range(5):
                    j = 5 * c + x
                    s = j % SLOTS
                    W.wait(pe, base, j)
                    hi, lo = (pT_hi, pT_lo) if x == 0 else (hT_hi, hT_lo)
                    for t in range(TT):
                        if x < 2 and j:
                            pe.wait_ge(read, TT * (2 * c + x - 1) + t + 1)
                        last = product(pe, ps[t][:, :], [
                            (hi[:, k, t * P:(t + 1) * P], lo[:, k, t * P:(t + 1) * P],
                             W.hi[:, s, (k % 2) * HALF:(k % 2 + 1) * HALF], W.lo[:, s, (k % 2) * HALF:(k % 2 + 1) * HALF])
                            for k in ((0, 1) if x == 0 else (2 * x - 2, 2 * x - 1))], start=(x < 2), stop=(x in (0, 4)))
                        if t == TT - 1:
                            last.then_inc(W.used, 1)
                        elif x in (0, 4):
                            last.then_inc(done, 1)


def decoder_layer(nc, drams, out):
    with ExitStack() as ctx:
        K = Core()
        K.W = Weights(nc, ctx, drams["units"])
        K.ps = [ctx.enter_context(nc.psum_tensor(f"bank{b}", [P, HALF], F32)) for b in range(8)]
        K.hT_hi = ctx.enter_context(nc.sbuf_tensor("hT_hi", [P, KT, SEQ], F32R))
        K.hT_lo = ctx.enter_context(nc.sbuf_tensor("hT_lo", [P, KT, SEQ], F32R))
        K.ident = ctx.enter_context(nc.sbuf_tensor("ident", [P, P], F32))
        K.const_ready = ctx.enter_context(nc.semaphore("const_ready"))
        K.passed = {e.engine: ctx.enter_context(nc.semaphore(f"passed_{n}")) for n, e in (("dve", nc.vector), ("pool", nc.gpsimd))}
        K.ident_dram, K.xT_dram, K.x_dram, K.pT_dram = drams["ident"], drams["xT"], drams["x"], drams["pT"]
        K.ln_cols_dram, K.ln_rows_dram = drams["ln_cols"], drams["ln_rows"]
        K.positions_dram, K.rope_cols_dram = drams["positions"], drams["rope_cols"]
        K.mask2_dram, K.mask3_dram = drams["mask2"], drams["mask3"]
        K.level_masks_dram, K.lb_logits_dram, K.norm_g_dram = drams["level_masks"], drams["lb_logits"], drams["norm_g"]

        def scratch(name, shape):
            return nc.dram_tensor(name, shape, F32, kind="Internal").ap()

        K.ffn_side = {"ffn1": NoSide, "ffn2": NoSide}
        K.res_scratch = scratch("res_scratch", (P, TT, DM))
        K.gates_scratch = scratch("gates_scratch", (2 * KT, P, SEQ))
        K.att_scratch = scratch("att_scratch", (PAIRS, P, SEQ))
        K.hgrn_scratch = scratch("hgrn_scratch", (HEADS, P, SEQ))

        with nc.sbuf_tensor("acc1", [P, TT, DM], F32) as K.acc:
            ffn_block(nc, K, "ffn1", FFN1_BASE, presplit=0, first=True, ln=0, res_out=K.res_scratch)
        attention_block(nc, K)
        hgrn_block(nc, K)
        with nc.sbuf_tensor("acc2", [P, TT, DM], F32) as K.acc:
            merge_block(nc, K)
            ffn_block(nc, K, "ffn2", FFN2_BASE, presplit=1, first=False, ln=2)
            ple_block(nc, K, out)
        print("SEMS", len(nc.free_semaphores), len(nc.released_uncleared_semaphores))


def kernel(**inputs):
    import numpy as _np
    import concourse.bacc as _bacc
    from concourse import mybir as _mybir
    from concourse.bass_utils import run_bass_kernel_spmd as _run

    given = {n: _np.asarray(a) for n, a in inputs.items()}

    def columns(w, first, n=P):
        return w[:, first:first + n].reshape(-1, P, n).transpose(1, 0, 2).reshape(P, -1)

    def slab(w, row, first, tiles):
        width = DM // tiles
        return w[row:row + tiles * P, first:first + width].reshape(tiles, P, width).transpose(1, 0, 2).reshape(P, -1)

    units = _np.empty((UNITS, P, DM), _np.float32)
    at = 0

    def put(unit):
        nonlocal at
        units[at] = unit
        at += 1

    def put_ffn(w_in, w_out):
        for step in range(FFN_STEPS):
            for f in (2 * step, 2 * step + 1):
                put(columns(w_in, f * P))
                put(columns(w_in, D_FF + f * P))
            for f in (2 * step, 2 * step + 1):
                put(slab(w_out, f * P, 0, 1))

    w_mix = given["w_mix_in"][0]
    att, hgrn = 3 * DM // 2, DM
    gates = 3 * att + 4 * hgrn
    put_ffn(given["ffn1_w_in"][0], given["ffn1_w_out"][0])
    for pair in range(PAIRS):
        for group in range(GROUPS):
            for part in range(3):
                put(columns(w_mix, part * att + (group * PAIRS + pair) * P))
        for n in range(3):
            put(columns(w_mix, gates + (3 * pair + n) * P))
    for n in range(3 * PAIRS, 2 * KT):
        put(columns(w_mix, gates + n * P))
    for head in range(HEADS):
        for part in range(4):
            put(columns(w_mix, 3 * att + part * hgrn + head * P))
    w_pa, w_pb, w_o = given["w_proj_attn"][0], given["w_proj_hgrn"][0], given["w_mix_out"][0]
    for j in range(0, KT, 2):
        put(columns(w_pb, j * P))
        put(columns(w_pb, (j + 1) * P))
        put(_np.concatenate([columns(w_pa, j * P), columns(w_pa, (j + 1) * P)], axis=1))
        put(slab(w_o, j * P, 0, 1))
        put(slab(w_o, (j + 1) * P, 0, 1))
    put_ffn(given["ffn2_w_in"][0], given["ffn2_w_out"][0])
    for c in range(2):
        put(slab(given["ple_w_proj"][0], 0, c * HALF, 2))
        for k in range(0, KT, 2):
            put(slab(given["ple_w_gate"][0], k * P, c * HALF, 2))
    assert at == UNITS

    def tiles_of_rows(a):
        return a.reshape(-1, P, a.shape[-1])

    x = given["x"][0]
    arrays = {
        "units": units,
        "xT": tiles_of_rows(x.T),
        "x": tiles_of_rows(x).transpose(1, 0, 2),
        "pT": tiles_of_rows(given["p"][0, 0].T),
        "positions": given["positions"],
        "ln_cols": _np.stack([_np.stack([given[f"ln{i}_{s}"][0].reshape(KT, P).T for s in "gb"], axis=1) for i in (1, 2, 3)]),
        "ln_rows": _np.stack([_np.stack([given[f"ln{i}_{s}"] for s in "gb"], axis=1) for i in (1, 2, 3)]),
        "lb_logits": given["hgrn_lb_logits"].reshape(2, HEADS, P).transpose(2, 0, 1),
        "norm_g": given["hgrn_norm_g"][0].reshape(HEADS, P).T,
        **constants(),
    }
    arrays = {n: _np.ascontiguousarray(a) for n, a in arrays.items()}
    nc = _bacc.Bacc("TRN2", target_bir_lowering=False, num_devices=1)
    drams = {n: nc.dram_tensor(f"in_{n}", a.shape, _mybir.dt.from_np(a.dtype), kind="ExternalInput").ap()
             for n, a in arrays.items()}
    out = nc.dram_tensor("out_0", (TT, P, DM), F32, kind="ExternalOutput").ap()
    decoder_layer(nc, drams, out)
    result = _run(nc, [{f"in_{n}": a for n, a in arrays.items()}], core_ids=[0])
    return result.results[0]["out_0"].reshape(1, SEQ, DM)
```

```python
import math

import numpy as np

import concourse.bass as bass
from concourse import mybir
from contextlib import ExitStack

F32 = mybir.dt.float32
F32R = mybir.dt.float32r
I32 = mybir.dt.int32
U8 = mybir.dt.uint8
ACT = mybir.ActivationFunctionType
ALU = mybir.AluOpType

P = 128
SEQ = 1024
DM = 1024
HALF = 512
KT = DM // P
TT = SEQ // P
D_FF = 2816
FT = D_FF // P
FFN_STEPS = FT // 2
ALPHA = 2.0 ** 0.25
LN_EPS = 1e-5
RMS_EPS = 1e-6

GROUPS = 3
PAIRS = 4
DH = 64
ROPE_DIM = 16
ROPE_THETA = 500000.0
ATT_SCALE = DH ** -0.5
HEADS = 8
CHUNK = 128
CHUNKS = SEQ // CHUNK
LEVELS = [1, 2, 4, 8, 16, 32, 64]
PLE_DIM = 256

FFN_UNITS = 6 * FFN_STEPS
ATT_UNITS = 12 * PAIRS
GATE_UNITS = 4
HGRN_UNITS = 4 * HEADS
MERGE_UNITS = 5 * 4
PLE_UNITS = 10
FFN1_BASE = 0
ATT_BASE = FFN1_BASE + FFN_UNITS
GATE_BASE = ATT_BASE + ATT_UNITS
HGRN_BASE = GATE_BASE + GATE_UNITS
MERGE_BASE = HGRN_BASE + HGRN_UNITS
FFN2_BASE = MERGE_BASE + MERGE_UNITS
PLE_BASE = FFN2_BASE + FFN_UNITS
UNITS = PLE_BASE + PLE_UNITS

RAW_SLOTS = 2
SLOTS = 4
FFN_SLOT = [0, 1, 2, 0, 3, 2]


class Step:

    def __init__(self, sem):
        self.sem, self.count = sem, 0

    def after(self, eng, instruction):
        self.count += 1
        instruction.then_inc(self.sem, 1)
        eng.wait_ge(self.sem, self.count)


class Weights:

    def __init__(self, nc, ctx, dram):
        self.dram = dram
        self.raw = ctx.enter_context(nc.sbuf_tensor("w_raw", [P, RAW_SLOTS, DM], F32))
        self.hi = ctx.enter_context(nc.sbuf_tensor("w_hi", [P, SLOTS, DM], F32R))
        self.lo = ctx.enter_context(nc.sbuf_tensor("w_lo", [P, SLOTS, DM], F32R))
        self.raw_ready = [ctx.enter_context(nc.semaphore(f"w_raw_ready{s}")) for s in range(RAW_SLOTS)]
        self.hi_ready = ctx.enter_context(nc.semaphore("w_hi_ready"))
        self.ready = ctx.enter_context(nc.semaphore("w_ready"))
        self.used = ctx.enter_context(nc.semaphore("w_used"))

    def load(self, sp, base, j, i=0, per=0):
        u = base + j + per * i
        sp.wait_ge(self.ready, u + 1)
        sp.dma_start(self.raw[:, j % 2, :], self.dram[u, :, :]).then_inc(self.raw_ready[j % 2], 16)

    def split_hi(self, act, slot, base, j, i=0, per=0, reuse=3):
        u = base + j + per * i
        act.wait_ge(self.raw_ready[j % 2], 16 * (base // 2 + j // 2 + 1) + 8 * per * i)
        act.wait_ge(self.used, u - reuse + 1 + SLOTS)
        act.activation(self.hi[:, slot, :], self.raw[:, j % 2, :], ACT.Copy).then_inc(self.hi_ready, 1)

    def split_lo(self, dve, slot, base, j, i=0, per=0):
        u = base + j + per * i
        dve.wait_ge(self.hi_ready, u + 1)
        dve.tensor_tensor(self.lo[:, slot, :], self.raw[:, j % 2, :], self.hi[:, slot, :].bitcast(F32),
                          ALU.subtract).then_inc(self.ready, 1)

    def done(self, eng, base, j, i=0, per=0):
        eng.wait_ge(self.used, base + j + per * i + 1 + SLOTS)

    def wait(self, pe, base, j, i=0, per=0):
        pe.wait_ge(self.ready, base + j + per * i + 1 + RAW_SLOTS)


class Core:

    def past_waits(self, eng):
        eng.sem_inc(self.passed[eng.engine], 1)


def product(pe, out, pairs, start=True, stop=True):
    n = len(pairs)
    for x, (s_hi, s_lo, m_hi, m_lo) in enumerate(pairs):
        pe.matmul(out, s_hi, m_hi, start=start and x == 0, stop=False)
        pe.matmul(out, s_hi, m_lo, start=False, stop=False)
        last = pe.matmul(out, s_lo, m_hi, start=False, stop=stop and x == n - 1)
    return last


def out_product(pe, K, slots, hi, lo, ready, free, done, step):
    W = K.W
    for t in range(0, TT, 2):
        for f in range(2):
            if t in (0, TT // 2):
                pe.wait_ge(ready, 4 * step + 2 * f + (1 if t == 0 else 2))
            for tt in (t, t + 1):
                for c in range(2):
                    bank = K.ps[4 + 2 * (tt % 2) + c][:, :]
                    if f == 0:
                        pe.wait_ge(free, 16 * step + 2 * tt + c + 1)
                    st_hi, st_lo = (x[:, f, tt * P:(tt + 1) * P] for x in (hi, lo))
                    m_hi, m_lo = (w[:, slots[f], c * HALF:(c + 1) * HALF] for w in (W.hi, W.lo))
                    last = product(pe, bank, [(st_hi, st_lo, m_hi, m_lo)], start=(f == 0), stop=(f == 1))
                    if f == 1:
                        if (tt, c) == (TT - 1, 1):
                            last.then_inc(W.used, 2)
                        else:
                            last.then_inc(done, 1)


def add_out(dve, K, done, free, res_ready, step, unit, factor, L=None):
    for t in range(TT):
        for c in range(2):
            if (t, c) == (TT - 1, 1):
                K.W.done(dve, *unit)
            else:
                dve.wait_ge(done, 15 * step + 2 * t + c + 1)
            if c == 0:
                dve.wait_ge(res_ready, t + 1)
            a = K.acc[:, t, c * HALF:(c + 1) * HALF]
            dve.scalar_tensor_tensor(a, K.ps[4 + 2 * (t % 2) + c][:, :], factor, a, ALU.mult, ALU.add).then_inc(free, 1)
        if L is not None:
            if t >= 1:
                dve.wait_ge(free, 16 * step + 2 * t + 4)
                L.statistics(dve, t - 1)
            if t == 5:
                L.scales(dve, 0)
            if t == 4:
                L.moments(dve, 0)
    if L is not None:
        dve.wait_ge(free, 16 * step + 2 * TT + 4)
        L.statistics(dve, TT - 1)
        L.moments(dve, 1)
        L.scales(dve, 1)
        L.columns(dve)


class Residual:

    def __init__(self, nc, ctx, K, name, index, rows=2, free=None):
        self.free = free
        self.K, self.index, self.rows = K, index, rows
        self.scale = 1.0 if index == 2 else ALPHA
        self.row = None if index is None else ctx.enter_context(nc.sbuf_tensor(f"{name}_res_row", [P, rows, DM], F32))
        self.ready = ctx.enter_context(nc.semaphore(f"{name}_res_ready"))
        if index is not None:
            self.loaded, self.scaled, self.gained = (
                ctx.enter_context(nc.semaphore(f"{name}_res_{n}")) for n in ("loaded", "scaled", "gained"))

    def load(self, eng, first, rows):
        eng.dma_start(self.row[:, 0:rows, :], self.K.ln_rows_dram[self.index, :, first:first + rows, :].broadcast_to([P, rows, DM]))\
           .then_inc(self.loaded, 16)

    def loads(self, sp):
        if self.index is not None and self.rows == 2:
            self.load(sp, 0, 2)

    def make(self, pool):
        acc = self.K.acc
        if self.index is None:
            for t in range(TT):
                pool.tensor_scalar(acc[:, t, :], acc[:, t, :], self.scale, None, ALU.mult).then_inc(self.ready, 1)
            return
        for r, op in ((0, ALU.mult), (1, ALU.add)):
            if r:
                pool.wait_ge(self.gained, TT)
            if self.rows == 1:
                self.load(pool, r, 1)
            pool.wait_ge(self.loaded, 16 * (r + 1) if self.rows == 1 else 16)
            row = self.row[:, r % self.rows, :]
            if self.scale != 1.0:
                pool.tensor_scalar(row, row, self.scale, None, ALU.mult).then_inc(self.scaled, 1)
                pool.wait_ge(self.scaled, r + 1)
            for t in range(TT):
                if r and self.free is not None:
                    pool.wait_ge(self.free, 2 * t + 2 + 4)
                pool.tensor_tensor(acc[:, t, :], acc[:, t, :], row, op).then_inc((self.gained, self.ready)[r], 1)


class LayerNorm:

    def __init__(self, nc, ctx, K, name, index, y=None):
        def sb(n, shape, dt=F32):
            return ctx.enter_context(nc.sbuf_tensor(f"{name}_{n}", shape, dt))

        def sem(n):
            return ctx.enter_context(nc.semaphore(f"{name}_ln_{n}"))

        self.K, self.index = K, index
        self.stats = sb("stats", [P, TT, 2, 6])
        self.mean_var = sb("mean_var", [P, TT, 2])
        self.std, self.rstd, self.shift = sb("std", [P, TT]), sb("rstd", [P, TT]), sb("shift", [P, TT])
        self.eps = sb("eps", [P, 1])
        self.y = sb("y", [P, 4, HALF]) if y is None else y
        self.cols = sb("cols", [P, 2, KT])
        self.step = Step(sem("step"))
        self.loaded, self.var_ready, self.std_ready, self.scale_ready, self.xn_ready = (
            sem(n) for n in ("loaded", "var_ready", "std_ready", "scale_ready", "xn_ready"))
        self.turned, self.y_ready, self.high = (sem(n) for n in ("turned", "y_ready", "high"))
        self.low = sem("low_even"), sem("low_odd")
        self.stored = sem("stored") if index == 0 else None

    def loads(self, sp):
        sp.dma_start(self.cols[:, :, :], self.K.ln_cols_dram[self.index, :, :, :]).then_inc(self.loaded, 16)

    def store(self, sp, dram):
        for half in range(2):
            sp.wait_ge(self.xn_ready, 4 * half + 4)
            tiles = slice(4 * half, 4 * half + 4)
            sp.dma_start(dram[:, tiles, :], self.K.acc[:, tiles, :]).then_inc(self.stored, 16)
        sp.wait_ge(self.stored, 32)

    def statistics(self, dve, t):
        if t == 0:
            dve.memset(self.eps[:, :], LN_EPS)
        for c in range(2):
            ins = dve.bn_stats(self.stats[:, t, c, :], self.K.acc[:, t, c * HALF:(c + 1) * HALF])
        self.step.count += 1
        ins.then_inc(self.step.sem, 1)

    def moments(self, dve, half):
        dve.wait_ge(self.step.sem, self.step.count)
        for t in range(4 * half, 4 * half + 4):
            ins = dve.bn_aggr(self.mean_var[:, t, :], self.stats[:, t, :, :].rearrange("p a b -> p (a b)"))
        ins.then_inc(self.var_ready, 1)

    def scales(self, dve, half):
        tiles = slice(4 * half, 4 * half + 4)
        dve.wait_ge(self.std_ready, half + 1)
        self.step.after(dve, dve.reciprocal(self.rstd[:, tiles], self.std[:, tiles]))
        dve.scalar_tensor_tensor(self.shift[:, tiles], self.mean_var[:, tiles, 0], -1.0, self.rstd[:, tiles],
                                 ALU.mult, ALU.mult).then_inc(self.scale_ready, 1)

    def part(self, n):
        return (slice(None), n % KT, slice(n // KT * HALF, (n // KT + 1) * HALF))

    def low_part(self, eng, n):
        eng.wait_ge(self.high, n + 1)
        eng.tensor_tensor(self.K.hT_lo[self.part(n)], self.y[:, n % 4, :], self.K.hT_hi[self.part(n)].bitcast(F32),
                          ALU.subtract).then_inc(self.low[n % 2], 1)

    def columns(self, dve):
        dve.wait_ge(self.loaded, 16)
        for n in range(2 * KT):
            if n >= 4:
                dve.wait_ge(self.low[n % 2], n // 2 - 1)
            dve.wait_ge(self.turned, n + 1)
            k = n % KT
            dve.tensor_scalar(self.y[:, n % 4, :], self.K.ps[k][:, :], self.cols[:, 0, k:k + 1], self.cols[:, 1, k:k + 1],
                              ALU.mult, ALU.add).then_inc(self.y_ready, 1)
            if n % 2 == 0 and n:
                dve.wait_ge(self.y_ready, n)
                self.low_part(dve, n - 1)
        dve.wait_ge(self.y_ready, 2 * KT)
        self.low_part(dve, 2 * KT - 1)

    def gpsimd(self, pool):
        for n in range(0, 2 * KT, 2):
            pool.wait_ge(self.y_ready, n + 1)
            self.low_part(pool, n)

    def scalar(self, act):
        K = self.K

        def rows(half):
            tiles = slice(4 * half, 4 * half + 4)
            act.wait_ge(self.var_ready, half + 1)
            act.activation(self.std[:, tiles], self.mean_var[:, tiles, 1], ACT.Sqrt, bias=self.eps[:, :]).then_inc(self.std_ready, 1)
            act.wait_ge(self.scale_ready, half + 1)
            for t in range(4 * half, 4 * half + 4):
                act.activation(K.acc[:, t, :], K.acc[:, t, :], ACT.Identity, bias=self.shift[:, t:t + 1],
                               scale=self.rstd[:, t:t + 1]).then_inc(self.xn_ready, 1)

        def highs():
            for n in range(2 * KT):
                act.wait_ge(self.y_ready, n + 1)
                act.activation(K.hT_hi[self.part(n)], self.y[:, n % 4, :], ACT.Copy).then_inc(self.high, 1)

        rows(0)
        rows(1)
        highs()

    def tensor(self, pe, free, end):
        K = self.K
        pe.wait_ge(K.const_ready, 16)
        for n in range(2 * KT):
            half, k = n // KT, n % KT
            if k == 0:
                pe.wait_ge(self.xn_ready, 4 * half + 4)
            if n == 4:
                pe.wait_ge(free, end)
            if half:
                pe.wait_ge(self.y_ready, k + 1)
            for t in range(4 * half, 4 * half + 4):
                last = pe.transpose(K.ps[k][:, (t % 4) * P:(t % 4 + 1) * P], K.acc[:, t, k * P:(k + 1) * P], K.ident[:, :])
            last.then_inc(self.turned, 1)


def ffn_block(nc, K, name, base, presplit, first, ln, side, res_out=None):
    W, ps, hT_hi, hT_lo, ident = K.W, K.ps, K.hT_hi, K.hT_lo, K.ident
    with ExitStack() as ctx:
        def sb(n, shape, dt=F32):
            return ctx.enter_context(nc.sbuf_tensor(f"{name}_{n}", shape, dt))

        def sem(n):
            return ctx.enter_context(nc.semaphore(f"{name}_{n}"))

        acc = K.acc
        silu = sb("silu", [P, 2, HALF])
        g = sb("g", [P, 2, HALF])
        g_hi = sb("g_hi", [P, 2, SEQ], F32R)
        g_lo = sb("g_lo", [P, 2, SEQ], F32R)
        a_done, u_done, out_done = sem("a_done"), sem("u_done"), sem("out_done")
        a_silu, g_mul, g_high, g_ready, out_free = sem("a_silu"), sem("g_mul"), sem("g_high"), sem("g_ready"), sem("out_free")
        if first:
            in_ready = [sem(f"in_ready{s}") for s in range(4)]
            acc_ready, x_high, x_ready = sem("acc_ready"), sem("x_high"), sem("x_ready")
        R = Residual(nc, ctx, K, name, None if first else ln - 1)
        L = LayerNorm(nc, ctx, K, name, ln)
        side = side(nc, ctx, K)
        block = ctx.enter_context(nc.Block())

        def staged(x):
            return slice(None), slice(x % 2 * 4, x % 2 * 4 + 4), slice(x // 2 * HALF, (x // 2 + 1) * HALF)

        def steps(eng, body):
            with eng.Fori(0, FFN_STEPS - 1) as i:
                body(i, False)
            body(FFN_STEPS - 1, True)

        @block.sync
        def _(sp):
            if first:
                def load_x(x):
                    _, tiles, tokens = staged(x)
                    sp.dma_start(acc[staged(x)], K.xT_dram[tiles, :, tokens].rearrange("k p n -> p k n")).then_inc(in_ready[x], 16)

                W.load(sp, base, 0)
                load_x(0)
                load_x(1)
                W.load(sp, base, 1)
                load_x(2)
                load_x(3)
                sp.dma_start(ident[:, :], K.ident_dram).then_inc(K.const_ready, 16)
            R.loads(sp)
            L.loads(sp)
            side.loads(sp)
            with sp.Fori(0, FFN_STEPS) as i:
                for j in range(6):
                    W.load(sp, base + 2, j, i, 6)
            if res_out is not None:
                L.store(sp, res_out)

        @block.scalar
        def _(act):
            if first:
                W.split_hi(act, 0, base, 0)
                for x in range(4):
                    act.wait_ge(in_ready[x], 16)
                    act.activation(hT_hi[staged(x)], acc[staged(x)], ACT.Copy).then_inc(x_high, 1)
                    if x == 1:
                        W.split_hi(act, 1, base, 1)
                act.wait_ge(x_ready, 4)
                act.dma_start(acc[:, :, :], K.x_dram).then_inc(acc_ready, 16)
            elif presplit == 1:
                W.split_hi(act, 1, base, 1)

            def body(i, last):
                def silus(f):
                    for h in range(2):
                        n = 2 * f + h
                        if h == 0:
                            act.wait_ge(a_done, 2 * i + f + 1)
                        else:
                            W.done(act, base, 2 * f, i, 6)
                        act.wait_ge(g_mul, 4 * i + n + 1)
                        act.activation(silu[:, h, :], ps[h][:, :], ACT.Silu).then_inc(a_silu, 1)

                def highs(f):
                    for h in range(2):
                        n = 2 * f + h
                        act.wait_ge(g_mul, 4 * i + n + 3)
                        act.activation(g_hi[:, f, h * HALF:(h + 1) * HALF], g[:, h, :], ACT.Copy).then_inc(g_high, 1)

                W.split_hi(act, FFN_SLOT[2], base, 2, i, 6)
                silus(0)
                W.split_hi(act, FFN_SLOT[3], base, 3, i, 6)
                highs(0)
                W.split_hi(act, FFN_SLOT[4], base, 4, i, 6)
                silus(1)
                W.split_hi(act, FFN_SLOT[5], base, 5, i, 6)
                highs(1)
                if last:
                    side.scalar(act)
                W.split_hi(act, 0, base, 6, i, 6)
                W.split_hi(act, 1, base, 7, i, 6, reuse=4)

            steps(act, body)
            L.scalar(act)

        @block.gpsimd
        def _(pool):
            if first:
                pool.wait_ge(acc_ready, 16)
            R.make(pool)
            L.gpsimd(pool)

        @block.vector
        def _(dve):
            if first:
                dve.sem_inc(W.ready, RAW_SLOTS)
                W.split_lo(dve, 0, base, 0)
                for x in range(4):
                    dve.wait_ge(x_high, x + 1)
                    dve.tensor_tensor(hT_lo[staged(x)], acc[staged(x)], hT_hi[staged(x)].bitcast(F32),
                                      ALU.subtract).then_inc(x_ready, 1)
                    if x == 1:
                        W.split_lo(dve, 1, base, 1)
            elif presplit == 1:
                W.split_lo(dve, 1, base, 1)
            dve.sem_inc(g_mul, 2)
            dve.sem_inc(out_free, 4)

            def body(i, last):
                def gates(f):
                    for h in range(2):
                        n = 2 * f + h
                        if h == 0:
                            dve.wait_ge(u_done, 2 * i + f + 1)
                        else:
                            W.done(dve, base, 2 * f + 1, i, 6)
                        dve.wait_ge(a_silu, 4 * i + n + 3)
                        dve.tensor_tensor(g[:, h, :], silu[:, h, :], ps[2 + h][:, :], ALU.mult).then_inc(g_mul, 1)
                        dve.wait_ge(g_high, 4 * i + n + 1)
                        dve.tensor_tensor(g_lo[:, f, h * HALF:(h + 1) * HALF], g[:, h, :],
                                          g_hi[:, f, h * HALF:(h + 1) * HALF].bitcast(F32),
                                          ALU.subtract).then_inc(g_ready, 1)

                W.split_lo(dve, FFN_SLOT[2], base, 2, i, 6)
                if last:
                    side.vector(dve, 0)
                W.split_lo(dve, FFN_SLOT[3], base, 3, i, 6)
                if last:
                    side.vector(dve, 1)
                gates(0)
                W.split_lo(dve, FFN_SLOT[4], base, 4, i, 6)
                if last:
                    side.vector(dve, 2)
                W.split_lo(dve, FFN_SLOT[5], base, 5, i, 6)
                gates(1)
                if last:
                    side.vector(dve, 3)
                W.split_lo(dve, 0, base, 6, i, 6)
                W.split_lo(dve, 1, base, 7, i, 6)
                add_out(dve, K, out_done, out_free, R.ready, i, (base, 5, i, 6), 0.5, L if last else None)

            steps(dve, body)

        @block.tensor
        def _(pe):
            if first:
                pe.sem_inc(W.used, SLOTS)
            pe.sem_inc(a_silu, 2)

            def body(i, last):
                for f in range(2):
                    for kind in range(2):
                        j = 2 * f + kind
                        W.wait(pe, base, j, i, 6)
                        s = FFN_SLOT[j]
                        for h in range(2):
                            n = 2 * f + h
                            if first and j == 0:
                                pe.wait_ge(x_ready, 2 * h + 2)
                            pe.wait_ge((a_silu, g_mul)[kind], 4 * i + n + 1)
                            ins = product(pe, ps[2 * kind + h][:, :], [
                                (W.hi[:, s, k * P:(k + 1) * P], W.lo[:, s, k * P:(k + 1) * P],
                                 hT_hi[:, k, h * HALF:(h + 1) * HALF], hT_lo[:, k, h * HALF:(h + 1) * HALF])
                                for k in range(KT)])
                            ins.then_inc(W.used if h else (a_done, u_done)[kind], 1)
                W.wait(pe, base, 4, i, 6)
                W.wait(pe, base, 5, i, 6)
                out_product(pe, K, FFN_SLOT[4:], g_hi, g_lo, g_ready, out_free, out_done, i)

            steps(pe, body)
            L.tensor(pe, out_free, 16 * FFN_STEPS + 4)


JOBS = 8
MAIN_BANKS, SCORE_BANKS, TURN_BANK, OUT_BANKS = (0, 1, 2), (3, 4), 5, (6, 7)
POSITIONS = 24
JOB_POS = [5, 6, 7, 8, 8, 9, 10, 10]
MERGE_POS = (1, 2, 4, 7)
NEG = -3.0e38
TWO_PI_PARTS = (6.28125, 0.001934051513671875, 1.2554228305816650390625e-06)
SWAP_ROPE_HALVES = list(range(8, 16)) + list(range(8)) + list(range(16, 32))


def query_tokens(g, dj):
    if g == 0:
        return slice(dj * P, (dj + 1) * P)
    if g == 1:
        first = dj // 2 + 4 * P * (dj % 2)
        return slice(first, first + 4 * (P - 1) + 1, 4)
    return slice(dj, dj + 8 * (P - 1) + 1, 8)


def key_tiles(g, dj):
    return 1 if g == 2 or (g == 0 and dj == 0) or (g == 1 and dj % 2 == 0) else 2


def key_tokens(g, dj):
    if key_tiles(g, dj) == 1:
        return query_tokens(g, dj)
    if g == 0:
        return slice((dj - 1) * P, (dj + 1) * P)
    return slice(dj // 2, dj // 2 + 4 * (2 * P - 1) + 1, 4)


def token_order(ap, g, x):
    if g == 0:
        return ap[:, x * HALF:(x + 1) * HALF].rearrange("p (r j) -> p r j", r=2)
    r = 4 if g == 1 else 8
    v = ap.rearrange("p (j r) -> p r j", r=r)
    return v[:, x * r // 2:(x + 1) * r // 2, :]


def tile_order(ap, g):
    return ap.rearrange("p (r j) -> p r j", r=4 if g == 2 else 2)


def score_uses():
    order = []
    for pos in range(POSITIONS + 1):
        for g in range(GROUPS):
            if pos == 6 * g + 12:
                order.append(("spread", g))
        for g in range(GROUPS):
            order += [("job", g, dj) for dj in range(JOBS) if JOB_POS[dj] + 6 * g == pos]
    return {key: n for n, key in enumerate(order)}


def at_position(pos, lag):
    return [(g, dj) for g in range(GROUPS) for dj in range(JOBS) if JOB_POS[dj] + 6 * g + lag == pos]


def turn_use(g, dj):
    return 10 * g + (dj + 2 if dj else 0)


def attention_block(nc, K):
    W, ps, hT_hi, hT_lo, ident = K.W, K.ps, K.hT_hi, K.hT_lo, K.ident
    USE = score_uses()
    N_USE = len(USE)
    base = ATT_BASE
    with ExitStack() as ctx:
        def sb(n, shape, dt=F32):
            return ctx.enter_context(nc.sbuf_tensor(f"att_{n}", shape, dt))

        def sem(n):
            return ctx.enter_context(nc.semaphore(f"att_{n}"))

        qT = [sb(f"qT{s}", [P, SEQ]) for s in range(2)]
        kT = [sb(f"kT{s}", [P, SEQ]) for s in range(2)]
        V = [sb(f"V{s}", [P, JOBS, P]) for s in range(2)]
        vT = sb("vT", [P, SEQ])
        cos, sin = K.cos, K.sin
        mask2, mask3 = sb("mask2", [P, 2 * P]), sb("mask3", [P, P])
        z, swapped = sb("z", [P, 2, HALF]), sb("swapped", [P, 2, HALF])
        prob, probT = sb("prob", [P, 2, 2, 2 * P]), sb("probT", [P, 2, 4, P])
        gate = sb("gate", [P, 2, HALF])
        O = [sb(f"O{g}", [P, SEQ]) for g in range(GROUPS)]
        lse = [sb(f"lse{g}", [P, SEQ]) for g in range(GROUPS)]
        total = sb("total", [P, SEQ])
        spread = sb("spread", [P, JOBS, 2, DH])
        row_max, row_sum = sb("row_max", [P, GROUPS, JOBS, 2]), sb("row_sum", [P, GROUPS, JOBS, 2])
        neg_max, inv_sum = sb("neg_max", [P, 2, 2]), sb("inv_sum", [P, 2, 2])
        log_sum, row_lse = sb("log_sum", [P, JOBS * 2]), sb("row_lse", [P, JOBS * 2])

        masks_ready = sem("masks_ready")
        main_done, main_free = sem("main_done"), sem("main_free")
        z_swapped, rope_part, rope_done = sem("z_swapped"), sem("rope_part"), sem("rope_done")
        vt_turned = sem("vt_turned")
        turn_free = sem("turn_free")
        score_done, score_free = sem("score_done"), sem("score_free")
        negmax_done, exp_done, inv_done, prob_done = sem("negmax_done"), sem("exp_done"), sem("inv_done"), sem("prob_done")
        prob_turned = sem("prob_turned")
        pv_done, out_free = sem("pv_done"), sem("out_free")
        log_done, lse_done, spread_done, spread_turned = sem("log_done"), sem("lse_done"), sem("spread_done"), sem("spread_turned")
        merge, weights_ready, weighted = sem("merge"), sem("weights_ready"), sem("weighted")
        merged, att_stored = sem("merged"), sem("att_stored")
        gate_stored = [sem(f"gate_stored{h}") for h in range(2)]
        MERGE_OPS = 11
        block = ctx.enter_context(nc.Block())

        def pairs(eng, body):
            body(0, False)
            with eng.Fori(1, PAIRS) as i:
                body(i, True)

        @block.sync
        def _(sp):
            sp.dma_start(mask2[:, :], K.mask2_dram).then_inc(masks_ready, 16)
            sp.dma_start(mask3[:, :], K.mask3_dram).then_inc(masks_ready, 16)
            for h in range(2):
                sp.sem_inc(gate_stored[h], 16)
            sp.sem_inc(att_stored, 16)
            W.load(sp, base + 2, 0)

            def store_gate(i, n):
                for h in range(2):
                    sp.wait_ge(main_free, POSITIONS * i + 18 + 2 * n + h + 1 + 3)
                    sp.dma_start(K.gates_scratch[3 * i + n, :, h * HALF:(h + 1) * HALF], gate[:, h, :])\
                      .then_inc(gate_stored[h], 16)

            def body(i, merging):
                for j in range(1, 13):
                    W.load(sp, base + 2, j, i, 12)
                    if j == 6 and merging:
                        store_merged(i)
                for n in range(3):
                    store_gate(i, n)

            def store_merged(i):
                sp.wait_ge(merged, i)
                sp.dma_start(K.att_scratch[i - 1, :, :], O[0][:, :]).then_inc(att_stored, 16)

            pairs(sp, body)
            W.load(sp, GATE_BASE, 3)
            for n in range(GATE_UNITS):
                W.load(sp, HGRN_BASE, n)
                store_gate(PAIRS - 1, 3 + n)
            store_merged(PAIRS)
            for h in range(2):
                sp.wait_ge(gate_stored[h], 16 * (3 * PAIRS + GATE_UNITS + 1))
            sp.wait_ge(att_stored, 16 * (PAIRS + 1))

        @block.scalar
        def _(act):
            W.split_hi(act, 2, base, 2)
            act.sem_inc(main_free, 3)

            def weights(i):
                for g in range(GROUPS):
                    act.wait_ge(merge, MERGE_OPS * i + 3 + g - MERGE_OPS)
                    act.activation(lse[g][:, :], lse[g][:, :], ACT.Exp).then_inc(weights_ready, 1)

            def body(i, merging):
                def evacuate(hx):
                    unit, h = hx // 2, hx % 2
                    if h:
                        W.done(act, base, unit, i, 12)
                    else:
                        act.wait_ge(main_done, 12 * i + unit + 1)
                    if unit >= 9:
                        act.wait_ge(gate_stored[h], 16 * (unit - 9) + 16 + 48 * i)
                        out = gate[:, h, :]
                    elif unit % 3 == 2:
                        act.wait_ge(vt_turned, 2 * (unit // 3) + 6 * i + 2)
                        out = vT[:, h * HALF:(h + 1) * HALF]
                    else:
                        rn = 4 * (unit // 3) + 2 * (unit % 3) + h
                        act.wait_ge(rope_done, 12 * i + rn + 1)
                        out = z[:, h, :]
                    act.activation(out, ps[MAIN_BANKS[hx % 3]][:, :], ACT.Copy).then_inc(main_free, 1)

                for pos in range(POSITIONS + 1):
                    if pos >= 1:
                        evacuate(pos - 1)
                    if pos == 3 and merging:
                        weights(i)
                    if pos % 2 == 0 and 2 <= pos < POSITIONS:
                        j = pos // 2 + 2
                        W.split_hi(act, j % SLOTS, base, j, i, 12)
                    for g in range(GROUPS):
                        if pos == 6 * g + 11:
                            act.wait_ge(lse_done, 3 * i + g + 1)
                            act.wait_ge(exp_done, 24 * i + 8 * g + 8)
                            act.activation(log_sum[:, :], row_sum[:, g, :, :].rearrange("p a b -> p (a b)"), ACT.Ln)\
                               .then_inc(log_done, 1)
                    for slot in range(2):
                        for g, dj in at_position(pos, 1)[slot:slot + 1]:
                            jn = 24 * i + 8 * g + dj
                            nk = key_tiles(g, dj)
                            act.wait_ge(prob_turned, jn + 3)
                            act.wait_ge(pv_done, jn + 23)
                            src = ps[TURN_BANK][:, :].rearrange("p (h k q) -> p h k q", h=2, k=2)[:, :, 2 - nk:2, :]
                            dst = probT[:, dj % 2, :, :].rearrange("p (h k) q -> p h k q", h=2)[:, :, 2 - nk:2, :]
                            act.activation(dst, src, ACT.Copy).then_inc(turn_free, 1)
                        for g, dj in at_position(pos, 0)[slot:slot + 1]:
                            jn = 24 * i + 8 * g + dj
                            first = 2 * P - P * key_tiles(g, dj)
                            act.wait_ge(negmax_done, jn + 1)
                            for h in range(2):
                                s = prob[:, dj % 2, h, first:2 * P]
                                ins = act.activation(s, s, ACT.Exp, bias=neg_max[:, dj % 2, h:h + 1], scale=ATT_SCALE,
                                                     accum_out=row_sum[:, g, dj, h:h + 1])
                            ins.then_inc(exp_done, 1)
                W.split_hi(act, 2, base, 14, i, 12)

            pairs(act, body)
            for n in range(GATE_UNITS):
                if n < 3:
                    W.split_hi(act, (n + 3) % SLOTS, GATE_BASE, n + 3)
                for h in range(2):
                    if h:
                        W.done(act, GATE_BASE, n)
                    else:
                        act.wait_ge(main_done, 12 * PAIRS + n + 1)
                    act.wait_ge(gate_stored[h], 16 * (3 * PAIRS + n + 1))
                    act.activation(gate[:, h, :], ps[MAIN_BANKS[(2 * n + h) % 3]][:, :], ACT.Copy).then_inc(main_free, 1)
                if n == 0:
                    weights(PAIRS)

        @block.gpsimd
        def _(pool):
            pool.sem_inc(rope_done, 2)

            def weigh(i):
                for g in range(GROUPS):
                    pool.wait_ge(weights_ready, 3 * i + g + 1 - 3)
                    pool.wait_ge(out_free, 6 * i + 2)
                    pool.tensor_tensor(O[g][:, :], O[g][:, :], lse[g][:, :], ALU.mult).then_inc(weighted, 1)

            def body(i, merging):
                def rope(g, part, h):
                    rn = 4 * g + 2 * part + h
                    hx = 6 * g + 2 * part + h
                    cols = slice(h * HALF, (h + 1) * HALF)
                    dst = (qT, kT)[part][g % 2][:, cols]
                    if h == 0:
                        pool.wait_ge(score_done, 24 * i + (24, 16, 32)[g])
                    pool.wait_ge(main_free, POSITIONS * i + hx + 4)
                    pool.tensor_tensor(dst, z[:, h, :], cos[:, cols], ALU.mult).then_inc(rope_part, 1)
                    pool.wait_ge(z_swapped, 12 * i + rn + 1)
                    pool.tensor_tensor(swapped[:, h, :], swapped[:, h, :], sin[:, cols], ALU.mult).then_inc(rope_part, 1)
                    pool.wait_ge(rope_part, 24 * i + 2 * rn + 2)
                    pool.tensor_tensor(dst, dst, swapped[:, h, :], ALU.add).then_inc(rope_done, 1)

                def spread_lse(g):
                    pool.wait_ge(lse_done, 3 * i + g + 2)
                    pool.wait_ge(spread_turned, 6 * i + 2 * g + 2)
                    K.past_waits(pool)
                    pool.tensor_copy(spread[:, :, :, :], row_lse[:, :].rearrange("p (a b) -> p a b", b=2)
                                     .unsqueeze(3).broadcast_to([P, JOBS, 2, DH])).then_inc(spread_done, 1)

                for g in range(GROUPS):
                    for part in range(2):
                        for h in range(2):
                            rope(g, part, h)
                    if g >= 1:
                        spread_lse(g - 1)
                    elif merging:
                        weigh(i)
                spread_lse(2)

            pairs(pool, body)
            weigh(PAIRS)

        @block.vector
        def _(dve):
            W.split_lo(dve, 2, base, 2)
            dve.wait_ge(masks_ready, 32)
            dve.sem_inc(turn_free, 1)
            dve.sem_inc(score_free, 2)
            dve.sem_inc(out_free, 2)
            dve.sem_inc(lse_done, 1)

            def merge_pair(i, part):
                steps = (0, 2, 5, 8)[part]

                def step(ins):
                    nonlocal steps
                    steps += 1
                    ins.then_inc(merge, 1)
                    dve.wait_ge(merge, MERGE_OPS * i + steps - MERGE_OPS)

                if part == 0:
                    spread_out(i, 2, -3)
                    dve.wait_ge(score_free, 2 * N_USE * i + 2)
                    step(dve.tensor_tensor(total[:, :], lse[0][:, :], lse[1][:, :], ALU.max))
                    step(dve.tensor_tensor(total[:, :], total[:, :], lse[2][:, :], ALU.max))
                if part == 1:
                    for g in range(GROUPS):
                        step(dve.tensor_tensor(lse[g][:, :], lse[g][:, :], total[:, :], ALU.subtract))
                if part == 2:
                    dve.wait_ge(weights_ready, 3 * i)
                    step(dve.tensor_tensor(total[:, :], lse[0][:, :], lse[1][:, :], ALU.add))
                    step(dve.tensor_tensor(total[:, :], total[:, :], lse[2][:, :], ALU.add))
                    step(dve.reciprocal(total[:, :], total[:, :]))
                if part == 3:
                    dve.wait_ge(weighted, 3 * i)
                    step(dve.tensor_tensor(O[1][:, :], O[1][:, :], O[2][:, :], ALU.add))
                    step(dve.tensor_tensor(O[0][:, :], O[0][:, :], O[1][:, :], ALU.add))
                    step(dve.tensor_tensor(O[0][:, :], O[0][:, :], total[:, :], ALU.mult))
                    dve.sem_inc(merged, 1)
                    assert steps == MERGE_OPS

            def spread_out(i, g, last=0):
                for x2 in range(2):
                    dve.wait_ge(spread_turned, 6 * i + 2 * g + x2 + 3 + 2 * last)
                    dve.tensor_copy(token_order(lse[g][:, :], g, x2), tile_order(ps[SCORE_BANKS[x2]][:, :], g))\
                       .then_inc(score_free, 1)

            def body(i, merging):
                for pos in range(POSITIONS + 1):
                    if pos % 2 == 0 and 2 <= pos < POSITIONS:
                        j = pos // 2 + 2
                        W.split_lo(dve, j % SLOTS, base, j, i, 12)
                    hx = pos - 1
                    if pos >= 1 and hx // 2 < 9 and (hx // 2) % 3 < 2:
                        rn = 4 * (hx // 6) + 2 * ((hx // 2) % 3) + hx % 2
                        dve.wait_ge(main_free, POSITIONS * i + hx + 4)
                        dve.wait_ge(rope_done, 12 * i + rn + 1)
                        K.past_waits(dve)
                        dve.stream_shuffle(swapped[:, hx % 2, :], z[:, hx % 2, :], SWAP_ROPE_HALVES).then_inc(z_swapped, 1)
                    if merging and pos in MERGE_POS:
                        merge_pair(i, MERGE_POS.index(pos))
                    for g in range(GROUPS):
                        if pos == 6 * g + 11:
                            dve.wait_ge(log_done, 3 * i + g + 1)
                            dve.wait_ge(spread_done, 3 * i + g + 1)
                            dve.scalar_tensor_tensor(row_lse[:, :], row_max[:, g, :, :].rearrange("p a b -> p (a b)"),
                                                     ATT_SCALE, log_sum[:, :], ALU.mult, ALU.add).then_inc(lse_done, 1)
                        if pos == 6 * g + 12 and g < 2:
                            spread_out(i, g)
                    for slot in range(2):
                        for g, dj in at_position(pos, 0)[slot:slot + 1]:
                            jn = 24 * i + 8 * g + dj
                            nk = key_tiles(g, dj)
                            first = 2 * P - P * nk
                            mask = mask3[:, :] if g == 2 else mask2[:, 2 * P - nk * P:2 * P]
                            dve.wait_ge(score_done, jn + 25)
                            dve.wait_ge(prob_turned, jn + 1)
                            K.past_waits(dve)
                            for h in range(2):
                                dve.tensor_tensor_reduce(
                                    prob[:, dj % 2, h, first:2 * P], ps[SCORE_BANKS[h]][:, 0:nk * P], mask,
                                    1.0, NEG, ALU.add, ALU.max, row_max[:, g, dj, h:h + 1]).then_inc(score_free, 1)
                            dve.wait_ge(score_free, 2 * N_USE * i + 2 * USE["job", g, dj] + 4)
                            dve.tensor_scalar(neg_max[:, dj % 2, :], row_max[:, g, dj, :], -ATT_SCALE, None, ALU.mult)\
                               .then_inc(negmax_done, 1)
                            dve.wait_ge(exp_done, jn + 1)
                            dve.reciprocal(inv_sum[:, dj % 2, :], row_sum[:, g, dj, :]).then_inc(inv_done, 1)
                            dve.wait_ge(inv_done, jn + 1)
                            for h in range(2):
                                s = prob[:, dj % 2, h, first:2 * P]
                                ins = dve.tensor_scalar(s, s, inv_sum[:, dj % 2, h:h + 1], None, ALU.mult)
                            ins.then_inc(prob_done, 1)
                        if slot == 0 and pos in (6, 12, 18):
                            g = pos // 6 - 1
                            dve.wait_ge(pv_done, 24 * i + (24, 16, 32)[g])
                            for x2 in range(2):
                                dve.wait_ge(vt_turned, 6 * i + 2 * g + x2 + 3)
                                dve.tensor_copy(V[g % 2][:, 4 * x2:4 * x2 + 4, :],
                                                ps[TURN_BANK][:, :].rearrange("p (k c) -> p k c", k=4)).then_inc(turn_free, 1)
                        for g, dj in at_position(pos, 2)[slot:slot + 1]:
                            if dj % 4 == 3:
                                jn = 24 * i + 8 * g + dj
                                dve.wait_ge(pv_done, jn + 25)
                                if g == 0 and dj == 3:
                                    dve.wait_ge(att_stored, 16 * i + 16)
                                dve.tensor_copy(token_order(O[g][:, :], g, dj // 4),
                                                tile_order(ps[OUT_BANKS[dj // 4]][:, :], g)).then_inc(out_free, 1)
                W.split_lo(dve, 2, base, 14, i, 12)

            pairs(dve, body)
            for part in range(4):
                merge_pair(PAIRS, part)
                if part:
                    W.split_lo(dve, (part + 2) % SLOTS, GATE_BASE, part + 2)

        @block.tensor
        def _(pe):
            pe.sem_inc(vt_turned, 2)
            pe.sem_inc(score_done, 24)
            pe.sem_inc(prob_turned, 2)
            pe.sem_inc(pv_done, 24)
            pe.sem_inc(spread_turned, 2)
            pe.sem_inc(spread_done, 1)

            def turn_spread(i, g, last=False):
                pe.wait_ge(spread_done, 3 * i + g + 2 - 3 * last)
                for x2 in range(2):
                    pe.wait_ge(score_free, 2 * N_USE * i + 2 * USE["spread", g] + x2 + 1 - 2 * N_USE * last)
                    for q in range(4):
                        ins = pe.transpose(ps[SCORE_BANKS[x2]][:, q * P:(q + 1) * P],
                                           spread[:, 4 * x2 + q, :, :].rearrange("p a b -> p (a b)"), ident[:, :])
                    ins.then_inc(spread_turned, 1)

            def project(hx, unit, unit_wait, between=()):
                h = hx % 2
                if h == 0:
                    W.wait(pe, *unit_wait)
                s = unit % SLOTS
                terms = [(W.hi[:, s, k * P:(k + 1) * P], W.lo[:, s, k * P:(k + 1) * P],
                          hT_hi[:, k, h * HALF:(h + 1) * HALF], hT_lo[:, k, h * HALF:(h + 1) * HALF])
                         for k in range(KT)]
                bank = ps[MAIN_BANKS[hx % 3]][:, :]
                for q in range(4):
                    last = product(pe, bank, terms[2 * q:2 * q + 2], start=(q == 0), stop=(q == 3))
                    if q < 3 and between:
                        between[q]()
                last.then_inc(W.used if h else main_done, 1)

            def body(i, merging):
                for pos in range(POSITIONS + 1):
                    for g in range(2):
                        if pos == 6 * g + 12:
                            turn_spread(i, g)
                    if pos == 1 and merging:
                        turn_spread(i, 2, last=True)

                    def scores(g, dj):
                        nk = key_tiles(g, dj)
                        if dj == 0:
                            pe.wait_ge(rope_done, 12 * i + 4 * (g + 1) + 2)
                        for h in range(2):
                            pe.wait_ge(score_free, 2 * N_USE * i + 2 * USE["job", g, dj] + h + 1)
                            rows = slice(h * DH, (h + 1) * DH)
                            ins = pe.matmul(ps[SCORE_BANKS[h]][:, 0:nk * P],
                                            qT[g % 2][rows, query_tokens(g, dj)], kT[g % 2][rows, key_tokens(g, dj)],
                                            start=True, stop=True)
                        ins.then_inc(score_done, 1)

                    def turn_v(g, x2):
                        pe.wait_ge(turn_free, 30 * i + 10 * g + x2 + 2)
                        for q in range(4):
                            ins = pe.transpose(ps[TURN_BANK][:, q * P:(q + 1) * P], vT[:, query_tokens(g, 4 * x2 + q)], ident[:, :])
                        ins.then_inc(vt_turned, 1)

                    def steps(slot):
                        for g, dj in at_position(pos, 0)[slot:slot + 1]:
                            scores(g, dj)
                        for g, dj in at_position(pos, 1)[slot:slot + 1]:
                            nk = key_tiles(g, dj)
                            pe.wait_ge(prob_done, 24 * i + 8 * g + dj + 1)
                            pe.wait_ge(turn_free, 30 * i + turn_use(g, dj) + 1)
                            for h in range(2):
                                for kt in range(2 - nk, 2):
                                    ins = pe.transpose(ps[TURN_BANK][:, (2 * h + kt) * P:(2 * h + kt + 1) * P],
                                                       prob[:, dj % 2, h, kt * P:(kt + 1) * P], ident[:, :])
                            ins.then_inc(prob_turned, 1)
                        for g, dj in at_position(pos, 2)[slot:slot + 1]:
                            nk = key_tiles(g, dj)
                            pe.wait_ge(turn_free, 30 * i + turn_use(g, dj) + 2)
                            if dj == 0:
                                pe.wait_ge(turn_free, 30 * i + 10 * g + 4)
                            if dj % 4 == 0:
                                pe.wait_ge(out_free, 6 * i + 2 * g + dj // 4 + 1)
                            for h in range(2):
                                cols = slice(h * DH, (h + 1) * DH)
                                for kt in range(2 - nk, 2):
                                    ins = pe.matmul(ps[OUT_BANKS[dj // 4]][cols, (dj % 4) * P:(dj % 4 + 1) * P],
                                                    V[g % 2][:, dj - 1 + kt, cols], probT[:, dj % 2, 2 * h + kt, :],
                                                    start=(kt == 2 - nk), stop=(kt == 1))
                            ins.then_inc(pv_done, 1)

                    def turn_half(x2):
                        if pos in (6, 12, 18):
                            if x2 == 0:
                                pe.wait_ge(main_free, POSITIONS * i + pos + 3)
                            turn_v(pos // 6 - 1, x2)

                    steps(0)
                    if pos < POSITIONS:
                        pe.wait_ge(main_free, POSITIONS * i + pos + 1)
                        project(pos, pos // 2, (base, pos // 2, i, 12),
                                (lambda: turn_half(0), lambda: steps(1), lambda: turn_half(1)))
                    else:
                        steps(1)

            pairs(pe, body)
            for hx in range(2 * GATE_UNITS):
                if hx == 2:
                    turn_spread(PAIRS, 2, last=True)
                pe.wait_ge(main_free, POSITIONS * PAIRS + hx + 1)
                project(hx, hx // 2, (GATE_BASE, hx // 2))


class RopeTables:

    def __init__(self, nc, ctx, K):
        def sb(n, dt=F32):
            return ctx.enter_context(nc.sbuf_tensor(f"rope_{n}", [P, SEQ], dt))

        self.K, self.positions, self.angle, self.turns, self.x = K, sb("positions", I32), sb("angle"), sb("turns"), sb("x")
        self.cols = ctx.enter_context(nc.sbuf_tensor("rope_cols", [P, 2], F32))
        self.loaded, self.ready = ctx.enter_context(nc.semaphore("rope_loaded")), ctx.enter_context(nc.semaphore("rope_ready"))
        self.setup = Step(ctx.enter_context(nc.semaphore("rope_setup")))

    def loads(self, sp):
        sp.dma_start(self.positions[:, :], self.K.positions_dram.broadcast_to([P, SEQ])).then_inc(self.loaded, 16)
        sp.dma_start(self.cols[:, :], self.K.rope_cols_dram).then_inc(self.loaded, 16)

    def vector(self, dve, part):
        angle, turns, x, after = self.angle[:, :], self.turns[:, :], self.x[:, :], self.setup.after
        if part == 0:
            dve.wait_ge(self.loaded, 32)
            after(dve, dve.tensor_copy(angle, self.positions[:, :]))
            after(dve, dve.tensor_scalar(angle, angle, self.cols[:, 0:1], None, ALU.mult))
            after(dve, dve.tensor_scalar(turns, angle, 1.0 / (2 * math.pi), 12582912.0, ALU.mult, ALU.add))
            after(dve, dve.tensor_scalar(turns, turns, 12582912.0, None, ALU.subtract))
        if part == 1:
            for two_pi in TWO_PI_PARTS:
                after(dve, dve.scalar_tensor_tensor(angle, turns, -two_pi, angle, ALU.mult, ALU.add))
        if part == 2:
            after(dve, dve.tensor_scalar(angle, angle, -3.1415925, 3.1415925, ALU.max, ALU.min))
            after(dve, dve.scalar_tensor_tensor(x, angle, -1.0, angle, ALU.mult, ALU.max))
            after(dve, dve.tensor_scalar(x, x, -1.0, math.pi / 2, ALU.mult, ALU.add))
            dve.tensor_scalar(angle, angle, self.cols[:, 1:2], None, ALU.mult).then_inc(self.ready, 1)

    def scalar(self, act):
        act.wait_ge(self.ready, 1)
        act.activation(self.K.sin[:, :], self.angle[:, :], ACT.Sin)
        act.activation(self.K.cos[:, :], self.x[:, :], ACT.Sin)


class PleInput:

    def __init__(self, nc, ctx, K):
        self.K = K
        self.pT = ctx.enter_context(nc.sbuf_tensor("ple_pT", [P, PLE_DIM // P, SEQ], F32))
        self.loaded, self.high = ctx.enter_context(nc.semaphore("ple_p_loaded")), ctx.enter_context(nc.semaphore("ple_p_high"))

    def loads(self, sp):
        sp.dma_start(self.pT[:, :, :], self.K.pT_dram.rearrange("k p n -> p k n")).then_inc(self.loaded, 16)

    def scalar(self, act):
        act.wait_ge(self.loaded, 16)
        act.activation(self.K.pT_hi[:, :, :], self.pT[:, :, :], ACT.Copy).then_inc(self.high, 1)

    def vector(self, dve, part):
        if part == 3:
            dve.wait_ge(self.high, 1)
            dve.tensor_tensor(self.K.pT_lo[:, :, :], self.pT[:, :, :], self.K.pT_hi[:, :, :].bitcast(F32), ALU.subtract)


CHAIN, FIRST_STEP = 43, 6
AFTER_KEYS, AFTER_DIAGONAL, AFTER_STATES = 1, 9, 43


def after_level(l):
    return AFTER_DIAGONAL + 4 * l + 2


def rights(ap, m):
    return ap.rearrange("p (b two m) -> p b two m", two=2, m=m)[:, :, 1, :]


def lefts(ap, m):
    return ap.rearrange("p (b two m) -> p b two m", two=2, m=m)[:, :, 0, :]


def hgrn_block(nc, K):
    W, ps, hT_hi, hT_lo, ident = K.W, K.ps, K.hT_hi, K.hT_lo, K.ident
    MAIN, LEVEL, TURN, OUT, MEAN = (0, 1), (2, 3), 4, (5, 6), 7
    with ExitStack() as ctx:
        def sb(n, shape, dt=F32):
            return ctx.enter_context(nc.sbuf_tensor(f"hg_{n}", shape, dt))

        def sem(n):
            return ctx.enter_context(nc.semaphore(f"hg_{n}"))

        Q = [sb(f"Q{s}", [P, SEQ]) for s in range(2)]
        F = [sb(f"F{s}", [P, SEQ]) for s in range(2)]
        G = [sb(f"G{s}", [P, SEQ]) for s in range(2)]
        keys, prods, vT = sb("keys", [P, SEQ]), sb("prods", [P, SEQ]), sb("vT", [P, SEQ])
        V, keysT = sb("V", [P, CHUNKS, P]), sb("keysT", [P, CHUNKS, P])
        att = sb("att", [P, CHUNKS, P])
        state = sb("state", [P, CHUNKS, P])
        z, sig = sb("z", [P, 2, HALF]), sb("sig", [P, 2, HALF])
        sq, rms, o = sb("sq", [P, 2, HALF]), sb("rms", [P, 2, HALF]), sb("o", [P, SEQ])
        masks = sb("masks", [P, len(LEVELS), CHUNK // 2], I32)
        logits, lb, one_minus_lb = sb("logits", [P, 2, HEADS]), sb("lb", [P, HEADS]), sb("one_minus_lb", [P, HEADS])
        lb_tmp, lb_exp = sb("lb_tmp", [P, HEADS]), sb("lb_exp", [P, 2, HEADS])
        norm_g, mean_w, eps = sb("norm_g", [P, HEADS]), sb("mean_w", [P, P]), sb("eps", [P, 1])

        setup, loaded, lb_ready, lb_expd = Step(sem("setup")), sem("loaded"), sem("lb_ready"), sem("lb_expd")
        main_done, main_read = sem("main_done"), sem("main_read")
        pool_used, dve_used = sem("pool_used"), sem("dve_used")
        v_turned, v_ready, k_turned, k_ready = sem("v_turned"), sem("v_ready"), sem("k_turned"), sem("k_ready")
        level_done, update_done, chain = sem("level_done"), sem("update_done"), sem("chain")
        o_done, squared, mean_done, rms_done = sem("o_done"), sem("squared"), sem("mean_done"), sem("rms_done")
        gated, stored = sem("gated"), sem("stored")
        tail_loaded = [sem("tail_loaded_5"), sem("tail_loaded_2")]
        tail_high, tail_low = sem("tail_high"), sem("tail_low")
        block = ctx.enter_context(nc.Block())

        def returned(n):
            return (Q[0][:, :], F[0][:, :], G[0][:, :], z[:, :, :].rearrange("p a n -> p (a n)"),
                    sig[:, :, :].rearrange("p a n -> p (a n)"), vT[:, :], Q[0][:, :], o[:, :])[n]

        def passes(eng, body):
            body(None, 0, 0, True)
            with eng.Fori(0, (HEADS - 2) // 2) as it:
                for a in range(2):
                    body(it, a, 1, True)
            body(0, HEADS - 2, 0, True)
            body(0, HEADS - 1, 0, False)

        def which(it, a, looped):
            if it is None:
                return None, None, 0, (0, 0)
            n = 2 * it + a if looped else a
            return n, a % 2, n + 1, ((4 * (a + 1), it) if looped else (4 * (a + 1), 0))

        @block.sync
        def _(sp):
            sp.dma_start(masks[:, :, :], K.level_masks_dram).then_inc(loaded, 16)
            sp.dma_start(logits[:, :, :], K.lb_logits_dram).then_inc(loaded, 16)
            sp.dma_start(norm_g[:, :], K.norm_g_dram).then_inc(loaded, 16)
            sp.sem_inc(stored, 16)
            for j in range(4, 8):
                W.load(sp, HGRN_BASE, j)

            def store(n):
                sp.wait_ge(gated, 2 * n + 2)
                sp.dma_start(K.hgrn_scratch[n, :, :], o[:, :]).then_inc(stored, 16)

            with sp.Fori(0, (HEADS - 2) // 2) as it:
                for a in range(2):
                    for j in range(4):
                        W.load(sp, HGRN_BASE, 4 * (a + 2) + j, it, 8)
                    store(2 * it + a)
            for j in range(2):
                W.load(sp, MERGE_BASE, j)
            store(HEADS - 2)
            sp.wait_ge(dve_used, 2 * HEADS)
            for n in range(HEADS - 1):
                if n == 5:
                    sp.wait_ge(v_turned, 2 * HEADS + 2)
                if n == 6:
                    sp.wait_ge(tail_low, 1)
                    sp.wait_ge(stored, 16 * HEADS)
                sp.dma_start(returned(n), K.hgrn_scratch[n, :, :]).then_inc(tail_loaded[n >= 5], 16)

        @block.scalar
        def _(act):
            act.wait_ge(lb_ready, 1)
            act.activation(lb_exp[:, :, :], logits[:, :, :], ACT.Exp).then_inc(lb_expd, 1)
            act.sem_inc(main_read, 2)
            act.sem_inc(k_ready, 1)
            act.sem_inc(rms_done, 1)
            def body(it, a, looped, projecting):
                n, par, nxt, (first, w_it) = which(it, a, looped)

                def evacuate(k):
                    if not projecting:
                        return
                    unit, h = k // 2, k % 2
                    if h:
                        W.done(act, HGRN_BASE, first + unit, w_it, 8 if looped else 0)
                    else:
                        act.wait_ge(main_done, 4 * nxt + unit + 1)
                    bank = ps[MAIN[k % 2]][:, :]
                    if unit == 2:
                        act.wait_ge(v_turned, 2 * nxt + 2)
                        act.activation(vT[:, h * HALF:(h + 1) * HALF], bank, ACT.Copy).then_inc(main_read, 1)
                        return
                    if unit == 0:
                        act.wait_ge(pool_used, 4 * nxt + h + 1)
                    elif unit == 1:
                        act.wait_ge(pool_used, 4 * nxt + h + 3)
                    else:
                        act.wait_ge(dve_used, 2 * nxt + h + 1)
                    if unit != 1:
                        act.activation(z[:, h, :], bank, ACT.Copy)
                    act.activation(sig[:, h, :], bank, ACT.Sigmoid).then_inc(main_read, 1)

                def split(j):
                    if projecting and not (n == HEADS - 2 and j == 3 if not looped else False):
                        act_first = first + j + 2
                        W.split_hi(act, (j + 2) % SLOTS, HGRN_BASE, act_first, w_it, 8 if looped else 0)

                split(0)
                if n is not None:
                    for x in range(2):
                        act.wait_ge(v_turned, 2 * n + x + 3)
                        act.activation(V[:, 4 * x:4 * x + 4, :], ps[TURN][:, :].rearrange("p (c v) -> p c v", c=4), ACT.Copy)\
                           .then_inc(v_ready, 1)
                evacuate(0)
                evacuate(1)
                split(1)
                evacuate(2)
                evacuate(3)
                split(2)
                evacuate(4)
                if not projecting:
                    W.done(act, HGRN_BASE, HGRN_UNITS - 1)
                    for y in range(HEADS - 1):
                        if y in (0, 5):
                            act.wait_ge(tail_loaded[y == 5], 16 * (2 if y else 5))
                        act.activation(hT_hi[:, y, :], returned(y), ACT.Copy).then_inc(tail_high, 1)
                if n is not None:
                    for x in range(2):
                        act.wait_ge(k_turned, 2 * n + x + 3)
                        act.activation(keysT[:, 4 * x:4 * x + 4, :], ps[TURN][:, :].rearrange("p (c v) -> p c v", c=4), ACT.Copy)\
                           .then_inc(k_ready, 1)
                        if x == 0:
                            evacuate(5)
                            split(3)
                    evacuate(6)
                    for x in range(2):
                        act.wait_ge(o_done, 2 * n + x + 2)
                        act.activation(sq[:, x, :], ps[OUT[x]][:, :], ACT.Square).then_inc(squared, 1)
                    for x in range(2):
                        act.wait_ge(mean_done, 2 * n + x + 1)
                        act.activation(rms[:, x, :], ps[MEAN][:, :], ACT.Sqrt, bias=eps[:, :]).then_inc(rms_done, 1)
                else:
                    evacuate(5)
                    split(3)
                    evacuate(6)
                evacuate(7)

            passes(act, body)
            act.wait_ge(gated, 2 * HEADS)
            act.activation(hT_hi[:, HEADS - 1, :], o[:, :], ACT.Copy).then_inc(tail_high, 1)

        @block.gpsimd
        def _(pool):
            pool.memset(mean_w[:, :], 1.0 / P).then_inc(setup.sem, 1)
            pool.memset(eps[:, :], RMS_EPS).then_inc(setup.sem, 1)
            pool.sem_inc(pool_used, 2)

            def body(it, a, looped, projecting):
                n, par, nxt, _ = which(it, a, looped)
                other = 0 if n is None else 1 - par

                def gate(dst, unit, h):
                    pool.wait_ge(main_read, 8 * nxt + 2 * unit + h + 3)
                    if unit == 0 and h == 0 and n is not None:
                        pool.wait_ge(o_done, 2 * n + 1)
                    pool.tensor_tensor(dst[:, h * HALF:(h + 1) * HALF], z[:, h, :], sig[:, h, :], ALU.mult).then_inc(pool_used, 1)

                if projecting:
                    for h in range(2):
                        gate(Q[other], 0, h)
                    for h in range(2):
                        gate(G[other], 3, h)
                else:
                    for y in range(HEADS - 1):
                        low_part(y)
                if n is not None:
                    for x in range(2):
                        pool.wait_ge(chain, CHAIN * n + FIRST_STEP + 42 + x)
                        part = o[:, x * HALF:(x + 1) * HALF]
                        pool.tensor_tensor(part, part, G[par][:, x * HALF:(x + 1) * HALF], ALU.mult).then_inc(gated, 1)

            def low_part(y):
                pool.wait_ge(tail_high, y + 1)
                pool.tensor_tensor(hT_lo[:, y, :], returned(y), hT_hi[:, y, :].bitcast(F32), ALU.subtract).then_inc(tail_low, 1)

            passes(pool, body)
            low_part(HEADS - 1)

        @block.vector
        def _(dve):
            dve.wait_ge(loaded, 48)
            setup.count = 2
            setup.after(dve, dve.tensor_tensor(lb_tmp[:, :], logits[:, 0, :], logits[:, 1, :], ALU.max))
            for r in range(2):
                setup.after(dve, dve.tensor_tensor(logits[:, r, :], logits[:, r, :], lb_tmp[:, :], ALU.subtract))
            dve.sem_inc(lb_ready, 1)
            dve.wait_ge(lb_expd, 1)
            setup.after(dve, dve.tensor_tensor(lb_tmp[:, :], lb_exp[:, 0, :], lb_exp[:, 1, :], ALU.add))
            setup.after(dve, dve.reciprocal(lb_tmp[:, :], lb_tmp[:, :]))
            setup.after(dve, dve.tensor_tensor(lb[:, :], lb_exp[:, 0, :], lb_tmp[:, :], ALU.mult))
            setup.after(dve, dve.tensor_scalar(one_minus_lb[:, :], lb[:, :], -1.0, 1.0, ALU.mult, ALU.add))

            def body(it, a, looped, projecting):
                n, par, nxt, (first, w_it) = which(it, a, looped)
                other = 0 if n is None else 1 - par
                steps = FIRST_STEP

                def step(ins, wait=False):
                    nonlocal steps
                    steps += 1
                    ins.then_inc(chain, 1)
                    if wait:
                        dve.wait_ge(chain, CHAIN * n + steps)

                def split(j):
                    if projecting and not (n == HEADS - 2 and j == 3 if not looped else False):
                        W.split_lo(dve, (j + 2) % SLOTS, HGRN_BASE, first + j + 2, w_it, 8 if looped else 0)

                def decay(h):
                    if not projecting:
                        return
                    dve.wait_ge(main_read, 8 * nxt + 2 + h + 3)
                    head = slice(nxt, nxt + 1) if isinstance(nxt, int) else bass.ds(nxt, 1)
                    dve.tensor_scalar(F[other][:, h * HALF:(h + 1) * HALF], sig[:, h, :], one_minus_lb[:, head], lb[:, head],
                                      ALU.mult, ALU.add).then_inc(dve_used, 1)

                def keys_of_next():
                    dve.wait_ge(dve_used, 2 * nxt + 2)
                    dve.wait_ge(k_turned, 2 * nxt + 2)
                    dve.tensor_scalar(keys[:, :], F[other][:, :], -1.0, 1.0, ALU.mult, ALU.add).then_inc(chain, 1)
                    f = F[other][:, :].rearrange("p (b two) -> p b two", two=2)
                    dve.tensor_tensor(prods[:, 0:SEQ // 2], f[:, :, 0], f[:, :, 1], ALU.mult).then_inc(chain, 1)

                split(0)
                if n is None:
                    split(1)
                    decay(0)
                    decay(1)
                    keys_of_next()
                    dve.wait_ge(chain, 2)
                    dve.sem_inc(chain, FIRST_STEP - 2)
                    split(2)
                    split(3)
                    return
                Qn, Fn = Q[par], F[par]
                tp = {1: Fn[:, :]}
                at = 0
                for m in LEVELS:
                    tp[2 * m] = prods[:, at:at + SEQ // (2 * m)]
                    at += SEQ // (2 * m)

                def pairs(m, side):
                    return tp[m].rearrange("p (b two) -> p b two", two=2)[:, :, side]

                def block_product(m):
                    return dve.tensor_tensor(tp[2 * m], pairs(m, 0), pairs(m, 1), ALU.mult)

                def level(l):
                    m = LEVELS[l]
                    dve.wait_ge(level_done, 9 * n + 2 + l + 1)
                    blocks = SEQ // (2 * m)
                    spread = [pairs(m, side).unsqueeze(2).broadcast_to([P, blocks, m]) for side in range(2)]
                    step(dve.tensor_tensor(rights(Qn[:, :], m), rights(Qn[:, :], m), spread[0], ALU.mult))
                    step(dve.tensor_tensor(lefts(keys[:, :], m), lefts(keys[:, :], m), spread[1], ALU.mult))
                    dve.wait_ge(chain, CHAIN * n + steps - 2)
                    if l < len(LEVELS) - 1:
                        step(block_product(2 * m))
                    out = att[:, :, :].rearrange("p c (b two m) -> p c b two m", two=2, m=m)[:, :, :, 1, :]
                    pick = masks[:, l, :].rearrange("p (b m) -> p b m", m=m).unsqueeze(1).broadcast_to([P, CHUNKS, 64 // m, m])
                    data = ps[LEVEL[l % 2]][:, :].rearrange("p (c b m) -> p c b m", c=CHUNKS, m=m)
                    if m == 1:
                        out, pick, data = out.squeeze(3), pick.squeeze(3), data.squeeze(3)
                    elif m == 64:
                        out, pick, data = out.squeeze(2), pick.squeeze(2), data.squeeze(2)
                    K.past_waits(dve)
                    step(dve.copy_predicated(out, pick, data))

                for x in range(2):
                    dve.wait_ge(level_done, 9 * n + x + 1)
                    step(dve.tensor_tensor(att[:, 4 * x:4 * x + 4, :], ps[LEVEL[x]][:, :].rearrange("p (c t) -> p c t", c=4),
                                           ident[:, :].unsqueeze(1).broadcast_to([P, 4, P]), ALU.mult))
                step(dve.tensor_tensor(Qn[:, :], Qn[:, :], Fn[:, :], ALU.mult))
                assert steps == AFTER_DIAGONAL
                level(0)
                level(1)
                split(1)
                level(2)
                level(3)
                decay(0)
                level(4)
                split(2)
                decay(1)
                level(5)
                level(6)
                split(3)
                dve.wait_ge(update_done, 2 * n + 1)
                step(dve.tensor_copy(state[:, 1, :], ps[LEVEL[0]][:, 0:P]), wait=True)
                for c in range(1, CHUNKS - 1):
                    if c == 4:
                        dve.wait_ge(update_done, 2 * n + 2)
                    step(dve.scalar_tensor_tensor(state[:, c + 1, :], state[:, c, :], tp[CHUNK][:, c:c + 1],
                                                  ps[LEVEL[c // 4]][:, (c % 4) * P:(c % 4 + 1) * P], ALU.mult, ALU.add), wait=True)
                assert steps == AFTER_STATES
                if projecting:
                    keys_of_next()
                else:
                    dve.sem_inc(chain, 2)
                steps += 2
                for x in range(2):
                    dve.wait_ge(rms_done, 2 * n + x + 2)
                    step(dve.reciprocal(rms[:, x, :], rms[:, x, :]), wait=True)
                dve.wait_ge(stored, 16 * n + 16)
                head = slice(n, n + 1) if isinstance(n, int) else bass.ds(n, 1)
                for x in range(2):
                    step(dve.scalar_tensor_tensor(o[:, x * HALF:(x + 1) * HALF], ps[OUT[x]][:, :], norm_g[:, head], rms[:, x, :],
                                                  ALU.mult, ALU.mult))
                assert steps == CHAIN + FIRST_STEP

            passes(dve, body)

        @block.tensor
        def _(pe):
            pe.sem_inc(v_turned, 2)
            pe.sem_inc(k_turned, 2)
            pe.sem_inc(o_done, 1)
            pe.wait_ge(setup.sem, 2)

            def body(it, a, looped, projecting):
                n, par, nxt, (first, w_it) = which(it, a, looped)

                def project(piece):
                    k, third = piece // 3, piece % 3
                    j, h = k // 2, k % 2
                    s = j % SLOTS
                    if third == 0:
                        if h == 0:
                            W.wait(pe, HGRN_BASE, first + j, w_it, 8 if looped else 0)
                        pe.wait_ge(main_read, 8 * nxt + k + 1)
                    out = ps[MAIN[h]][:, :]
                    for x in range(8 * third, 8 * third + 8):
                        kt, part = x // 3, x % 3
                        cols = slice(kt * P, (kt + 1) * P)
                        toks = slice(h * HALF, (h + 1) * HALF)
                        st = (W.lo if part == 2 else W.hi)[:, s, cols]
                        mv = (hT_lo if part == 1 else hT_hi)[:, kt, toks]
                        ins = pe.matmul(out, st, mv, start=(x == 0), stop=(x == 23))
                    if third == 2:
                        ins.then_inc(W.used if h else main_done, 1)

                def chunk(c):
                    return slice(c * CHUNK, (c + 1) * CHUNK)

                def turn(src, x, done):
                    for q in range(4):
                        ins = pe.transpose(ps[TURN][:, q * P:(q + 1) * P], src[:, chunk(4 * x + q)], ident[:, :])
                    ins.then_inc(done, 1)

                def steps(pos):
                    if pos == 0:
                        pe.wait_ge(main_read, 8 * n + 6 + 2)
                        pe.wait_ge(k_ready, 2 * n + 1)
                        turn(vT, 0, v_turned)
                        pe.wait_ge(chain, CHAIN * n + AFTER_KEYS)
                        pe.wait_ge(pool_used, 4 * n + 2 + 2)
                        for x in range(2):
                            for c in range(4):
                                ins = pe.matmul(ps[LEVEL[x]][:, c * P:(c + 1) * P], keys[:, chunk(4 * x + c)],
                                                Q[par][:, chunk(4 * x + c)], start=True, stop=True)
                            ins.then_inc(level_done, 1)
                    if pos == 1:
                        pe.wait_ge(v_ready, 2 * n + 1)
                        turn(vT, 1, v_turned)
                    if pos >= 3 and pos % 2 == 1 and pos <= 15:
                        l = (pos - 3) // 2
                        m = LEVELS[l]
                        pe.wait_ge(chain, CHAIN * n + (after_level(l - 1) if l else AFTER_DIAGONAL))
                        for c in range(CHUNKS):
                            mv = rights(Q[par][:, chunk(c)], m)
                            ins = pe.matmul(ps[LEVEL[l % 2]][:, c * 64:(c + 1) * 64].rearrange("p (b m) -> p b m", m=m),
                                            keys[:, chunk(c)], mv, start=True, stop=True)
                        ins.then_inc(level_done, 1)
                    if pos == 17:
                        pe.wait_ge(v_ready, 2 * n + 2)
                        pe.wait_ge(chain, CHAIN * n + after_level(6))
                        turn(keys, 0, k_turned)
                    if pos == 18:
                        pe.wait_ge(k_ready, 2 * n + 2)
                        turn(keys, 1, k_turned)
                    if pos == 19:
                        pe.wait_ge(k_ready, 2 * n + 3)
                        pe.wait_ge(chain, CHAIN * n + after_level(6) + 1)
                        for x in range(2):
                            for c in range(4 * x, min(4 * x + 4, CHUNKS - 1)):
                                ins = pe.matmul(ps[LEVEL[x]][:, (c % 4) * P:(c % 4 + 1) * P], keysT[:, c, :], V[:, c, :],
                                                start=True, stop=True)
                            ins.then_inc(update_done, 1)
                    if pos == 21:
                        pe.wait_ge(chain, CHAIN * n + AFTER_STATES)
                        for c in range(CHUNKS):
                            out = ps[OUT[c // 4]][:, (c % 4) * P:(c % 4 + 1) * P]
                            ins = pe.matmul(out, V[:, c, :], att[:, c, :], start=True, stop=(c == 0))
                            if c:
                                ins = pe.matmul(out, state[:, c, :], Q[par][:, chunk(c)], start=False, stop=True)
                            if c % 4 == 3:
                                ins.then_inc(o_done, 1)
                    if pos in (22, 23):
                        x = pos - 22
                        pe.wait_ge(squared, 2 * n + x + 1)
                        pe.wait_ge(rms_done, 2 * n + x + 1)
                        pe.matmul(ps[MEAN][:, :], mean_w[:, :], sq[:, x, :], start=True, stop=True).then_inc(mean_done, 1)

                for pos in range(24):
                    if n is not None:
                        steps(pos)
                    if projecting:
                        project(pos)

            passes(pe, body)


def constants():
    q, k = np.arange(P)[:, None], np.arange(P)[None, :]
    half = ROPE_DIM // 2
    freq = np.exp(np.float32(-math.log(ROPE_THETA)) * np.arange(half, dtype=np.float32) * np.float32(2.0 / ROPE_DIM))
    rope = np.zeros((P, 2), np.float32)
    for h in range(2):
        for part, sign in ((0, -1.0), (1, 1.0)):
            rows = slice(h * DH + part * half, h * DH + (part + 1) * half)
            rope[rows, 0], rope[rows, 1] = freq, sign
    level = []
    for m in LEVELS:
        t = np.concatenate([np.arange(b + m, b + 2 * m) for b in range(0, CHUNK, 2 * m)])[None, :]
        level.append((q // (2 * m) == t // (2 * m)) & (q % (2 * m) < m))
    return {
        "ident": np.eye(P, dtype=np.float32),
        "rope_cols": rope,
        "mask2": np.where(np.concatenate([k >= q, k <= q], axis=1), 0.0, NEG).astype(np.float32),
        "mask3": np.where((k <= q) & ((q - k) % 2 == 0), 0.0, NEG).astype(np.float32),
        "level_masks": np.stack(level, axis=1).astype(np.int32),
    }


MERGE_SLOT = [0, 1, 2, 3, 1]
MERGE_STEPS = KT // 2


def merge_block(nc, K):
    W, ps, hT_hi, hT_lo = K.W, K.ps, K.hT_hi, K.hT_lo
    base = MERGE_BASE
    with ExitStack() as ctx:
        def sb(n, shape, dt=F32):
            return ctx.enter_context(nc.sbuf_tensor(f"mg_{n}", shape, dt))

        def sem(n):
            return ctx.enter_context(nc.semaphore(f"mg_{n}"))

        acc = K.acc
        aT_hi, aT_lo = sb("aT_hi", [P, PAIRS, SEQ], F32R), sb("aT_lo", [P, PAIRS, SEQ], F32R)
        m_hi, m_lo = sb("m_hi", [P, 2, SEQ], F32R), sb("m_lo", [P, 2, SEQ], F32R)
        gate, m = sb("gate", [P, 2, SEQ]), sb("m", [P, 2, SEQ])
        in_ready = [sem(f"in_ready{x}") for x in range(2)]
        acc_ready, in_high, in_split = sem("acc_ready"), sem("in_high"), sem("in_split")
        gate_ready = [sem(f"gate_ready{x}") for x in range(2)]
        gate_sig = sem("gate_sig")
        y_done, y_read = sem("y_done"), sem("y_read")
        m_sum, m_high, m_ready = sem("m_sum"), sem("m_high"), sem("m_ready")
        out_done, out_free = sem("out_done"), sem("out_free")
        R = Residual(nc, ctx, K, "mg", 0, rows=1, free=out_free)
        L = LayerNorm(nc, ctx, K, "ln2", 1, y=gate[:, :, :].rearrange("p a (b n) -> p (a b) n", b=2))
        block = ctx.enter_context(nc.Block())

        def pairs(eng, body):
            with eng.Fori(0, MERGE_STEPS // 2 - 1) as it:
                body(it, False)
            body(MERGE_STEPS // 2 - 1, True)

        @block.sync
        def _(sp):
            sp.sem_inc(y_read, 4)
            sp.sem_inc(m_sum, 4)
            for x in range(2):
                sp.dma_start((m, gate)[x][:, :, :], K.att_scratch[2 * x:2 * x + 2, :, :].rearrange("k p n -> p k n"))\
                  .then_inc(in_ready[x], 16)
            sp.dma_start(acc[:, :, :], K.res_scratch).then_inc(acc_ready, 16)
            R.loads(sp)
            L.loads(sp)

            def body(it, last):
                for a in range(2):
                    i = 2 * it + a

                    def load_gate(q):
                        sp.wait_ge(*((m_sum, 4 * i + 2 * q + 2) if q < 2 else (y_read, 8 * i + 2 * q + 2)))
                        tile = (KT if q < 2 else 0) + 2 * i + q % 2
                        sp.dma_start(gate[:, q % 2, :], K.gates_scratch[tile, :, :]).then_inc(gate_ready[q % 2], 16)

                    if a == 0:
                        sp.wait_ge(in_split, 2)
                    load_gate(0)
                    load_gate(1)
                    W.load(sp, base + 2, 5 * a, it, 10)
                    W.load(sp, base + 2, 5 * a + 1, it, 10)
                    load_gate(2)
                    W.load(sp, base + 2, 5 * a + 2, it, 10)
                    load_gate(3)
                    W.load(sp, base + 2, 5 * a + 3, it, 10)
                    W.load(sp, base + 2, 5 * a + 4, it, 10)

            pairs(sp, body)

        @block.scalar
        def _(act):
            for x in range(2):
                act.wait_ge(in_ready[x], 16)
                act.activation(aT_hi[:, 2 * x:2 * x + 2, :], (m, gate)[x][:, :, :], ACT.Copy).then_inc(in_high, 1)

            def body(it, last):
                for a in range(2):
                    i = 2 * it + a

                    def sigmoid(q):
                        act.wait_ge(gate_ready[q % 2], 32 * i + 16 * (q // 2) + 16)
                        act.activation(gate[:, q % 2, :], gate[:, q % 2, :], ACT.Sigmoid).then_inc(gate_sig, 1)

                    W.split_hi(act, 1, base, 5 * a + 1, it, 10, reuse=2)
                    W.split_hi(act, 2, base, 5 * a + 2, it, 10)
                    sigmoid(0)
                    sigmoid(1)
                    W.split_hi(act, 3, base, 5 * a + 3, it, 10)
                    sigmoid(2)
                    W.split_hi(act, 1, base, 5 * a + 4, it, 10)
                    sigmoid(3)
                    for n in range(4):
                        d, h = n // 2, n % 2
                        act.wait_ge(m_sum, 4 * i + n + 5)
                        part = slice(h * HALF, (h + 1) * HALF)
                        act.activation(m_hi[:, d, part], m[:, d, part], ACT.Copy).then_inc(m_high, 1)
                    W.split_hi(act, 0, base, 5 * a + 5, it, 10)

            pairs(act, body)
            L.scalar(act)

        @block.gpsimd
        def _(pool):
            pool.wait_ge(acc_ready, 16)
            R.make(pool)
            L.gpsimd(pool)

        @block.vector
        def _(dve):
            for x in range(2):
                dve.wait_ge(in_high, x + 1)
                dve.tensor_tensor(aT_lo[:, 2 * x:2 * x + 2, :], (m, gate)[x][:, :, :], aT_hi[:, 2 * x:2 * x + 2, :].bitcast(F32),
                                  ALU.subtract).then_inc(in_split, 1)
            dve.sem_inc(out_free, 4)

            def body(it, last):
                for a in range(2):
                    i = 2 * it + a

                    def weigh(q):
                        for h in range(2):
                            part = slice(h * HALF, (h + 1) * HALF)
                            if h and q != 2:
                                W.done(dve, base, 5 * a + min(q, 2), it, 10)
                            else:
                                dve.wait_ge(y_done, 5 * i + (1, 2, 3, 5)[q] + h)
                            dve.wait_ge(gate_sig, 4 * i + q + 1)
                            g = gate[:, q % 2, part]
                            dve.tensor_tensor(m[:, q, part] if q < 2 else g, g, ps[2 * (q % 2) + h][:, :], ALU.mult).then_inc(y_read, 1)

                    def merge(d):
                        for h in range(2):
                            n, part = 2 * d + h, slice(h * HALF, (h + 1) * HALF)
                            dve.wait_ge(y_read, 8 * i + n + 9)
                            dve.tensor_tensor(m[:, d, part], m[:, d, part], gate[:, d, part], ALU.add).then_inc(m_sum, 1)
                        for h in range(2):
                            n, part = 2 * d + h, slice(h * HALF, (h + 1) * HALF)
                            dve.wait_ge(m_high, 4 * i + n + 1)
                            dve.tensor_tensor(m_lo[:, d, part], m[:, d, part], m_hi[:, d, part].bitcast(F32), ALU.subtract)\
                               .then_inc(m_ready, 1)

                    W.split_lo(dve, 1, base, 5 * a + 1, it, 10)
                    W.split_lo(dve, 2, base, 5 * a + 2, it, 10)
                    weigh(0)
                    W.split_lo(dve, 3, base, 5 * a + 3, it, 10)
                    weigh(1)
                    W.split_lo(dve, 1, base, 5 * a + 4, it, 10)
                    weigh(2)
                    merge(0)
                    weigh(3)
                    merge(1)
                    W.split_lo(dve, 0, base, 5 * a + 5, it, 10)
                    add_out(dve, K, out_done, out_free, R.ready if a or last else R.gained, i, (base, 5 * a + 4, it, 10), 1.0,
                            L if last and a else None)

            pairs(dve, body)

        @block.tensor
        def _(pe):
            def body(it, last):
                for a in range(2):
                    i = 2 * it + a

                    def branch_product(q, stationary, hi, lo, tiles):
                        for h in range(2):
                            part = slice(h * HALF, (h + 1) * HALF)
                            pe.wait_ge(y_read, 8 * i + 2 * q + h + 1)
                            product(pe, ps[2 * (q % 2) + h][:, :], [
                                (*stationary(k), hi[:, k, part], lo[:, k, part]) for k in range(tiles)])\
                                .then_inc(W.used if h and q != 2 else y_done, 1)

                    def columns(slot, first=0):
                        return lambda k: (W.hi[:, slot, first + k * P:first + (k + 1) * P], W.lo[:, slot, first + k * P:first + (k + 1) * P])

                    for q in range(2):
                        W.wait(pe, base, 5 * a + q, it, 10)
                        branch_product(q, columns(MERGE_SLOT[q]), hT_hi, hT_lo, KT)
                    W.wait(pe, base, 5 * a + 2, it, 10)
                    if a == 0:
                        pe.wait_ge(in_split, 2)
                    for q in (2, 3):
                        branch_product(q, columns(MERGE_SLOT[2], (q - 2) * PAIRS * P), aT_hi, aT_lo, PAIRS)
                    W.wait(pe, base, 5 * a + 3, it, 10)
                    W.wait(pe, base, 5 * a + 4, it, 10)
                    out_product(pe, K, MERGE_SLOT[3:], m_hi, m_lo, m_ready, out_free, out_done, i)

            pairs(pe, body)
            L.tensor(pe, out_free, 16 * MERGE_STEPS + 4)


def ple_block(nc, K, out):
    W, ps, hT_hi, hT_lo, acc = K.W, K.ps, K.hT_hi, K.hT_lo, K.acc
    base = PLE_BASE
    with ExitStack() as ctx:
        def sb(n, shape, dt=F32):
            return ctx.enter_context(nc.sbuf_tensor(f"ple_{n}", shape, dt))

        def sem(n):
            return ctx.enter_context(nc.semaphore(f"ple_{n}"))

        pT_hi, pT_lo = K.pT_hi, K.pT_lo
        emb, gate = sb("emb", [P, TT, HALF]), sb("gate", [P, TT, HALF])
        done, read = sem("done"), sem("read")
        scaled, summed, stored = sem("scaled"), sem("summed"), sem("stored")
        R = Residual(nc, ctx, K, "ple", 2)
        block = ctx.enter_context(nc.Block())

        @block.sync
        def _(sp):
            R.loads(sp)
            for j in range(2, 6):
                W.load(sp, base, j)

            def store(n):
                t, c = n % TT, n // TT
                sp.wait_ge(summed, n + 1)
                sp.dma_start(out[t, :, c * HALF:(c + 1) * HALF], acc[:, t, c * HALF:(c + 1) * HALF]).then_inc(stored, 16)

            for j in range(6, PLE_UNITS):
                W.load(sp, base, j)
            for n in range(2 * TT):
                store(n)
            sp.wait_ge(stored, 16 * 2 * TT)

        def bank_done(eng, c, x, t):
            if t == TT - 1:
                W.done(eng, base, 5 * c + x)
            else:
                eng.wait_ge(done, (TT - 1) * (2 * c + (x == 4)) + t + 1)

        @block.scalar
        def _(act):
            for c in range(2):
                for x in range(5):
                    j = 5 * c + x + 2
                    if j < PLE_UNITS:
                        W.split_hi(act, j % SLOTS, base, j, reuse=4)
                    if x == 0:
                        for t in range(TT):
                            bank_done(act, c, 0, t)
                            if c:
                                act.wait_ge(scaled, t + 1)
                            act.activation(emb[:, t, :], ps[t][:, :], ACT.Copy).then_inc(read, 1)
                for t in range(TT):
                    bank_done(act, c, 4, t)
                    if c:
                        act.wait_ge(summed, t + 1)
                    act.activation(gate[:, t, :], ps[t][:, :], ACT.Sigmoid).then_inc(read, 1)

        block.gpsimd(R.make)

        @block.vector
        def _(dve):
            for c in range(2):
                for x in range(5):
                    j = 5 * c + x + 2
                    if j < PLE_UNITS:
                        W.split_lo(dve, j % SLOTS, base, j)
                for t in range(TT):
                    n = TT * c + t
                    dve.wait_ge(read, 16 * c + TT + t + 1)
                    dve.tensor_tensor(gate[:, t, :], gate[:, t, :], emb[:, t, :], ALU.mult).then_inc(scaled, 1)
                    dve.wait_ge(scaled, n + 1)
                    dve.wait_ge(R.ready, t + 1)
                    part = acc[:, t, c * HALF:(c + 1) * HALF]
                    dve.tensor_tensor(part, part, gate[:, t, :], ALU.add).then_inc(summed, 1)

        @block.tensor
        def _(pe):
            for c in range(2):
                for x in range(5):
                    j = 5 * c + x
                    s = j % SLOTS
                    W.wait(pe, base, j)
                    hi, lo = (pT_hi, pT_lo) if x == 0 else (hT_hi, hT_lo)
                    for t in range(TT):
                        if x < 2 and j:
                            pe.wait_ge(read, TT * (2 * c + x - 1) + t + 1)
                        last = product(pe, ps[t][:, :], [
                            (hi[:, k, t * P:(t + 1) * P], lo[:, k, t * P:(t + 1) * P],
                             W.hi[:, s, (k % 2) * HALF:(k % 2 + 1) * HALF], W.lo[:, s, (k % 2) * HALF:(k % 2 + 1) * HALF])
                            for k in ((0, 1) if x == 0 else (2 * x - 2, 2 * x - 1))], start=(x < 2), stop=(x in (0, 4)))
                        if t == TT - 1:
                            last.then_inc(W.used, 1)
                        elif x in (0, 4):
                            last.then_inc(done, 1)


def decoder_layer(nc, drams, out):
    with ExitStack() as ctx:
        K = Core()
        K.W = Weights(nc, ctx, drams["units"])
        K.ps = [ctx.enter_context(nc.psum_tensor(f"bank{b}", [P, HALF], F32)) for b in range(8)]
        K.hT_hi = ctx.enter_context(nc.sbuf_tensor("hT_hi", [P, KT, SEQ], F32R))
        K.hT_lo = ctx.enter_context(nc.sbuf_tensor("hT_lo", [P, KT, SEQ], F32R))
        K.ident = ctx.enter_context(nc.sbuf_tensor("ident", [P, P], F32))
        K.const_ready = ctx.enter_context(nc.semaphore("const_ready"))
        K.passed = {e.engine: ctx.enter_context(nc.semaphore(f"passed_{n}")) for n, e in (("dve", nc.vector), ("pool", nc.gpsimd))}
        K.ident_dram, K.xT_dram, K.x_dram, K.pT_dram = drams["ident"], drams["xT"], drams["x"], drams["pT"]
        K.ln_cols_dram, K.ln_rows_dram = drams["ln_cols"], drams["ln_rows"]
        K.positions_dram, K.rope_cols_dram = drams["positions"], drams["rope_cols"]
        K.mask2_dram, K.mask3_dram = drams["mask2"], drams["mask3"]
        K.level_masks_dram, K.lb_logits_dram, K.norm_g_dram = drams["level_masks"], drams["lb_logits"], drams["norm_g"]

        def scratch(name, shape):
            return nc.dram_tensor(name, shape, F32, kind="Internal").ap()

        K.res_scratch = scratch("res_scratch", (P, TT, DM))
        K.gates_scratch = scratch("gates_scratch", (2 * KT, P, SEQ))
        K.att_scratch = scratch("att_scratch", (PAIRS, P, SEQ))
        K.hgrn_scratch = scratch("hgrn_scratch", (HEADS, P, SEQ))

        with nc.sbuf_tensor("cos", [P, SEQ], F32) as K.cos, nc.sbuf_tensor("sin", [P, SEQ], F32) as K.sin:
            with nc.sbuf_tensor("acc1", [P, TT, DM], F32) as K.acc:
                ffn_block(nc, K, "ffn1", FFN1_BASE, presplit=0, first=True, ln=0, side=RopeTables, res_out=K.res_scratch)
            attention_block(nc, K)
        hgrn_block(nc, K)
        with nc.sbuf_tensor("acc2", [P, TT, DM], F32) as K.acc:
            merge_block(nc, K)
            tiles = PLE_DIM // P
            with nc.sbuf_tensor("pT_hi", [P, tiles, SEQ], F32R) as K.pT_hi, nc.sbuf_tensor("pT_lo", [P, tiles, SEQ], F32R) as K.pT_lo:
                ffn_block(nc, K, "ffn2", FFN2_BASE, presplit=1, first=False, ln=2, side=PleInput)
                ple_block(nc, K, out)


def kernel(**inputs):
    import numpy as _np
    import concourse.bacc as _bacc
    from concourse import mybir as _mybir
    from concourse.bass_utils import run_bass_kernel_spmd as _run

    given = {n: _np.asarray(a) for n, a in inputs.items()}

    def columns(w, first, n=P):
        return w[:, first:first + n].reshape(-1, P, n).transpose(1, 0, 2).reshape(P, -1)

    def slab(w, row, first, tiles):
        width = DM // tiles
        return w[row:row + tiles * P, first:first + width].reshape(tiles, P, width).transpose(1, 0, 2).reshape(P, -1)

    units = _np.empty((UNITS, P, DM), _np.float32)
    at = 0

    def put(unit):
        nonlocal at
        units[at] = unit
        at += 1

    def put_ffn(w_in, w_out):
        for step in range(FFN_STEPS):
            for f in (2 * step, 2 * step + 1):
                put(columns(w_in, f * P))
                put(columns(w_in, D_FF + f * P))
            for f in (2 * step, 2 * step + 1):
                put(slab(w_out, f * P, 0, 1))

    w_mix = given["w_mix_in"][0]
    att, hgrn = 3 * DM // 2, DM
    gates = 3 * att + 4 * hgrn
    put_ffn(given["ffn1_w_in"][0], given["ffn1_w_out"][0])
    for pair in range(PAIRS):
        for group in range(GROUPS):
            for part in range(3):
                put(columns(w_mix, part * att + (group * PAIRS + pair) * P))
        for n in range(3):
            put(columns(w_mix, gates + (3 * pair + n) * P))
    for n in range(3 * PAIRS, 2 * KT):
        put(columns(w_mix, gates + n * P))
    for head in range(HEADS):
        for part in range(4):
            put(columns(w_mix, 3 * att + part * hgrn + head * P))
    w_pa, w_pb, w_o = given["w_proj_attn"][0], given["w_proj_hgrn"][0], given["w_mix_out"][0]
    for j in range(0, KT, 2):
        put(columns(w_pb, j * P))
        put(columns(w_pb, (j + 1) * P))
        put(_np.concatenate([columns(w_pa, j * P), columns(w_pa, (j + 1) * P)], axis=1))
        put(slab(w_o, j * P, 0, 1))
        put(slab(w_o, (j + 1) * P, 0, 1))
    put_ffn(given["ffn2_w_in"][0], given["ffn2_w_out"][0])
    for c in range(2):
        put(slab(given["ple_w_proj"][0], 0, c * HALF, 2))
        for k in range(0, KT, 2):
            put(slab(given["ple_w_gate"][0], k * P, c * HALF, 2))
    assert at == UNITS

    def tiles_of_rows(a):
        return a.reshape(-1, P, a.shape[-1])

    x = given["x"][0]
    arrays = {
        "units": units,
        "xT": tiles_of_rows(x.T),
        "x": tiles_of_rows(x).transpose(1, 0, 2),
        "pT": tiles_of_rows(given["p"][0, 0].T),
        "positions": given["positions"],
        "ln_cols": _np.stack([_np.stack([given[f"ln{i}_{s}"][0].reshape(KT, P).T for s in "gb"], axis=1) for i in (1, 2, 3)]),
        "ln_rows": _np.stack([_np.stack([given[f"ln{i}_{s}"] for s in "gb"], axis=1) for i in (1, 2, 3)]),
        "lb_logits": given["hgrn_lb_logits"].reshape(2, HEADS, P).transpose(2, 0, 1),
        "norm_g": given["hgrn_norm_g"][0].reshape(HEADS, P).T,
        **constants(),
    }
    arrays = {n: _np.ascontiguousarray(a) for n, a in arrays.items()}
    nc = _bacc.Bacc("TRN2", target_bir_lowering=False, num_devices=1)
    drams = {n: nc.dram_tensor(f"in_{n}", a.shape, _mybir.dt.from_np(a.dtype), kind="ExternalInput").ap()
             for n, a in arrays.items()}
    out = nc.dram_tensor("out_0", (TT, P, DM), F32, kind="ExternalOutput").ap()
    decoder_layer(nc, drams, out)
    result = _run(nc, [{f"in_{n}": a for n, a in arrays.items()}], core_ids=[0])
    return result.results[0]["out_0"].reshape(1, SEQ, DM)
```
